# Optimizing a Trainium2 kernel written in Bass

```python
import math
import jax
import jax.numpy as jnp
from jax import lax
import numpy as np
import jax, jax.numpy as jnp

D_MODEL = 1024
BATCH = 1
SEQ = 256
DEPTH = 2

HEAD_DIM = 64
MIX_WIDTH = D_MODEL
N_HEADS_A = (MIX_WIDTH // 2) // (2 * HEAD_DIM)
DV_A = 2 * HEAD_DIM
N_HEADS_B = (MIX_WIDTH // 2) // HEAD_DIM
DILATED_PATTERNS = ((128, 1), (512, 4), (2048, 16))
N_HEADS_C = (MIX_WIDTH // 2) // HEAD_DIM
MOBA_BLOCK = 256
MOBA_TOPK = 3
MOBA_Q_CHUNK = 16
N_HEADS_D = (MIX_WIDTH // 2) // HEAD_DIM
FORGET_BIAS_INIT = 4.0
Q_BLOCK = 128
NUM_BUCKETS = 32
MAX_DISTANCE = 128
N_BIAS_HEADS = max(N_HEADS_A + N_HEADS_B, N_HEADS_C)
D_FF = -(-8 * D_MODEL // (3 * 256)) * 256
LN_EPS = 1e-5
DEEPNORM_ALPHA = (2 * DEPTH) ** 0.25
DEEPNORM_BETA = (8 * DEPTH) ** -0.25
ATTN_SCALE = HEAD_DIM ** -0.5

AB_SIZES = [N_HEADS_A * 2 * HEAD_DIM, N_HEADS_A * 2 * HEAD_DIM, N_HEADS_A * DV_A,
            N_HEADS_B * HEAD_DIM, N_HEADS_B * HEAD_DIM, N_HEADS_B * HEAD_DIM]
CD_SIZES = [N_HEADS_C * HEAD_DIM] * 3 + [N_HEADS_D * HEAD_DIM] * 3 + [N_HEADS_D]
AB_SPLITS = [int(s) for s in np.cumsum(AB_SIZES)[:-1]]
CD_SPLITS = [int(s) for s in np.cumsum(CD_SIZES)[:-1]]
IN_AB = sum(AB_SIZES)
IN_CD = sum(CD_SIZES)


f32 = jnp.float32

def t5_bucket(dist):
    n = jnp.maximum(dist, 0)
    max_exact = NUM_BUCKETS // 2
    nf = jnp.maximum(n, 1).astype(f32)
    large = max_exact + (jnp.log(nf / max_exact) / math.log(MAX_DISTANCE / max_exact)
                         * (NUM_BUCKETS - max_exact)).astype(jnp.int32)
    large = jnp.minimum(large, NUM_BUCKETS - 1)
    return jnp.where(n < max_exact, n, large)

def t5_bias(table_cols, dist):
    return jnp.moveaxis(table_cols[t5_bucket(dist)], -1, 0).astype(f32)

def layer_norm(x, g, b):
    xf = x.astype(f32)
    mu = xf.mean(-1, keepdims=True)
    var = jnp.square(xf - mu).mean(-1, keepdims=True)
    return ((xf - mu) * lax.rsqrt(var + LN_EPS) * g + b).astype(x.dtype)

def causal_block_attention(q, k, v, map_w, bias_fn):
    B, H, M, T, _ = q.shape
    k_pos = jnp.arange(T)

    def block(q0):
        qb = lax.dynamic_slice_in_dim(q, q0, Q_BLOCK, axis=3)
        q_pos = q0 + jnp.arange(Q_BLOCK)
        s = jnp.einsum('bhmqd,bhmkd->bhmqk', qb, k).astype(f32) + bias_fn(q_pos)
        s = jnp.where(k_pos[None, :] <= q_pos[:, None], s, -jnp.inf)
        p = jnp.einsum('bhmqk,m->bhqk', jax.nn.softmax(s, axis=-1), map_w)
        return jnp.einsum('bhqk,bhkd->bhqd', p.astype(v.dtype), v)

    out = lax.map(block, jnp.arange(T // Q_BLOCK) * Q_BLOCK)
    return jnp.moveaxis(out, 0, 2).reshape(B, H, T, v.shape[-1])

def dilated_attention(q, k, v, table_cols):
    B, H, T, dh = q.shape
    outs, lses = [], []
    for window, dil in DILATED_PATTERNS:
        W = window // dil
        L = T // dil
        nb = -(-L // W)
        pad = nb * W - L

        def strided(a):
            a = a.reshape(B, H, L, dil, a.shape[-1]).swapaxes(2, 3)
            return jnp.pad(a, ((0, 0), (0, 0), (0, 0), (0, pad), (0, 0)))

        def with_prev(a):
            ab = a.reshape(B, H, dil, nb, W, a.shape[-1])
            prev = jnp.pad(ab, ((0, 0), (0, 0), (0, 0), (1, 0), (0, 0), (0, 0)))[:, :, :, :-1]
            return jnp.concatenate([prev, ab], axis=4)

        qb = strided(q).reshape(B, H, dil, nb, W, dh)
        kb = with_prev(strided(k))
        vb = with_prev(strided(v))
        u_q = jnp.arange(nb)[:, None] * W + jnp.arange(W)[None, :]
        u_k = jnp.arange(nb)[:, None] * W + jnp.arange(-W, W)[None, :]
        du = u_q[:, :, None] - u_k[:, None, :]
        valid = (du >= 0) & (du <= W) & (u_k[:, None, :] >= 0)
        bias = t5_bias(table_cols, du * dil)
        s = jnp.einsum('bhrnqd,bhrnkd->bhrnqk', qb, kb).astype(f32) + bias[None, :, None]
        s = jnp.where(valid, s, -jnp.inf)
        m = s.max(-1, keepdims=True)
        p = jnp.exp(s - m)
        den = p.sum(-1)
        o = jnp.einsum('bhrnqk,bhrnkd->bhrnqd', p.astype(vb.dtype), vb) / den[..., None]
        o = o.reshape(B, H, dil, nb * W, dh)[:, :, :, :L].swapaxes(2, 3).reshape(B, H, T, dh)
        lse = (m[..., 0] + jnp.log(den)).reshape(B, H, dil, nb * W)[..., :L]
        outs.append(o)
        lses.append(lse.swapaxes(2, 3).reshape(B, H, T))
    w = jax.nn.softmax(jnp.stack(lses), axis=0)
    return jnp.sum(w[..., None] * jnp.stack(outs), axis=0).astype(q.dtype)

def moba_attention(q, k, v, table_cols):
    B, H, T, dh = q.shape
    n_blk = -(-T // MOBA_BLOCK)
    pad = n_blk * MOBA_BLOCK - T
    kp = jnp.pad(k, ((0, 0), (0, 0), (0, pad), (0, 0)))
    vp = jnp.pad(v, ((0, 0), (0, 0), (0, pad), (0, 0)))
    k_blk = kp.reshape(B, H, n_blk, MOBA_BLOCK, dh)
    v_blk = vp.reshape(B, H, n_blk, MOBA_BLOCK, dh)
    k_mean = k_blk.mean(axis=3)
    top = min(MOBA_TOPK, n_blk)
    b_idx = jnp.arange(B)[:, None, None, None]
    h_idx = jnp.arange(H)[None, :, None, None]
    bias_flat = table_cols.T.reshape(-1).astype(f32)
    in_blk = jnp.arange(MOBA_BLOCK)

    def chunk(q0):
        qc = lax.dynamic_slice_in_dim(q, q0, MOBA_Q_CHUNK, axis=2)
        q_pos = q0 + jnp.arange(MOBA_Q_CHUNK)
        own = q0 // MOBA_BLOCK
        gate = jnp.einsum('bhcd,bhnd->bhcn', qc, k_mean).astype(f32)
        gate = jnp.where(jnp.arange(n_blk) < own, gate, -jnp.inf)
        top_s, top_i = lax.top_k(gate, top)
        sel_ok = jnp.isfinite(top_s)
        k_sel = k_blk[b_idx, h_idx, top_i]
        v_sel = v_blk[b_idx, h_idx, top_i]
        sel_pos = top_i[..., None] * MOBA_BLOCK + in_blk
        sel_bucket = t5_bucket(q_pos[:, None, None] - sel_pos)
        s_sel = (jnp.einsum('bhcd,bhcnkd->bhcnk', qc, k_sel).astype(f32)
                 + bias_flat[h_idx[..., None] * NUM_BUCKETS + sel_bucket])
        s_sel = jnp.where(sel_ok[..., None], s_sel, -jnp.inf)
        own_start = own * MOBA_BLOCK
        k_own = lax.dynamic_slice_in_dim(kp, own_start, MOBA_BLOCK, axis=2)
        v_own = lax.dynamic_slice_in_dim(vp, own_start, MOBA_BLOCK, axis=2)
        own_dist = q_pos[:, None] - (own_start + in_blk)[None, :]
        s_own = (jnp.einsum('bhcd,bhkd->bhck', qc, k_own).astype(f32)
                 + t5_bias(table_cols, own_dist)[None])
        s_own = jnp.where(own_dist >= 0, s_own, -jnp.inf)
        s = jnp.concatenate([s_sel.reshape(B, H, MOBA_Q_CHUNK, top * MOBA_BLOCK), s_own], axis=-1)
        p = jax.nn.softmax(s, axis=-1).astype(v.dtype)
        p_sel = p[..., :top * MOBA_BLOCK].reshape(B, H, MOBA_Q_CHUNK, top, MOBA_BLOCK)
        p_own = p[..., top * MOBA_BLOCK:]
        return (jnp.einsum('bhcnk,bhcnkd->bhcd', p_sel, v_sel)
                + jnp.einsum('bhck,bhkd->bhcd', p_own, v_own))

    out = lax.map(chunk, jnp.arange(T // MOBA_Q_CHUNK) * MOBA_Q_CHUNK)
    return jnp.moveaxis(out, 0, 2).reshape(B, H, T, dh)

def split_heads(a, dh):
    B, T, _ = a.shape
    return a.reshape(B, T, -1, dh).transpose(0, 2, 1, 3)

def merge_heads(a):
    B, H, T, dh = a.shape
    return a.transpose(0, 2, 1, 3).reshape(B, T, H * dh)

def mixer_ab(h, w_in, w_o, lam, subln_g, table, lambda_init):
    B, T, _ = h.shape
    qa, ka, va, qb, kb, vb = jnp.split(h @ w_in, AB_SPLITS, axis=-1)
    qa = qa.reshape(B, T, N_HEADS_A, 2, HEAD_DIM).transpose(0, 2, 3, 1, 4) * ATTN_SCALE
    ka = ka.reshape(B, T, N_HEADS_A, 2, HEAD_DIM).transpose(0, 2, 3, 1, 4)
    va = split_heads(va, DV_A)
    lamf = lam.astype(f32)
    lam_full = (jnp.exp(jnp.sum(lamf[0] * lamf[1])) - jnp.exp(jnp.sum(lamf[2] * lamf[3]))
                + lambda_init)
    map_w = jnp.stack([jnp.ones((), f32), -lam_full])
    table_a = table[:, :N_HEADS_A]
    k_pos = jnp.arange(T)
    bias_a = lambda q_pos: t5_bias(table_a, q_pos[:, None] - k_pos[None, :])[None, :, None]
    oa = causal_block_attention(qa, ka, va, map_w, bias_a).astype(f32)
    oa = oa * lax.rsqrt(jnp.mean(jnp.square(oa), -1, keepdims=True) + LN_EPS)
    oa = (oa * subln_g * (1.0 - lambda_init)).astype(h.dtype)
    ob = dilated_attention(split_heads(qb, HEAD_DIM) * ATTN_SCALE, split_heads(kb, HEAD_DIM),
                           split_heads(vb, HEAD_DIM), table[:, N_HEADS_A:N_HEADS_A + N_HEADS_B])
    return jnp.concatenate([merge_heads(oa), merge_heads(ob)], axis=-1) @ w_o

def mixer_cd(h, w_in, w_o, forget_b, table):
    qc, kc, vc, qd, kd, vd, fd = jnp.split(h @ w_in, CD_SPLITS, axis=-1)
    oc = moba_attention(split_heads(qc, HEAD_DIM) * ATTN_SCALE, split_heads(kc, HEAD_DIM),
                        split_heads(vc, HEAD_DIM), table[:, :N_HEADS_C])
    log_f = jax.nn.log_sigmoid((fd + forget_b).astype(f32)).transpose(0, 2, 1)
    cum = jnp.cumsum(log_f, axis=-1)
    fox_bias = lambda q_pos: (cum[:, :, q_pos, None] - cum[:, :, None, :])[:, :, None]
    od = causal_block_attention((split_heads(qd, HEAD_DIM) * ATTN_SCALE)[:, :, None],
                                split_heads(kd, HEAD_DIM)[:, :, None],
                                split_heads(vd, HEAD_DIM), jnp.ones((1,), f32), fox_bias)
    return jnp.concatenate([merge_heads(oc), merge_heads(od)], axis=-1) @ w_o

def swiglu(h, w_in, w_out):
    g, u = jnp.split(h @ w_in, 2, axis=-1)
    return (jax.nn.silu(g) * u) @ w_out

def first_inputs(seed: int = 0) -> dict:
    key = jax.random.key(seed)
    ks = jax.random.split(key, 15)
    n_even = (DEPTH + 1) // 2
    n_odd = DEPTH // 2
    nrm = lambda k, shape, std: jax.random.normal(k, shape, f32) * std
    return {
        "x": nrm(ks[0], (BATCH, SEQ, D_MODEL), 1.0),
        "c": nrm(ks[1], (BATCH, D_MODEL), 1.0),
        "rel_bias": nrm(ks[2], (NUM_BUCKETS, N_BIAS_HEADS), 0.5),
        "w_ada": nrm(ks[3], (DEPTH, D_MODEL, 6 * D_MODEL), 0.1 * D_MODEL ** -0.5),
        "b_ada": nrm(ks[4], (DEPTH, 6 * D_MODEL), 0.01),
        "ln_g": 1.0 + nrm(ks[5], (DEPTH, 2, D_MODEL), 0.01),
        "ln_b": nrm(ks[6], (DEPTH, 2, D_MODEL), 0.01),
        "w_in_ab": nrm(ks[7], (n_even, D_MODEL, IN_AB), D_MODEL ** -0.5),
        "diff_lambda": nrm(ks[8], (n_even, 4, HEAD_DIM), 0.1),
        "diff_subln_g": 1.0 + nrm(ks[9], (n_even, DV_A), 0.01),
        "w_in_cd": nrm(ks[10], (n_odd, D_MODEL, IN_CD), D_MODEL ** -0.5),
        "forget_b": FORGET_BIAS_INIT + nrm(ks[11], (n_odd, N_HEADS_D), 0.5),
        "w_o": nrm(ks[12], (DEPTH, MIX_WIDTH, D_MODEL), DEEPNORM_BETA * MIX_WIDTH ** -0.5),
        "w_ffn_in": nrm(ks[13], (DEPTH, D_MODEL, 2 * D_FF), D_MODEL ** -0.5),
        "w_ffn_out": nrm(ks[14], (DEPTH, D_FF, D_MODEL), DEEPNORM_BETA * D_FF ** -0.5),
    }

def first_block(x, c, rel_bias, w_ada, b_ada, ln_g, ln_b, w_in_ab, diff_lambda, diff_subln_g,
              w_in_cd, forget_b, w_o, w_ffn_in, w_ffn_out):
    for l in range(DEPTH):
        ada = jax.nn.silu(c) @ w_ada[l] + b_ada[l]
        sh1, sc1, g1, sh2, sc2, g2 = [a[:, None, :] for a in jnp.split(ada, 6, axis=-1)]
        h = x * (1.0 + sc1) + sh1
        if l % 2 == 0:
            i = l // 2
            lambda_init = 0.8 - 0.6 * math.exp(-0.3 * l)
            y = mixer_ab(h, w_in_ab[i], w_o[l], diff_lambda[i], diff_subln_g[i], rel_bias,
                         lambda_init)
        else:
            i = l // 2
            y = mixer_cd(h, w_in_cd[i], w_o[l], forget_b[i], rel_bias)
        x = layer_norm(DEEPNORM_ALPHA * x + (1.0 + g1) * y, ln_g[l, 0], ln_b[l, 0])
        h = x * (1.0 + sc2) + sh2
        y = swiglu(h, w_ffn_in[l], w_ffn_out[l])
        x = layer_norm(DEEPNORM_ALPHA * x + (1.0 + g2) * y, ln_g[l, 1], ln_b[l, 1])
    return x


CTX_LEN = 256
GRID_W = 64
N_HEADS = D_MODEL // HEAD_DIM
NA_HEADS = N_HEADS // 2
WA_HEADS = N_HEADS - NA_HEADS
WA_KV_HEADS = max(1, WA_HEADS // 4)
NA_KH = 8
NA_KW = 16
WA_WINDOW = 128
WA_BLOCK = 128
D_FF_2 = ((8 * D_MODEL // 3 + 127) // 128) * 128
ROPE_BASE = 10000.0
N_MOD = 9
MACARON_W = 0.5
NORM_EPS = 1e-6
NEG_INF = -1e30
NA_W = NA_HEADS * HEAD_DIM
WA_W = WA_HEADS * HEAD_DIM
WA_KV_W = WA_KV_HEADS * HEAD_DIM
Q_W = NA_W + WA_W
IN_W = Q_W + 2 * NA_W + 2 * WA_KV_W


def rms_norm(x, g):
    xf = x.astype(jnp.float32)
    y = xf * lax.rsqrt(jnp.mean(xf * xf, axis=-1, keepdims=True) + NORM_EPS)
    return (y * g.astype(jnp.float32)).astype(x.dtype)

def modulate(h, shift, scale):
    return h * (1 + scale) + shift

def ada_params(cond, w_ada, b_ada):
    m = jax.nn.silu(cond) @ w_ada + b_ada
    return m.reshape(m.shape[:-1] + (N_MOD, D_MODEL))

def swiglu_half_step(x, g, mod, j, w_up, w_down):
    h = modulate(rms_norm(x, g), mod[..., j, :], mod[..., j + 1, :])
    gt, up = jnp.split(h @ w_up, 2, axis=-1)
    return x + MACARON_W * mod[..., j + 2, :] * ((jax.nn.silu(gt) * up) @ w_down)

def heads(t):
    return t.reshape(t.shape[:-1] + (t.shape[-1] // HEAD_DIM, HEAD_DIM))

def axial_rope_tables(n_tokens):
    rot = HEAD_DIM // 2
    inv_freq = ROPE_BASE ** (-jnp.arange(0, rot, 2, dtype=jnp.float32) / rot)
    t = jnp.arange(n_tokens)
    row = (t // GRID_W).astype(jnp.float32)
    col = (t % GRID_W).astype(jnp.float32)
    ang = jnp.stack([row[:, None] * inv_freq, col[:, None] * inv_freq], axis=1)
    return jnp.cos(ang), jnp.sin(ang)

def apply_axial_rope(x, cos, sin):
    B, S, H, Dh = x.shape
    xr = x.reshape(B, S, H, 2, 2, Dh // 4)
    x1, x2 = xr[..., 0, :], xr[..., 1, :]
    c = cos[:, None].astype(x.dtype)
    s = sin[:, None].astype(x.dtype)
    out = jnp.stack([x1 * c - x2 * s, x2 * c + x1 * s], axis=-2)
    return out.reshape(B, S, H, Dh)

def context_self_attention(q, k, v, sink):
    B, C, Hq, Dh = q.shape
    Hkv = k.shape[2]
    G = Hq // Hkv
    qg = (q * Dh ** -0.5).reshape(B, C, Hkv, G, Dh)
    s = jnp.einsum('bqkgd,bckd->bkgqc', qg, k).astype(jnp.float32)
    if sink is not None:
        sink_col = jnp.broadcast_to(sink.astype(jnp.float32).reshape(1, Hkv, G, 1, 1), s.shape[:-1] + (1,))
        s = jnp.concatenate([s, sink_col], axis=-1)
    p = jax.nn.softmax(s, axis=-1)[..., :C].astype(v.dtype)
    out = jnp.einsum('bkgqc,bckd->bqkgd', p, v)
    return out.reshape(B, C, Hq * Dh)

def neighbourhood_attention(q, k, v, k_ctx, v_ctx, rpb):
    B, S, H, Dh = q.shape
    rows = S // GRID_W
    kh = min(NA_KH, rows)
    n_nb = kh * NA_KW
    qg = (q * Dh ** -0.5).reshape(B, rows, GRID_W, H, Dh)
    kg = k.reshape(B, rows, GRID_W, H, Dh)
    vg = v.reshape(B, rows, GRID_W, H, Dh)
    col = jnp.arange(GRID_W)
    c0 = jnp.clip(col - NA_KW // 2, 0, GRID_W - NA_KW)
    col_idx = c0[:, None] + jnp.arange(NA_KW)[None, :]
    dc = col_idx - col[:, None] + (NA_KW - 1)
    rpb32 = rpb.astype(jnp.float32)

    def one_row(r):
        r0 = jnp.clip(r - kh // 2, 0, rows - kh)
        q_r = lax.dynamic_index_in_dim(qg, r, axis=1, keepdims=False)
        k_rows = lax.dynamic_slice_in_dim(kg, r0, kh, axis=1)
        v_rows = lax.dynamic_slice_in_dim(vg, r0, kh, axis=1)
        k_win = k_rows[:, :, col_idx]
        v_win = v_rows[:, :, col_idx]
        dr = r0 + jnp.arange(kh) - r + (NA_KH - 1)
        bias = rpb32[:, dr[:, None, None], dc[None, :, :]].transpose(0, 2, 1, 3)
        s_nb = jnp.einsum('bqhd,biqjhd->bhqij', q_r, k_win).astype(jnp.float32) + bias[None]
        s_ctx = jnp.einsum('bqhd,bchd->bhqc', q_r, k_ctx).astype(jnp.float32)
        logits = jnp.concatenate([s_nb.reshape(B, H, GRID_W, n_nb), s_ctx], axis=-1)
        p = jax.nn.softmax(logits, axis=-1).astype(v.dtype)
        p_nb = p[..., :n_nb].reshape(B, H, GRID_W, kh, NA_KW)
        return (jnp.einsum('bhqij,biqjhd->bqhd', p_nb, v_win)
                + jnp.einsum('bhqc,bchd->bqhd', p[..., n_nb:], v_ctx))

    out = lax.map(one_row, jnp.arange(rows))
    return out.transpose(1, 0, 2, 3, 4).reshape(B, S, H * Dh)

def windowed_gqa_attention(q, k, v, k_ctx, v_ctx, sink):
    B, S, Hq, Dh = q.shape
    Hkv = k.shape[2]
    G = Hq // Hkv
    nb = S // WA_BLOCK
    n_loc = 3 * WA_BLOCK
    qb = (q * Dh ** -0.5).reshape(B, nb, WA_BLOCK, Hkv, G, Dh)
    pad = ((0, 0), (WA_BLOCK, WA_BLOCK), (0, 0), (0, 0))
    kp = jnp.pad(k, pad)
    vp = jnp.pad(v, pad)
    q_off = jnp.arange(WA_BLOCK)
    k_off = jnp.arange(n_loc) - WA_BLOCK
    band = jnp.abs(k_off[None, :] - q_off[:, None]) <= WA_WINDOW
    sink_col = jnp.broadcast_to(sink.astype(jnp.float32).reshape(1, Hkv, G, 1, 1), (B, Hkv, G, WA_BLOCK, 1))

    def one_block(i):
        q_i = lax.dynamic_index_in_dim(qb, i, axis=1, keepdims=False)
        k_i = lax.dynamic_slice_in_dim(kp, i * WA_BLOCK, n_loc, axis=1)
        v_i = lax.dynamic_slice_in_dim(vp, i * WA_BLOCK, n_loc, axis=1)
        k_pos = i * WA_BLOCK + k_off
        valid = band & ((k_pos >= 0) & (k_pos < S))[None, :]
        s_loc = jnp.einsum('bqkgd,bjkd->bkgqj', q_i, k_i).astype(jnp.float32)
        s_loc = jnp.where(valid, s_loc, NEG_INF)
        s_ctx = jnp.einsum('bqkgd,bckd->bkgqc', q_i, k_ctx).astype(jnp.float32)
        p = jax.nn.softmax(jnp.concatenate([s_loc, s_ctx, sink_col], axis=-1), axis=-1).astype(v.dtype)
        out = (jnp.einsum('bkgqj,bjkd->bqkgd', p[..., :n_loc], v_i)
               + jnp.einsum('bkgqc,bckd->bqkgd', p[..., n_loc:-1], v_ctx))
        return out.reshape(B, WA_BLOCK, Hq * Dh)

    out = lax.map(one_block, jnp.arange(nb))
    return out.transpose(1, 0, 2, 3).reshape(B, S, Hq * Dh)

def split_kv(p):
    o1, o2, o3 = NA_W, 2 * NA_W, 2 * NA_W + WA_KV_W
    return p[..., :o1], p[..., o1:o2], p[..., o2:o3], p[..., o3:]

def second_inputs(seed: int = 0) -> dict:
    key = jax.random.key(seed)
    ks = jax.random.split(key, 14)
    f32 = jnp.float32

    def nrm(k, shape, scale):
        return jax.random.normal(k, shape, f32) * scale

    return {
        "x": nrm(ks[0], (BATCH, SEQ, D_MODEL), 1.0),
        "c": nrm(ks[1], (BATCH, D_MODEL), 1.0),
        "ctx": nrm(ks[2], (BATCH, CTX_LEN, D_MODEL), 1.0),
        "c_ctx": nrm(ks[3], (D_MODEL,), 1.0),
        "w_ada": nrm(ks[4], (DEPTH, D_MODEL, N_MOD * D_MODEL), 0.5 * D_MODEL ** -0.5),
        "b_ada": nrm(ks[5], (DEPTH, N_MOD * D_MODEL), 0.02),
        "norm_g": 1.0 + nrm(ks[6], (DEPTH, 3, D_MODEL), 0.02),
        "w_ffn_up": nrm(ks[7], (DEPTH, 2, D_MODEL, 2 * D_FF_2), D_MODEL ** -0.5),
        "w_ffn_down": nrm(ks[8], (DEPTH, 2, D_FF_2, D_MODEL), D_FF_2 ** -0.5),
        "w_in": nrm(ks[9], (DEPTH, D_MODEL, IN_W), D_MODEL ** -0.5),
        "w_out": nrm(ks[10], (DEPTH, Q_W, D_MODEL), Q_W ** -0.5),
        "qk_norm_g": 1.0 + nrm(ks[11], (DEPTH, 4, HEAD_DIM), 0.02),
        "na_rpb": nrm(ks[12], (DEPTH, NA_HEADS, 2 * NA_KH - 1, 2 * NA_KW - 1), 0.1),
        "wa_sink": nrm(ks[13], (DEPTH, WA_HEADS), 0.5),
    }

def second_block(x, c, ctx, c_ctx, w_ada, b_ada, norm_g, w_ffn_up, w_ffn_down, w_in, w_out,
              qk_norm_g, na_rpb, wa_sink):
    S = x.shape[1]
    cos, sin = axial_rope_tables(S)
    h_ctx = ctx
    for l in range(DEPTH):
        last = l == DEPTH - 1
        mod_x = ada_params(c, w_ada[l], b_ada[l])[:, None]
        mod_c = ada_params(c_ctx, w_ada[l], b_ada[l])[None, None]

        x = swiglu_half_step(x, norm_g[l, 0], mod_x, 0, w_ffn_up[l, 0], w_ffn_down[l, 0])
        h_ctx = swiglu_half_step(h_ctx, norm_g[l, 0], mod_c, 0, w_ffn_up[l, 0], w_ffn_down[l, 0])

        hx = modulate(rms_norm(x, norm_g[l, 1]), mod_x[..., 3, :], mod_x[..., 4, :])
        hc = modulate(rms_norm(h_ctx, norm_g[l, 1]), mod_c[..., 3, :], mod_c[..., 4, :])
        px = hx @ w_in[l]
        pc = hc @ (w_in[l, :, Q_W:] if last else w_in[l])
        pc_kv = pc[..., -(IN_W - Q_W):]

        qa = rms_norm(heads(px[..., :NA_W]), qk_norm_g[l, 0])
        qb = rms_norm(heads(px[..., NA_W:Q_W]), qk_norm_g[l, 2])
        ka, va, kb, vb = split_kv(px[..., Q_W:])
        ka = rms_norm(heads(ka), qk_norm_g[l, 1])
        kb = rms_norm(heads(kb), qk_norm_g[l, 3])
        va, vb = heads(va), heads(vb)
        qb = apply_axial_rope(qb, cos, sin)
        kb = apply_axial_rope(kb, cos, sin)

        ka_c, va_c, kb_c, vb_c = split_kv(pc_kv)
        ka_c = rms_norm(heads(ka_c), qk_norm_g[l, 1])
        kb_c = rms_norm(heads(kb_c), qk_norm_g[l, 3])
        va_c, vb_c = heads(va_c), heads(vb_c)

        out_a = neighbourhood_attention(qa, ka, va, ka_c, va_c, na_rpb[l])
        out_b = windowed_gqa_attention(qb, kb, vb, kb_c, vb_c, wa_sink[l])
        x = x + mod_x[..., 5, :] * (jnp.concatenate([out_a, out_b], axis=-1) @ w_out[l])

        if not last:
            qa_c = rms_norm(heads(pc[..., :NA_W]), qk_norm_g[l, 0])
            qb_c = rms_norm(heads(pc[..., NA_W:Q_W]), qk_norm_g[l, 2])
            out_a_c = context_self_attention(qa_c, ka_c, va_c, None)
            out_b_c = context_self_attention(qb_c, kb_c, vb_c, wa_sink[l])
            h_ctx = h_ctx + mod_c[..., 5, :] * (jnp.concatenate([out_a_c, out_b_c], axis=-1) @ w_out[l])

        x = swiglu_half_step(x, norm_g[l, 2], mod_x, 6, w_ffn_up[l, 1], w_ffn_down[l, 1])
        if not last:
            h_ctx = swiglu_half_step(h_ctx, norm_g[l, 2], mod_c, 6, w_ffn_up[l, 1], w_ffn_down[l, 1])
    return x


def setup_inputs(seed=0):
    out = dict(first_inputs(seed))
    for name, value in second_inputs(seed + 1).items():
        if name != "x":
            out[name + "_2"] = value
    return out


def reference(
    x, c, rel_bias, w_ada, b_ada, ln_g, ln_b, w_in_ab, diff_lambda, diff_subln_g, w_in_cd,
    forget_b, w_o, w_ffn_in, w_ffn_out, c_2, ctx_2, c_ctx_2, w_ada_2, b_ada_2, norm_g_2,
    w_ffn_up_2, w_ffn_down_2, w_in_2, w_out_2, qk_norm_g_2, na_rpb_2, wa_sink_2,
):
    x = first_block(
        x, c, rel_bias, w_ada, b_ada, ln_g, ln_b, w_in_ab, diff_lambda, diff_subln_g, w_in_cd,
        forget_b, w_o, w_ffn_in, w_ffn_out,
    )
    return second_block(
        x, c_2, ctx_2, c_ctx_2, w_ada_2, b_ada_2, norm_g_2, w_ffn_up_2, w_ffn_down_2, w_in_2,
        w_out_2, qk_norm_g_2, na_rpb_2, wa_sink_2,
    )


_drawn_inputs = setup_inputs


def setup_inputs(seed=0):
    import zlib

    import numpy as np

    out = dict(_drawn_inputs(seed))
    spreads = {}
    factors = {'b_ada': 3.955,
     'diff_subln_g': 8.0,
     'forget_b': 32.056,
     'b_ada_2': 2.797,
     'norm_g_2': 8.0,
     'qk_norm_g_2': 8.0,
     'na_rpb_2': 8.0,
     'wa_sink_2': 8.0}
    for name, (base, spread) in spreads.items():
        noise = np.random.default_rng([zlib.crc32(name.encode()), seed]).standard_normal(out[name].shape)
        drawn = base * np.exp(spread * noise) if base else spread * noise
        out[name] = jnp.asarray(drawn.astype(out[name].dtype))
    for name, factor in factors.items():
        out[name] = (out[name] * factor).astype(out[name].dtype)
    return out
```

```python
from contextlib import ExitStack

import numpy as np

import concourse.bass as bass
from concourse import mybir

F32 = mybir.dt.float32
F32R = mybir.dt.float32r
ALU = mybir.AluOpType
ACT = mybir.ActivationFunctionType
AX = mybir.AxisListType

P = 128
D = 1024
NT = D // P
T = 256
DFF = 2816
NF = DFF // P
DEPTH = 2
HD = 64
CW = 256
KC = 8
PIECE = 4
RAW = 4
ALPHA = (2 * DEPTH) ** 0.25
LN_EPS, NORM_EPS = 1e-5, 1e-6
SCALE = HD ** -0.5
LAMBDA_INIT = 0.8 - 0.6
NA_H = 8
RPB_H, RPB_W = 15, 31
NEG = -1e30
BIAS_L = 384
N_T5 = 20
NA_ROWS, NA_WIDTH = 7, 128


def shape_constants():
    f = np.float32
    c = {}
    c["ident"] = np.eye(P, dtype=f)
    c["ones"] = np.ones((P, P), f)
    half = np.arange(P) // HD
    c["head_ones"] = (half[:, None] == half[None, :]).astype(f)
    for kv in range(2):
        m = np.zeros((P, P), f)
        m[kv * HD + np.arange(P) % HD, np.arange(P)] = 1
        c[f"dup{kv}"] = m
    quarter = (np.arange(P) // 16) % 2
    m = np.zeros((P, P), f)
    for o in range(P):
        m[o + 16 if quarter[o] == 0 else o - 16, o] = -1 if quarter[o] == 0 else 1
    c["rotate"] = m
    inv = (f(10000.0) ** (-np.arange(0, 32, 2, dtype=f) / f(32))).astype(f)
    t = np.arange(T)
    pos = np.stack([(t // 64).astype(f), (t % 64).astype(f)])
    axis = (np.arange(P) // 32) % 2
    ang = (pos[axis] * inv[np.arange(P) % 16][:, None]).astype(f)
    c["cos"], c["sin"] = np.cos(ang).astype(f), np.sin(ang).astype(f)
    d = 255 - np.arange(BIAS_L)
    n = np.maximum(d, 0)
    nf = np.maximum(n, 1).astype(f)
    large = 16 + (np.log(nf / f(16)) / f(np.log(8.0)) * f(16)).astype(np.int32)
    bucket = np.where(n < 16, n, np.minimum(large, 31))
    c["bucket_onehot"] = (np.arange(32)[:, None] == bucket[None, :]).astype(f)
    count = (d <= 128).astype(int) + (d % 4 == 0) + (d % 16 == 0)
    dil = np.where((d >= 0) & (count > 0), np.log(np.maximum(count, 1)), NEG).astype(f)
    causal = np.where(d >= 0, 0, NEG).astype(f)
    c["t5_mask"] = np.stack([causal] * 4 + [dil] * 8 + [causal] * 8).astype(f)
    i, j = np.arange(P)[:, None], np.arange(T)[None, :]
    c["causal"] = np.where(P + i - j >= 0, 0, NEG).astype(f)
    col, kcol = (i % 64), (j % 64)
    c0 = np.clip(col - 8, 0, 48)
    c["neighbour"] = np.where((kcol >= c0) & (kcol < c0 + 16), 0, NEG).astype(f)
    c["window"] = np.concatenate([np.where(np.abs(P * q + i - j) <= 128, 0, NEG) for q in range(2)],
                                 axis=1).astype(f)
    neg = np.zeros((8, 8, P), f)
    for h in range(8):
        neg[h, h] = -1
    c["neg_select"] = neg.reshape(8, 8 * P)
    return c


class Tally:

    def __init__(self, sem, credit=0):
        self.sem, self.total, self.credit = sem, credit, credit

    def take(self, n):
        at = self.total
        self.total += n
        return at


class At:

    def __init__(self, reg, u, unroll, n):
        self.reg, self.u, self.unroll, self.n = reg, u, unroll, n

    def __call__(self, f):
        first = f(self.u)
        if self.reg is None:
            return first
        steps = [f(self.u + self.unroll * k) for k in range(self.n)]
        by = steps[1] - steps[0]
        assert all(b - a == by for a, b in zip(steps, steps[1:])), steps
        return self.reg * by + first if by else first


def each(eng, lo, hi, unroll, body, chain=None, links=0):
    n = (hi - lo) // unroll
    if n < 2:
        for s in range(lo, hi):
            body(At(None, s, 1, 1))
        return
    with eng.Fori(0, n) as reg:
        if chain:
            chain.enter(reg, links)
        for u in range(unroll):
            body(At(reg, lo + u, unroll, n))
        if chain:
            chain.leave(n)
    for s in range(lo + n * unroll, hi):
        body(At(None, s, 1, 1))


class Chain:

    def __init__(self, eng, sem):
        self.eng, self.sem, self.k, self.reg, self.per = eng, sem, 0, None, 0

    def enter(self, reg, per):
        self.reg, self.per, self.start = reg, per, self.k

    def leave(self, n):
        assert self.k - self.start == self.per, (self.k - self.start, self.per)
        self.k, self.reg = self.start + n * self.per, None

    def link(self, ins):
        self.k += 1
        ins.then_inc(self.sem, 1)
        self.eng.wait_ge(self.sem, self.reg * self.per + self.k if self.reg is not None else self.k)


class Chunk:
    def __init__(self, n, kind, weight, k0, kt, c0, cw, order):
        self.n, self.kind, self.weight = n, kind, weight
        self.k0, self.kt, self.c0, self.cw, self.order = k0, kt, c0, cw, order
        self.pieces = []


class Piece:
    def __init__(self, g, chunk, k0, kt):
        self.g, self.chunk, self.k0, self.kt = g, chunk, k0, kt


class Stage:

    def __init__(self, kind, *, a_out=None, ada=None, bias=None, bias_in=None, chunks=None, diff=None,
                 first=None, gain=None, gain_b=None, gate=None, groups=None, h_wait=None, half=None, hidden=None,
                 hi=None, host=None, items=None, koff=None, ktile=None, last_ln=None, layer=None, logits=None,
                 mm=None, n=None, name=None, nblk=None, normed=None, o_wait=None, out=None, pairs=None,
                 q_in=None, qoff=None, qtile=None, ready=None, rmm=None, ro=None, rows=None, rt=None, scale=None,
                 shift=None, silu=None, sink=None, sq=None, steps=None, take=None, unroll=None, vblk=None,
                 vcol=None, vrow=None, vw=None, what=None, x=None, x_out=None, a32=None):
        self.kind, self.a_out, self.ada, self.bias, self.bias_in = kind, a_out, ada, bias, bias_in
        self.chunks, self.diff, self.first, self.gain, self.gain_b = chunks, diff, first, gain, gain_b
        self.gate, self.groups, self.h_wait, self.half, self.hidden = gate, groups, h_wait, half, hidden
        self.hi, self.host, self.items, self.koff, self.ktile = hi, host, items, koff, ktile
        self.last_ln, self.layer, self.logits, self.mm, self.n = last_ln, layer, logits, mm, n
        self.name, self.nblk, self.normed, self.o_wait, self.out = name, nblk, normed, o_wait, out
        self.pairs, self.q_in, self.qoff, self.qtile, self.ready = pairs, q_in, qoff, qtile, ready
        self.rmm, self.ro, self.rows, self.rt, self.scale = rmm, ro, rows, rt, scale
        self.shift, self.silu, self.sink, self.sq, self.steps = shift, silu, sink, sq, steps
        self.take, self.unroll, self.vblk, self.vcol, self.vrow = take, unroll, vblk, vcol, vrow
        self.vw, self.what, self.x, self.x_out, self.a32 = vw, what, x, x_out, a32


class Group:

    def __init__(self, n, tally, done):
        self.n, self.tally, self.done = n, tally, done


class Item:

    def __init__(self, what, chunk, grp):
        self.what, self.chunk, self.grp = what, chunk, grp


class Rows:

    def __init__(self, chunks, host, grp):
        self.chunks, self.host, self.grp = chunks, host, grp


class Step:

    def __init__(self, g, u, hosts, gg, ug):
        self.g, self.u, self.hosts, self.gg, self.ug = g, u, hosts, gg, ug


def build(nc, a, c, out):
    ctx = ExitStack()
    with ctx:
        _build(nc, ctx, a, c, out)


def _build(nc, ctx, a, c, out):
    def sem(name):
        return ctx.enter_context(nc.semaphore(name))

    def sb(name, shape, dt=F32):
        return ctx.enter_context(nc.sbuf_tensor(name, shape, dt))

    X = sb("X", [P, NT, 2 * T])
    HH = sb("H_hi", [P, NT, 2 * T], F32R)
    HL = sb("H_lo", [P, NT, 2 * T], F32R)
    RAWS = sb("raw_weights", [P, RAW, KC * CW])
    WH = sb("weight_hi", [P, 2, PIECE * CW], F32R)
    WL = sb("weight_lo", [P, 2, PIECE * CW], F32R)
    T1 = sb("tmp1", [P, 2, 2 * T])
    T2 = sb("tmp2", [P, 2, 2 * T])
    RB = sb("rstd", [P, 2 * T])
    ident = sb("ident", [P, P])
    ones = sb("ones", [P, P])
    head_ones = sb("head_ones", [P, P])
    rotate = sb("rotate", [P, P])
    dup = [sb(f"dup{k}", [P, P]) for k in range(2)]
    SILU_C = sb("silu_c", [P, 24])
    C_COLS = sb("c_cols", [P, 24])
    B1 = sb("b_ada_cols", [P, 2, 48])
    B2 = sb("b_ada2_cols", [P, 2, 72])
    G_COLS = sb("gain_cols", [P, 112])
    E_COLS = sb("head_gain_cols", [P, 9])
    AD = [sb("ada0", [P, 48, 1]), sb("ada1", [P, 48, 1]), sb("ada2", [P, 72, 2]), sb("ada3", [P, 72, 2])]
    GS = sb("gain_scale", [P, NT, 2])
    EPS = sb("eps", [P, 2])
    SINK = sb("sink", [P, 16])
    LAM = sb("lam", [P, 8])
    FB = sb("forget_bias", [8, 1])
    NM = sb("neg_max", [P, 4])
    RS = sb("row_sum", [P, 4])
    ES = sb("sink_exp", [P, 4])
    RI = sb("row_scale", [P, 4])
    CUMT = sb("cum_cols", [P, 2, 8])

    base = (nc.sbuf_base + 63) // 64 * 64
    used = {"at": base}

    def region(name, shape, dt=F32, at=None):
        size = 4 * int(np.prod(shape[1:]))
        if at is None:
            at = used["at"]
            used["at"] = at + (size + 31) // 32 * 32
        return nc.alloc_sbuf_tensor_at(name, shape, dt, offset=at)

    AH = region("hidden_hi", [P, NF, 2 * T], F32R)
    AL = region("hidden_lo", [P, NF, 2 * T], F32R)
    used["at"] = base
    QB = region("q", [P, 8, 2 * T])
    KB = region("k", [P, 8, 2 * T])
    VB = region("v", [P, 4 * 640])
    PR = region("probs", [P, 4, 512])
    PT = region("probs_turned", [P, 4, 4, P])
    BT = region("bias", [P, 4096])
    OF = region("o_diff", [P, 4, T])
    QS = region("q_pair", [P, T])
    KS = region("k_pair", [P, 2 * T])
    VS = region("v_pair", [P, 4, P])
    COS = region("cos", [P, T])
    SIN = region("sin", [P, T])
    CAUSAL = region("causal", [P, T])
    NEIGH = region("neighbour", [P, T])
    WINDOW = region("window", [P, 2, T])
    assert used["at"] <= nc.sbuf_usable_end and base + 2 * NF * 2 * T * 4 <= nc.sbuf_usable_end
    used["at"] = base
    XIN = region("x_rows", [P, 2, D])
    CIN = region("ctx_rows", [P, 2, D])
    ROWS = [region(f"rows{k}", [n, P]) for k, n in enumerate((120, 72, 72, 112, 9))]
    ONEHOT = region("onehot", [32, BIAS_L])
    TABLE = region("table", [32, N_T5])
    T5MASK = region("t5_mask", [N_T5, BIAS_L])
    T5ROW = region("t5_rows", [N_T5, BIAS_L])
    RPB = region("rpb_rows", [NA_H, 2, NA_ROWS, NA_WIDTH])
    LROW = region("lambda_rows", [P, 4, HD])
    LPROD = region("lambda_prod", [P, 2, HD])
    assert used["at"] <= nc.sbuf_usable_end
    OUTR = XIN
    FD = PR[0:8, 0, 0:T]
    FD_ABS = PR[0:8, 0, T:2 * T]
    FD_MIN = PR[0:8, 1, 0:T]
    CUM = PR[0:8, 1, T:2 * T]
    FD_ONE = PT[0:8, 0, 0:2, :]
    NEGSEL = PT[0:8, 1:3, :, :]

    BANK = [ctx.enter_context(nc.psum_tensor(f"bank{b}", [P, 512], F32)) for b in range(8)]
    PAIR = [(BANK[0], BANK[1]), (BANK[2], BANK[3])]
    B_T, B_STAT, B_ADA = (BANK[4], BANK[5]), BANK[6], BANK[7]

    t5_dram = nc.dram_tensor("t5_skew", (N_T5, P, BIAS_L), F32, kind="Internal").ap()
    na_dram = nc.dram_tensor("na_skew", (2, NA_H, 64, NA_ROWS * NA_WIDTH), F32, kind="Internal").ap()

    landed = [sem(f"chunk_landed{i}") for i in range(RAW)]
    hi_done, lo_done = sem("hi_done"), sem("lo_done")
    piece_used = Tally(sem("piece_used"), 2)
    ada_used, ada_out = sem("ada_used"), Tally(sem("ada_out"), 1)
    ev_act, ev_dve = Tally(sem("evac_act"), 2), Tally(sem("evac_dve"), 2)
    const_in, rows_in, setup_mm = sem("const_in"), sem("rows_in"), sem("setup_mm")
    setup_act, t5_rows, region_free = sem("x_turned"), sem("t5_rows_ready"), sem("lambda_done")
    skew_out, skew_src = sem("skew_out"), sem("skew_src")
    silu_done, cols_done = sem("silu_done"), sem("cols_done")
    lam_sum, lam_exp = sem("lambda_sums"), sem("lambda_exp")
    h_ready = Tally(sem("h_ready"), 2)
    mod_src, mod_hi, mod_t2 = Tally(sem("mod_src")), Tally(sem("mod_hi")), Tally(sem("mod_t2"), 2)
    centred = Tally(sem("centred"))
    stat_in, stat_mm = Tally(sem("stat_in")), Tally(sem("stat_mm"), 2)
    rstd_sq, mean_mm, x_ready = Tally(sem("rstd_sqrt")), Tally(sem("mean_mm")), Tally(sem("x_ready"))
    silu_g, act32, act_hi = Tally(sem("silu_g")), Tally(sem("act32"), 1), Tally(sem("act_hi"))
    act_ready = Tally(sem("act_ready"), 1)
    bias_in = Tally(sem("bias_in"))
    fg_x, fg_abs, fg_exp = sem("forget_logit"), sem("forget_abs"), sem("forget_exp")
    fg_cum, fg_sel, fg_mm, fg_free = sem("forget_cum"), sem("forget_select"), sem("forget_mm"), sem("forget_free")
    qn_sq, qn_mm, qn_rt = Tally(sem("qknorm_sq")), Tally(sem("qknorm_mm"), 2), Tally(sem("qknorm_root"), 2)
    qn_out = Tally(sem("qknorm_out"), 2)
    rope_mm, rope_out = Tally(sem("rope_mm")), Tally(sem("rope_out"), 1)
    q_staged, v_staged = Tally(sem("q_staged")), Tally(sem("v_staged"))
    scores, nmax = Tally(sem("scores"), 4), Tally(sem("neg_max_ready"))
    sink_done = Tally(sem("sink_exp_done"))
    exp_done, probs = Tally(sem("exp_done"), 4), Tally(sem("probs_ready"))
    turned, copied = Tally(sem("probs_turned"), 4), Tally(sem("turned_copied"), 2)
    pv_done, o_done = Tally(sem("pv_done"), 1), Tally(sem("o_done"), 1)
    sub_sq, sub_mm, sub_rt, sub_out = sem("sub_sq"), sem("sub_mm"), sem("sub_root"), sem("sub_out")
    dve_chain, act_chain, pool_chain = sem("dve_chain"), sem("act_chain"), sem("pool_chain")
    out_mm, out_cp, out_dma = sem("out_mm"), sem("out_cp"), sem("out_dma")
    credited = [piece_used, ada_out, ev_act, ev_dve, h_ready, mod_t2, act32, stat_mm, act_ready, qn_mm, qn_rt,
                qn_out, rope_out, scores, exp_done, turned, copied, pv_done, o_done]

    CHUNKS, PIECES, GROUPS = [], [], []
    W = {"ada": [a["w_ada"][0], a["w_ada"][1], a["w_ada_2"][0], a["w_ada_2"][1]]}
    counts = {"a": 0}

    def view(w):
        return w.rearrange("(t p) n -> p t n", p=P)

    def chunk(kind, w, k0, kt, c0, cw=CW, order=None):
        ch = Chunk(len(CHUNKS), kind, w, k0, kt, c0, cw, order)
        CHUNKS.append(ch)
        if kind == "g":
            for k in range(0, kt, PIECE):
                pc = Piece(len(PIECES), ch, k, min(PIECE, kt - k))
                PIECES.append(pc)
                ch.pieces.append(pc)
        else:
            ch.raw_order = counts["a"]
            counts["a"] += 1
        return ch

    def group(engine):
        tally = ev_act if engine == "act" else ev_dve
        g = Group(n=len(GROUPS), tally=tally, done=tally.take(1) + 1)
        GROUPS.append(g)
        return g

    ada_at = {"m": 0, "c": 0}
    ADA_CHUNKS = [24, 24, 36, 36]

    def ada_chunk():
        m, k = ada_at["m"], ada_at["c"]
        ch = chunk("a", view(W["ada"][m]), 0, KC, CW * k, order=(m, k))
        ch.out = ada_out.take(1) + 1
        ada_at["c"] += 1
        if ada_at["c"] == ADA_CHUNKS[m]:
            ada_at.update(m=m + 1, c=0)
        return ch

    PLAN = []
    state = {"q_in": 0, "normed": None}
    def add(kind, **k):
        now = dict(h_wait=h_ready.total, o_wait=o_done.total, a_out=ada_out.total, x=x_ready.total,
                   bias_in=bias_in.total, last_ln=False, logits=counts["a"])
        PLAN.append(Stage(kind, **{**now, **k}))
        return PLAN[-1]

    def ada_run(n):
        add("ada", chunks=[ada_chunk() for _ in range(n)])

    def mod(kind, ada, shift, scale, n, gain=None, gain_b=None, last_ln=False):
        s = add(kind, ada=ada, shift=shift, scale=scale, n=n, gain=gain, gain_b=gain_b, last_ln=last_ln)
        if kind != "mod":
            s.x = x_ready.total
            s.stat_in, s.stat = stat_in.take(8), stat_mm.take(8)
            s.rstd = rstd_sq.take(1)
            if kind == "ln":
                s.mean, s.cen = mean_mm.take(1), centred.take(8)
        if kind == "ln":
            s.x_out = x_ready.take(1)
        if not last_ln:
            s.src = mod_src.take(8) if kind != "mod" else None
            s.hi, s.t2, s.h = (t.take(8) for t in (mod_hi, mod_t2, h_ready))

    def ffn(w_in, w_out, n, ada, gate, half, hosted, first):
        steps = []
        host = hosted and ada_at["m"] < 4 and ADA_CHUNKS[ada_at["m"]] - ada_at["c"] >= 22
        for s in range(NF // 2):
            g = chunk("g", view(w_in), 0, KC, CW * s)
            h1 = ada_chunk() if host else None
            u = chunk("g", view(w_in), 0, KC, DFF + CW * s)
            h2 = ada_chunk() if host else None
            steps.append(Step(g=g, u=u, hosts=[h1, h2] if host else [None, None],
                               gg=group("act"), ug=group("dve")))
        add("ffn_in", n=n, steps=steps, silu=silu_g.take(11), a32=act32.take(11), hi=act_hi.take(11),
            ready=act_ready.take(11), host=host)
        groups = []
        host = hosted and ada_at["m"] < 4 and ADA_CHUNKS[ada_at["m"]] - ada_at["c"] >= 4
        for m in range(4):
            cs = [chunk("g", view(w_out), k, min(KC, NF - k), CW * m) for k in range(0, NF, KC)]
            groups.append(Rows(chunks=cs, host=ada_chunk() if host else None, grp=group("dve")))
        add("proj", n=n, groups=groups, ada=ada, gate=gate, half=half, hidden=True, first=first,
            ready=act_ready.total, x_out=x_ready.take(1))

    def w_out(w, n, ada, gate, first):
        groups = [Rows(chunks=[chunk("g", view(w), 0, KC, CW * m)], host=None, grp=group("dve"))
                  for m in range(4)]
        add("proj", n=n, groups=groups, ada=ada, gate=gate, half=False, hidden=False, first=first,
            ready=o_done.total, x_out=x_ready.take(1))

    def qkv(w, items, n):
        st = add("qkv", n=n, items=[], ready=h_ready.total, first=n == T)
        for c0, what in items:
            if what[0] == "forget":
                st.items.append(Item(what=what, chunk=chunk("f", view(w), 0, KC, c0, 8), grp=None))
            else:
                st.items.append(Item(what=what, chunk=chunk("g", view(w), 0, KC, c0),
                                      grp=group("act")))
        st.done = ev_act.total
        state.update(q_in=st.done, normed=None)

    def attention(name, pairs, unroll, **k):
        s = add("attn", name=name, pairs=pairs, unroll=unroll, **state, **k)
        s.tper = 2 if s.diff else 4
        s.units, s.bias_in = 4 * pairs, bias_in.total
        s.q, s.v = q_staged.take(pairs), v_staged.take(pairs)
        s.sc, s.mx, s.ex = scores.take(s.units), nmax.take(s.units), exp_done.take(s.units)
        s.sk = sink_done.take(s.units) if s.sink else None
        s.pb, s.tu, s.cp = (t.take(s.tper * pairs) for t in (probs, turned, copied))
        s.pv, s.o = pv_done.take(pairs), o_done.take(pairs)

    def causal_heads(name, q, k, vcol, out_tile, bias, diff=False):
        attention(name, 4, 1, diff=diff, sink=None, qtile=lambda p: q + p, ktile=lambda p: k + p,
                  vcol=lambda p: vcol + P * p, vw=P, vblk=0, vrow=D, nblk=lambda qt: qt + 1, qoff=0, koff=0,
                  bias=bias, out=lambda p: out_tile + p)

    def t5(h0):
        def bias(p, hh, qt):
            return "bias", T * (h0(p, hh)) + (P if qt == 0 else 0), P * (qt + 1)
        return bias

    add("setup")
    ada_run(24)
    mod("mod", 0, 0, 1, T)
    qkv(a["w_in_ab"][0],
        [(0, ("q", 0)), (256, ("q", 2)), (512, ("k", 0)), (768, ("k", 2)), (1024, ("v", 0)), (1280, ("v", 256)),
         (1536, ("q", 4)), (1792, ("q", 6)), (2048, ("k", 4)), (2304, ("k", 6)), (2560, ("v", 512)),
         (2816, ("v", 768))], T)
    add("bias", what="t5", rows=(0, 12), take=bias_in.take(32))
    causal_heads("differential", 0, 0, 0, 0, t5(lambda p, hh: p), diff=True)
    add("sub_norm")
    causal_heads("dilated", 4, 4, 512, 4, t5(lambda p, hh: 4 + 2 * p + hh))
    w_out(a["w_o"][0], T, 0, 2, True)
    mod("ln", 0, 3, 4, T, gain=0, gain_b=32)
    ffn(a["w_ffn_in"][0], a["w_ffn_out"][0], T, 0, 5, False, True, True)
    ada_run(2 if ada_at["m"] == 1 else 0)
    mod("ln", 1, 0, 1, T, gain=8, gain_b=40)
    qkv(a["w_in_cd"][0],
        [(0, ("q", 0)), (256, ("q", 2)), (512, ("k", 0)), (768, ("k", 2)), (1024, ("v", 0)), (1280, ("v", 256)),
         (1536, ("q", 4)), (1792, ("q", 6)), (2048, ("k", 4)), (2304, ("k", 6)), (2560, ("v", 512)),
         (2816, ("v", 768)), (3072, ("forget",))], T)
    add("bias", what="t5", rows=(12, 8), take=bias_in.take(32))
    causal_heads("moba", 0, 0, 0, 0, t5(lambda p, hh: 2 * p + hh))
    add("forget_bias")
    causal_heads("forget", 4, 4, 512, 4,
                 lambda p, hh, qt: ("bias", 512 * (2 * p + hh) + T * qt, P * (qt + 1)))
    w_out(a["w_o"][1], T, 1, 2, True)
    mod("ln", 1, 3, 4, T, gain=16, gain_b=48)
    ffn(a["w_ffn_in"][1], a["w_ffn_out"][1], T, 1, 5, False, True, True)
    mod("ln", 1, 0, 0, T, gain=24, gain_b=56, last_ln=True)
    ada_run(ADA_CHUNKS[2] - ada_at["c"])
    for l in range(DEPTH):
        last = l == DEPTH - 1
        n = 2 * T
        mod("rms", 2 + l, 0, 1, n, gain=64 + 24 * l)
        ffn(a["w_ffn_up_2"][l, 0], a["w_ffn_down_2"][l, 0], n, 2 + l, 2, True, True, False)
        mod("rms", 2 + l, 3, 4, n, gain=64 + 24 * l + 8)
        qkv(a["w_in_2"][l],
            [(0, ("q", 0)), (256, ("q", 2)), (512, ("q", 4)), (768, ("q", 6)), (1024, ("k", 0)),
             (1280, ("k", 2)), (1536, ("v", 0)), (1792, ("v", 256)), (2048, ("kv",))], n)
        add("bias", what="na", layer=l, take=bias_in.take(16 * 36))
        add("qk_norm", layer=l, sq=qn_sq.take(13), mm=qn_mm.take(13), rt=qn_rt.take(13),
            out=qn_out.take(13), rmm=rope_mm.take(7), ro=rope_out.take(7), q_in=state["q_in"],
            bias_in=bias_in.total)
        state["normed"] = (qn_out.total, rope_out.total)
        two = dict(diff=False, nblk=lambda qt: 4, qoff=0, koff=0, vblk=0, vrow=640)
        attention("neighbourhood", 4, 1, sink=None, qtile=lambda p: p, ktile=lambda p: p,
                  vcol=lambda p: P * p, vw=P,
                  bias=lambda p, hh, qt: ("bias", 512 * (2 * p + hh) + T * qt, T), out=lambda p: p, **two)
        attention("window", 4, 2, sink=(lambda p, hh: 8 * l + 2 * p + hh) if l == 0 else
                  (lambda p, hh: 8 + 2 * p + hh), qtile=lambda p: 4 + p, ktile=lambda p: 5 + p // 2,
                  vcol=lambda p: 512 + HD * (p // 2), vw=HD,
                  bias=lambda p, hh, qt: ("window", qt, T), out=lambda p: 4 + p, **two)
        if not last:
            one = dict(diff=False, nblk=lambda qt: 2, qoff=T, koff=T, vblk=2, vrow=640, bias=None)
            attention("context_a", 4, 1, sink=None, qtile=lambda p: p, ktile=lambda p: p,
                      vcol=lambda p: P * p, vw=P, out=lambda p: p, **one)
            attention("context_b", 4, 2, sink=lambda p, hh: 2 * p + hh, qtile=lambda p: 4 + p,
                      ktile=lambda p: 5 + p // 2, vcol=lambda p: 512 + HD * (p // 2), vw=HD,
                      out=lambda p: 4 + p, **one)
        n2 = T if last else 2 * T
        w_out(a["w_out_2"][l], n2, 2 + l, 5, False)
        mod("rms", 2 + l, 6, 7, n2, gain=64 + 24 * l + 16)
        ffn(a["w_ffn_up_2"][l, 1], a["w_ffn_down_2"][l, 1], n2, 2 + l, 8, True, False, False)
        if not last:
            ada_run(ADA_CHUNKS[3] - ada_at["c"])
    add("finish")
    ada_ready = {}
    for ch in CHUNKS:
        if ch.kind == "a":
            ada_ready[ch.order[0]] = ch.out
    bias_stages = [s for s in PLAN if s.kind == "bias"]

    def raw_ap(n, kt, cw):
        return RAWS[:, n % RAW, 0:kt * cw].rearrange("p (t n) -> p t n", t=kt)

    def wait_landed(eng, at, f):
        eng.wait_ge(landed[f(at.u).n % RAW], at(lambda s: 16 * (f(s).n // RAW + 1)))

    def wait_slot(eng, at, f):
        if f(at.u).n < RAW:
            return
        before = lambda s: CHUNKS[f(s).n - RAW]
        if before(at.u).kind == "g":
            eng.wait_ge(lo_done, at(lambda s: before(s).pieces[-1].g + 1))
        else:
            eng.wait_ge(ada_used, at(lambda s: before(s).raw_order + 1))

    act_waited, pool_waited = sem("act_waited"), sem("pool_waited")

    def wait_apart(eng, on, value, count):
        eng.wait_ge(on, value)
        eng.sem_inc(count, 1)

    block = ctx.enter_context(nc.Block())

    @block.sync
    def _(sp):
        def load(at, f):
            ch = f(at.u)
            wait_slot(sp, at, f)
            src = ch.weight[:, ch.k0:ch.k0 + ch.kt, bass.ds(at(lambda s: f(s).c0), ch.cw)]
            sp.dma_start(raw_ap(ch.n, ch.kt, ch.cw), src).then_inc(landed[ch.n % RAW], 16)

        def load_one(ch):
            load(At(None, 0, 1, 1), lambda s: ch)

        def ffn_in(s):
            parts = 2 if not s.host else 4

            def step(at):
                load(at, lambda k: s.steps[k].g)
                if s.host:
                    load(at, lambda k: s.steps[k].hosts[0])
                load(at, lambda k: s.steps[k].u)
                if s.host:
                    load(at, lambda k: s.steps[k].hosts[1])
            step(At(None, 0, 1, 1))
            if not s.host:
                step(At(None, 1, 1, 1))
                each(sp, 2, 10, 2, step)
                step(At(None, 10, 1, 1))
            else:
                each(sp, 1, 11, RAW // parts, step)

        for s in PLAN:
            if s.kind == "ada":
                for ch in s.chunks:
                    load_one(ch)
            elif s.kind == "qkv":
                for it in s.items:
                    load_one(it.chunk)
            elif s.kind == "ffn_in":
                ffn_in(s)
            elif s.kind == "proj":
                for g in s.groups:
                    for ch in g.chunks:
                        load_one(ch)
                    if g.host:
                        load_one(g.host)
        sp.wait_ge(out_cp, 4)
        sp.dma_start(out.rearrange("a (q p) d -> p (a q) d", p=P), OUTR[:, :, :]).then_inc(out_dma, 16)
        sp.wait_ge(out_dma, 16)

    @block.gpsimd
    def _(pool):
        chain = Chain(pool, pool_chain)
        loads = {"const": 0, "rows": 0}

        def const(dst, src):
            loads["const"] += 16
            pool.dma_start(dst, src).then_inc(const_in, 16)

        def rows(dst, src):
            loads["rows"] += 16
            pool.dma_start(dst, src).then_inc(rows_in, 16)

        def setup():
            for t in credited:
                pool.sem_inc(t.sem, t.credit)
            rows(ROWS[0][0:8, :], a["c"].rearrange("a (t p) -> (a t) p", p=P))
            rows(ROWS[0][8:16, :], a["c_2"].rearrange("a (t p) -> (a t) p", p=P))
            rows(ROWS[0][16:24, :], a["c_ctx_2"].rearrange("(t p) -> t p", p=P))
            rows(ROWS[0][24:120, :], a["b_ada"].rearrange("l (t p) -> (l t) p", p=P))
            rows(ident[:, :], c["ident"])
            rows(ones[:, :], c["ones"])
            for l in range(2):
                rows(ROWS[1 + l][:, :], a["b_ada_2"][l].rearrange("(t p) -> t p", p=P))
            rows(ROWS[3][0:32, :], a["ln_g"].rearrange("l j (t p) -> (l j t) p", p=P))
            rows(ROWS[3][32:64, :], a["ln_b"].rearrange("l j (t p) -> (l j t) p", p=P))
            rows(ROWS[3][64:112, :], a["norm_g_2"].rearrange("l j (t p) -> (l j t) p", p=P))
            rows(ROWS[4][0:1, :], a["diff_subln_g"])
            for hf in range(2):
                rows(ROWS[4][1:9, hf * HD:(hf + 1) * HD], a["qk_norm_g_2"].rearrange("l j d -> (l j) d"))
            rows(XIN[:, :, :], a["x"].rearrange("a (q p) d -> p (a q) d", p=P))
            rows(CIN[:, :, :], a["ctx_2"].rearrange("a (q p) d -> p (a q) d", p=P))
            const(head_ones[:, :], c["head_ones"])
            const(rotate[:, :], c["rotate"])
            for k in range(2):
                const(dup[k][:, :], c[f"dup{k}"])
            const(ONEHOT[:, :], c["bucket_onehot"])
            const(T5MASK[:, :], c["t5_mask"])
            const(TABLE[:, 0:12], a["rel_bias"])
            const(TABLE[:, 12:20], a["rel_bias"][:, 0:8])
            const(SINK[:, :], a["wa_sink_2"].rearrange("l h -> (l h)").rearrange("(o n) -> o n", o=1)
                  .broadcast_to([P, 16]))
            const(FB[:, :], a["forget_b"].rearrange("l h -> h l"))
            const(LROW[:, :, :], a["diff_lambda"].broadcast_to([P, 4, HD]))
            chain.link(pool.memset(RPB[:, :, :, :], 0.0))
            for l in range(2):
                pool.dma_start(RPB[:, l, :, 48:48 + RPB_W],
                               a["na_rpb_2"][l, :, 4:4 + NA_ROWS, :]).then_inc(skew_src, 16)
            pool.wait_ge(skew_src, 32)
            for l in range(2):
                src = RPB[:, l, :, :].rearrange("h i w -> h (i w)")
                pool.dma_start(na_dram[l], src[:, None, :].broadcast_to([NA_H, 64, NA_ROWS * NA_WIDTH])
                               ).then_inc(skew_out, 16)
            pool.wait_ge(t5_rows, 1)
            pool.dma_start(t5_dram, T5ROW[:, None, :].broadcast_to([N_T5, P, BIAS_L])).then_inc(skew_out, 16)
            pool.wait_ge(skew_out, 48)

        def bias(s):
            pool.wait_ge(region_free, 1)
            pool.wait_ge(h_ready.sem, s.h_wait)
            if s.what == "t5":
                h0, n = s.rows
                src = bass.AP(t5_dram.tensor, h0 * P * BIAS_L + P - 1,
                              [[BIAS_L - 1, P], [P * BIAS_L, n], [1, T]])
                pool.dma_start(BT[:, 0:n * T].rearrange("p (h k) -> p h k", h=n), src).then_inc(bias_in.sem, 16)
                pool.dma_start(CAUSAL[:, :], c["causal"]).then_inc(bias_in.sem, 16)
            else:
                row = NA_ROWS * NA_WIDTH
                for q in range(4):
                    half, qt = q % 2, q // 2
                    for h in range(NA_H):
                        src = bass.AP(na_dram.tensor, (s.layer * NA_H + h) * 64 * row + (3 - q) * NA_WIDTH + 63,
                                      [[row - 1, 64], [NA_WIDTH, 4], [1, 64]])
                        dst = BT[64 * half:64 * half + 64, 512 * h + T * qt:512 * h + T * qt + T]
                        pool.dma_start(dst.rearrange("p (i k) -> p i k", i=4), src).then_inc(bias_in.sem, 16)
                for d, nm in ((COS, "cos"), (SIN, "sin"), (NEIGH, "neighbour")):
                    pool.dma_start(d[:, :], c[nm]).then_inc(bias_in.sem, 16)
                pool.dma_start(WINDOW[:, :, :].rearrange("p q k -> p (q k)"), c["window"]
                               ).then_inc(bias_in.sem, 16)

        def low(s):
            def tile(at):
                par = at.u % 2
                t = at(lambda k: k)
                pool.wait_ge(mod_hi.sem, at(lambda k: s.hi + k + 1))
                pool.wait_ge(mod_t2.sem, at(lambda k: s.t2 + k + 1))
                pool.tensor_tensor(HL[:, bass.ds(t, 1), 0:s.n], T2[:, par:par + 1, 0:s.n],
                                   HH[:, bass.ds(t, 1), 0:s.n].bitcast(F32), ALU.subtract
                                   ).then_inc(h_ready.sem, 1)
            each(pool, 0, 8, 2, tile)

        def ffn_in(s):
            def step(at):
                t = at(lambda k: 2 * k)
                pool.wait_ge(act_hi.sem, at(lambda k: s.hi + k + 1))
                pool.tensor_tensor(AL[:, bass.ds(t, 2), 0:s.n], T2[:, :, 0:s.n],
                                   AH[:, bass.ds(t, 2), 0:s.n].bitcast(F32), ALU.subtract
                                   ).then_inc(act_ready.sem, 1)
            each(pool, 0, 11, 1, step)

        def attn(s):
            vb = VB[:, 0:4 * s.vrow if s.vrow == 640 else 2 * s.vrow].rearrange("p (b n) -> p b n", n=s.vrow)
            nb = s.nblk(1)

            def pair(at):
                wait_apart(pool, scores.sem, at(lambda p: s.sc + 4 * p), pool_waited)
                pool.tensor_copy(QS[:, :], QB[:, bass.ds(at(s.qtile), 1), s.qoff:s.qoff + T]
                                 .rearrange("p o t -> p (o t)"))
                nk = P * nb
                pool.tensor_copy(KS[:, 0:nk], KB[:, bass.ds(at(s.ktile), 1), s.koff:s.koff + nk]
                                 .rearrange("p o t -> p (o t)")).then_inc(q_staged.sem, 1)
                wait_apart(pool, pv_done.sem, at(lambda p: s.pv + p), pool_waited)
                pool.tensor_copy(VS[:, 0:nb, 0:s.vw], vb[:, s.vblk:s.vblk + nb, bass.ds(at(s.vcol), s.vw)]
                                 ).then_inc(v_staged.sem, 1)
            pool.wait_ge(ev_act.sem, s.q_in)
            if s.normed:
                pool.wait_ge(qn_out.sem, s.normed[0])
                pool.wait_ge(rope_out.sem, s.normed[1])
            each(pool, 0, s.pairs, s.unroll, pair)

        for s in PLAN:
            if s.kind == "setup":
                setup()
            elif s.kind in ("mod", "ln", "rms") and not s.last_ln:
                low(s)
            elif s.kind == "ffn_in":
                ffn_in(s)
            elif s.kind == "bias":
                bias(s)
            elif s.kind == "forget_bias":
                pool.wait_ge(o_done.sem, s.o_wait)
                pool.dma_start(NEGSEL, c["neg_select"].rearrange("h (a b p) -> h a b p", a=2, b=4)
                               ).then_inc(fg_sel, 16)
            elif s.kind == "attn":
                attn(s)


    @block.tensor
    def _(pe):
        def mm(o, w, x, start, stop):
            return pe.matmul(o, w, x, start=start, stop=stop, skip_group_check=True)

        def product(o, kt, wh, wl, xh, xl, start, stop):
            mm(o, wh, xh, start, False)
            mm(o, wh, xl, False, False)
            return mm(o, wl, xh, False, stop)

        def ada(at, f):
            ch = f(at.u)
            m = ch.order[0]
            nv = 1 if m < 2 else 2
            wait_landed(pe, at, f)
            pe.wait_ge(ada_out.sem, at(lambda s: f(s).out - 1))
            w = raw_ap(ch.n, KC, CW)
            for j in range(2):
                for k in range(KC):
                    cv = SILU_C[:, k:k + 1] if m < 2 else SILU_C[:, 8 + 2 * k:10 + 2 * k]
                    ins = mm(B_ADA[:, j * nv:(j + 1) * nv], w[:, k, j * P:(j + 1) * P], cv, k == 0, k == KC - 1)
            ins.then_inc(ada_used, 1)

        def wait_bank(at, f):
            g = f(at.u)
            if g.n >= 2:
                before = lambda s: GROUPS[f(s).n - 2]
                pe.wait_ge(before(at.u).tally.sem, at(lambda s: before(s).done))

        def features(at, f, grp, kt_all, k_base, xh, xl, n, width=2, left=None):
            ch = f(at.u)
            for i, pc in enumerate(ch.pieces):
                pe.wait_ge(lo_done, at(lambda s: f(s).pieces[i].g + 1))
                wh = WH[:, pc.g % 2, :].rearrange("p (t n) -> p t n", n=CW)
                wl = WL[:, pc.g % 2, :].rearrange("p (t n) -> p t n", n=CW)
                for k in range(pc.kt):
                    kk = k_base + pc.k0 + k
                    for j in range(width):
                        ins = product(PAIR[grp.n % 2][j][:, 0:n], kk, wh[:, k, j * P:(j + 1) * P],
                                      wl[:, k, j * P:(j + 1) * P], xh[:, kk, 0:n], xl[:, kk, 0:n],
                                      kk == 0, kk == kt_all - 1)
                    if left:
                        ins = left(wh, wl, k, kk)
                ins.then_inc(piece_used.sem, 1)

        def tokens(ch, grp, n, col, cw, bank_of, at_col):
            def part(wh, wl, k, kk):
                for tt in range(n // P):
                    o = bank_of(tt)[:, at_col(tt):at_col(tt) + cw]
                    first = kk == 0 and at_col(tt) == 0
                    h, lo = HH[:, kk, tt * P:(tt + 1) * P], HL[:, kk, tt * P:(tt + 1) * P]
                    mm(o, h, wh[:, k, col:col + cw], first, False)
                    mm(o, h, wl[:, k, col:col + cw], False, False)
                    ins = mm(o, lo, wh[:, k, col:col + cw], False, kk == KC - 1)
                return ins
            return part

        def qkv(s):
            pe.wait_ge(h_ready.sem, s.ready)
            for it in s.items:
                ch, grp, one = it.chunk, it.grp, At(None, 0, 1, 1)
                if it.what[0] == "forget":
                    wait_landed(pe, one, lambda _: ch)
                    pe.wait_ge(ada_out.sem, s.a_out)
                    w = raw_ap(ch.n, KC, 8)
                    for k in range(KC):
                        mm(B_ADA[0:8, 0:T], w[:, k, :], HH[:, k, 0:T].bitcast(F32), k == 0, False)
                        ins = mm(B_ADA[0:8, 0:T], w[:, k, :], HL[:, k, 0:T].bitcast(F32), False, k == KC - 1)
                    ins.then_inc(ada_used, 1)
                    continue
                wait_bank(one, lambda _: grp)
                pair = PAIR[grp.n % 2]
                if it.what[0] == "v":
                    part = tokens(ch, grp, s.n, 0, CW, lambda tt: pair[tt // 2], lambda tt: CW * (tt % 2))
                    features(one, lambda _: ch, grp, KC, 0, HH, HL, s.n, 0, part)
                elif it.what[0] == "kv":
                    part = tokens(ch, grp, s.n, P, P, lambda tt: pair[1], lambda tt: P * tt)
                    features(one, lambda _: ch, grp, KC, 0, HH, HL, s.n, 1, part)
                else:
                    features(one, lambda _: ch, grp, KC, 0, HH, HL, s.n)

        def ffn_in(s):
            def step(at):
                wait_bank(at, lambda k: s.steps[k].gg)
                features(at, lambda k: s.steps[k].g, s.steps[at.u].gg, KC, 0, HH, HL, s.n)
                if s.host:
                    ada(at, lambda k: s.steps[k].hosts[0])
                wait_bank(at, lambda k: s.steps[k].ug)
                features(at, lambda k: s.steps[k].u, s.steps[at.u].ug, KC, 0, HH, HL, s.n)
                if s.host:
                    ada(at, lambda k: s.steps[k].hosts[1])
            pe.wait_ge(h_ready.sem, s.h_wait)
            step(At(None, 0, 1, 1))
            each(pe, 1, 11, 1, step)

        def proj(s):
            xh, xl, kt = (AH, AL, NF) if s.hidden else (HH, HL, NT)
            if s.hidden:
                pe.wait_ge(act_ready.sem, s.ready)
            else:
                pe.wait_ge(o_done.sem, s.ready)

            def two(at):
                for b in range(2):
                    grp = lambda k: s.groups[2 * k + b]
                    wait_bank(at, lambda k: grp(k).grp)
                    for j in range(len(grp(0).chunks)):
                        features(at, lambda k: grp(k).chunks[j], grp(at.u).grp, kt, KC * j, xh, xl, s.n)
                    if grp(0).host:
                        ada(at, lambda k: grp(k).host)
            for k in range(2):
                two(At(None, k, 1, 1))

        def setup():
            pe.wait_ge(rows_in, 16 * 16)
            at = 0
            for r in ROWS:
                n = r.shape[0]
                ins = pe.transpose(BANK[0][:, at:at + n], r[:, :], ident[0:n, 0:n])
                at += n
            ins.then_inc(setup_mm, 1)

            def turn(src, b, k):
                for t in range(2):
                    for q in range(2):
                        ins = pe.transpose(b[:, T * t + P * q:T * t + P * q + P],
                                           src[:, q, P * (2 * k + t):P * (2 * k + t + 1)], ident[:, :])
                ins.then_inc(setup_mm, 1)
            for k in range(4):
                turn(XIN, BANK[1 + k], k)
            for k in range(3):
                turn(CIN, BANK[5 + k], k)
            pe.wait_ge(setup_act, 1)
            turn(CIN, BANK[1], 3)
            pe.wait_ge(const_in, 16 * 11)
            pe.wait_ge(setup_act, 2)
            mm(BANK[2][0:N_T5, 0:BIAS_L], TABLE[:, :], ONEHOT[:, :], True, True).then_inc(setup_mm, 1)
            pe.wait_ge(silu_done, 1)
            pe.wait_ge(cols_done, 1)

        def stats(s):
            if s.kind == "ln":
                pe.wait_ge(x_ready.sem, s.x)
                for t in range(NT):
                    ins = mm(B_STAT[:, 0:s.n], ones[:, :], X[:, t, 0:s.n], t == 0, t == NT - 1)
                ins.then_inc(mean_mm.sem, 1)
            bank = B_T[0] if s.kind == "ln" else B_STAT
            for t in range(NT):
                pe.wait_ge(stat_in.sem, s.stat_in + t + 1)
                mm(bank[:, 0:s.n], ones[:, :], T1[:, t % 2, 0:s.n], t == 0, t == NT - 1).then_inc(stat_mm.sem, 1)

        def sub_norm():
            for t in range(4):
                pe.wait_ge(sub_sq, t + 1)
                if t >= 2:
                    pe.wait_ge(sub_rt, t - 1)
                mm(B_T[t % 2][:, 0:T], ones[:, :], T1[:, t % 2, 0:T], True, True).then_inc(sub_mm, 1)

        def forget_bias(s):
            pe.wait_ge(fg_cum, 1)
            for q in range(2):
                ins = pe.transpose(B_T[0][:, 8 * q:8 * q + 8], CUM[:, P * q:P * q + P], ident[0:8, 0:8])
            ins.then_inc(fg_mm, 1)
            pe.wait_ge(fg_sel, 16)
            for h in range(8):
                if h >= 2:
                    pe.wait_ge(fg_free, h - 1)
                sel = NEGSEL[:, h // 4, h % 4, :]
                mm(BANK[h % 2][:, 0:T], sel, CUM, True, True).then_inc(fg_mm, 1)
            pe.wait_ge(fg_free, 8)

        def qk_norm(s):
            def tile(at):
                par = at.u % 2
                pe.wait_ge(qn_sq.sem, at(lambda i: s.sq + i + 1))
                pe.wait_ge(qn_rt.sem, at(lambda i: s.rt + i - 1))
                mm(B_T[par][:, :], head_ones[:, :], T1[:, par, :], True, True).then_inc(qn_mm.sem, 1)
            each(pe, 0, 13, 2, tile)
            pe.wait_ge(qn_out.sem, s.out + 13)
            for r in range(5):
                src = QB[:, 4 + r, 0:T] if r < 4 else KB[:, 4, 0:T]
                pe.wait_ge(rope_out.sem, s.ro + r)
                mm(B_STAT[:, 0:T], rotate[:, :], src, True, True).then_inc(rope_mm.sem, 1)
            pe.wait_ge(rope_out.sem, s.ro + 5)
            for kv in range(2):
                mm(BANK[kv][:, :], dup[kv][:, :], KB[:, 4, :], True, True).then_inc(rope_mm.sem, 1)

        def attn(s):
            def pair(at):
                pe.wait_ge(q_staged.sem, at(lambda p: s.q + p + 1))
                for hh in range(2):
                    for qt in range(2):
                        j, nk = 2 * hh + qt, P * s.nblk(qt)
                        pe.wait_ge(exp_done.sem, at(lambda p: s.ex + 4 * p + j - 3))
                        mm(BANK[j][:, 0:nk], QS[HD * hh:HD * hh + HD, P * qt:P * qt + P],
                           KS[HD * hh:HD * hh + HD, 0:nk], True, True).then_inc(scores.sem, 1)
                for jj in range(s.tper):
                    nb = s.nblk(jj % 2)
                    pe.wait_ge(probs.sem, at(lambda p: s.pb + s.tper * p + jj + 1))
                    pe.wait_ge(copied.sem, at(lambda p: s.cp + s.tper * p + jj - 1))
                    for b in range(nb):
                        ins = pe.transpose(B_T[jj % 2][:, P * b:P * b + P], PR[:, jj, P * b:P * b + P],
                                           ident[:, :])
                    ins.then_inc(turned.sem, 1)
                pe.wait_ge(v_staged.sem, at(lambda p: s.v + p + 1))
                pe.wait_ge(copied.sem, at(lambda p: s.cp + s.tper * (p + 1)))
                pe.wait_ge(o_done.sem, at(lambda p: s.o + p))
                for jj in range(s.tper):
                    hh, qt = jj // 2, jj % 2
                    nb = s.nblk(qt)
                    vc = 0 if s.diff or s.vw == HD else HD * hh
                    w = P if s.diff else HD
                    o = B_STAT[:, P * qt:P * qt + P] if s.diff else B_STAT[HD * hh:HD * hh + HD, P * qt:P * qt + P]
                    for b in range(nb):
                        ins = mm(o, VS[:, b, vc:vc + w], PT[:, jj, b, :], b == 0, b == nb - 1)
                ins.then_inc(pv_done.sem, 1)
            each(pe, 0, s.pairs, s.unroll, pair)

        def finish(s):
            pe.wait_ge(x_ready.sem, s.x)
            for b in range(4):
                q, f0 = b // 2, 4 * (b % 2)
                for t in range(4):
                    ins = pe.transpose(BANK[b][:, P * t:P * t + P], X[:, f0 + t, P * q:P * q + P], ident[:, :])
                ins.then_inc(out_mm, 1)

        one = At(None, 0, 1, 1)
        for s in PLAN:
            if s.kind == "setup":
                setup()
            elif s.kind == "ada":
                for ch in s.chunks:
                    ada(one, lambda _, ch=ch: ch)
            elif s.kind in ("ln", "rms"):
                stats(s)
            elif s.kind == "qkv":
                qkv(s)
            elif s.kind == "ffn_in":
                ffn_in(s)
            elif s.kind == "proj":
                proj(s)
            elif s.kind == "sub_norm":
                sub_norm()
            elif s.kind == "forget_bias":
                forget_bias(s)
            elif s.kind == "qk_norm":
                qk_norm(s)
            elif s.kind == "attn":
                attn(s)
            elif s.kind == "finish":
                finish(s)

    def ahead(at, f, split, late):
        p = f(at.u)
        if p.g + 2 >= len(PIECES):
            return
        if PIECES[p.g + 2].chunk.n - p.chunk.n > RAW:
            late.append(p.g + 2)
        else:
            split(at, lambda s: PIECES[f(s).g + 2])

    @block.scalar
    def _(act):
        chain = Chain(act, act_chain)
        late = [0, 1]
        one = At(None, 0, 1, 1)

        def split(at, f):
            p = f(at.u)
            ch = p.chunk
            wait_landed(act, at, lambda s: f(s).chunk)
            act.wait_ge(piece_used.sem, at(lambda s: f(s).g + 1))
            act.activation(WH[:, p.g % 2, 0:p.kt * CW].rearrange("p (t n) -> p t n", n=CW),
                           raw_ap(ch.n, ch.kt, CW)[:, p.k0:p.k0 + p.kt, :], ACT.Copy).then_inc(hi_done, 1)

        def flush():
            while late:
                g = late.pop(0)
                split(one, lambda _: PIECES[g])

        def used(at, f):
            act.wait_ge(piece_used.sem, at(lambda s: f(s).g + 3))

        def setup():
            for k in range(4):
                act.wait_ge(setup_mm, 2 + k)
                act.activation(X[:, 2 * k:2 * k + 2, 0:T], BANK[1 + k][:, :].rearrange("p (t n) -> p t n", t=2),
                               ACT.Copy).then_inc(setup_act, 1)
            act.wait_ge(cols_done, 1)
            act.activation(SILU_C[:, 0:8], C_COLS[:, 0:8], ACT.Silu)
            pairs = SILU_C[:, 8:24].rearrange("p (t v) -> p t v", v=2)
            for v in range(2):
                ins = act.activation(pairs[:, :, v], C_COLS[:, 8 + 8 * v:16 + 8 * v], ACT.Silu)
            ins.then_inc(silu_done, 1)
            act.wait_ge(lam_sum, 1)
            act.activation(LAM[:, 2:4], LAM[:, 0:2], ACT.Exp).then_inc(lam_exp, 1)

        def stats(s):
            act.wait_ge(x_ready.sem, s.x)
            for t in range(NT):
                if s.kind == "ln":
                    act.wait_ge(centred.sem, s.cen + t + 1)
                act.wait_ge(stat_mm.sem, s.stat + t - 1)
                act.activation(T1[:, t % 2, 0:s.n], X[:, t, 0:s.n], ACT.Square).then_inc(stat_in.sem, 1)
            act.wait_ge(stat_mm.sem, s.stat + NT)
            bank, eps = (B_T[0], EPS[:, 0:1]) if s.kind == "ln" else (B_STAT, EPS[:, 1:2])
            act.activation(RB[:, 0:s.n], bank[:, 0:s.n], ACT.Sqrt, bias=eps, scale=1.0 / D).then_inc(rstd_sq.sem, 1)

        def modulate(s):
            act.wait_ge(ada_out.sem, ada_ready[s.ada])
            ad = AD[s.ada]

            def tile(at):
                par, t = at.u % 2, at(lambda k: k)
                if s.kind != "mod":
                    act.wait_ge(mod_src.sem, at(lambda k: s.src + k + 1))
                wait_apart(act, h_ready.sem, at(lambda k: s.h + k - 1), act_waited)
                for v in range(s.n // T):
                    cols = slice(v * T, v * T + T)
                    src = T1[:, par, cols] if s.kind == "rms" else \
                        X[:, bass.ds(t, 1), cols].rearrange("p o n -> p (o n)")
                    sc = GS[:, bass.ds(t, 1), v] if s.kind == "rms" else ad[:, bass.ds(at(lambda k: 8 * s.scale + k), 1), v]
                    sh = ad[:, bass.ds(at(lambda k: 8 * s.shift + k), 1), v]
                    ins = act.activation(T2[:, par, cols], src, ACT.Identity, bias=sh, scale=sc)
                ins.then_inc(mod_t2.sem, 1)
            each(act, 0, 8, 2, tile)

        def qkv(s):
            for it in s.items:
                if it.what[0] == "forget":
                    continue
                for p in it.chunk.pieces:
                    ahead(one, lambda _: p, split, late)
                used(one, lambda _: it.chunk.pieces[-1])
                pair, kind, n = PAIR[it.grp.n % 2], it.what[0], s.n
                if kind in "qk":
                    dst, t = (QB if kind == "q" else KB), it.what[1]
                    for j in range(2):
                        ins = act.activation(dst[:, t + j, 0:n], pair[j][:, 0:n], ACT.Copy,
                                             scale=SCALE if s.first and kind == "q" else 1.0)
                elif kind == "v":
                    row = D if s.first else 640
                    v = VB[:, 0:n // P * row].rearrange("p (b n) -> p b n", n=row)
                    for j in range(n // T):
                        ins = act.activation(v[:, 2 * j:2 * j + 2, it.what[1]:it.what[1] + CW],
                                             pair[j][:, :].rearrange("p (b n) -> p b n", b=2), ACT.Copy)
                else:
                    v = VB[:, :].rearrange("p (b n) -> p b n", n=640)
                    act.activation(KB[:, 4, :], pair[0][:, :], ACT.Copy)
                    ins = act.activation(v[:, :, 512:640], pair[1][:, :].rearrange("p (b n) -> p b n", b=4),
                                         ACT.Copy)
                ins.then_inc(ev_act.sem, 1)

        def ffn_in(s):
            n = s.n

            def hidden_hi(at):
                t = at(lambda k: 2 * k)
                wait_apart(act, act32.sem, at(lambda k: s.a32 + k + 1), act_waited)
                act.activation(AH[:, bass.ds(t, 2), 0:n], T2[:, :, 0:n], ACT.Copy).then_inc(act_hi.sem, 1)

            def step(at):
                gg = s.steps[at.u].gg
                for i in range(2):
                    ahead(at, lambda k: s.steps[k].g.pieces[i], split, late)
                used(at, lambda k: s.steps[k].g.pieces[-1])
                act.wait_ge(act32.sem, at(lambda k: s.a32 + k))
                act.activation(T1[:, 0, 0:n], PAIR[gg.n % 2][0][:, 0:n], ACT.Silu)
                act.activation(T1[:, 1, 0:n], PAIR[gg.n % 2][1][:, 0:n], ACT.Silu).then_inc(silu_g.sem, 1)
                act.wait_ge(silu_g.sem, at(lambda k: s.silu + k + 1))
                act.sem_inc(ev_act.sem, 1)
                for i in range(2):
                    ahead(at, lambda k: s.steps[k].u.pieces[i], split, late)
                hidden_hi(at)
            each(act, 0, 10, 1 if s.host else 2, step)
            step(At(None, 10, 1, 1))

        def proj(s):
            for g in s.groups:
                for ch in g.chunks:
                    for p in ch.pieces:
                        ahead(one, lambda _: p, split, late)

        def sub_norm(s):
            act.wait_ge(o_done.sem, s.o_wait)
            for t in range(4):
                if t >= 2:
                    act.wait_ge(sub_mm, t - 1)
                act.activation(T1[:, t % 2, 0:T], OF[:, t, :], ACT.Square).then_inc(sub_sq, 1)
                act.wait_ge(sub_mm, t + 1)
                if t >= 2:
                    act.wait_ge(sub_out, t - 1)
                act.activation(T2[:, t % 2, 0:T], B_T[t % 2][:, 0:T], ACT.Sqrt, bias=EPS[:, 0:1], scale=1.0 / P
                               ).then_inc(sub_rt, 1)

        def forget_bias(s):
            act.wait_ge(o_done.sem, s.o_wait)
            act.wait_ge(ada_used, s.logits)
            act.activation(FD, B_ADA[0:8, 0:T], ACT.Identity, bias=FB[:, 0:1]).then_inc(fg_x, 1)
            act.wait_ge(fg_abs, 1)
            chain.link(act.activation(FD_ABS, FD_ABS, ACT.Exp, scale=-1.0))
            act.activation(FD_ABS, FD_ABS, ACT.Ln, bias=1.0).then_inc(fg_exp, 1)

        def qk_norm(s):
            act.wait_ge(ev_act.sem, s.q_in)

            def tiles(at2, first, n):
                tb, off = (QB, 0) if first < 8 else (KB, 8)
                for u in range(n):
                    at = at2[u]
                    par = at.u % 2
                    wait_apart(act, qn_mm.sem, at(lambda i: s.mm + i - 1), act_waited)
                    act.activation(T1[:, par, :], tb[:, bass.ds(at(lambda i: i - off), 1), :]
                                   .rearrange("p o n -> p (o n)"), ACT.Square).then_inc(qn_sq.sem, 1)
                for u in range(n):
                    at = at2[u]
                    par = at.u % 2
                    act.wait_ge(qn_mm.sem, at(lambda i: s.mm + i + 1))
                    act.wait_ge(qn_out.sem, at(lambda i: s.out + i - 1))
                    act.activation(T2[:, par, :], B_T[par][:, :], ACT.Sqrt, bias=EPS[:, 1:2], scale=1.0 / HD
                                   ).then_inc(qn_rt.sem, 1)
            for lo, n in ((0, 4), (8, 2)):
                with act.Fori(0, n) as reg:
                    tiles([At(reg, lo + u, 2, n) for u in range(2)], lo, 2)
            tiles([At(None, 12, 1, 1)], 12, 1)

        def attn(s):
            def pair(at):
                for hh in range(2):
                    for qt in range(2):
                        j, nk = 2 * hh + qt, P * s.nblk(qt)
                        back = j % 2 if s.diff else j
                        act.wait_ge(nmax.sem, at(lambda p: s.mx + 4 * p + j + 1))
                        wait_apart(act, turned.sem, at(lambda p: s.tu + s.tper * (p - 1) + back + 1), act_waited)
                        if s.sink:
                            act.activation(ES[:, j:j + 1], SINK[:, bass.ds(at(lambda p: s.sink(p, hh)), 1)],
                                           ACT.Exp, bias=NM[:, j:j + 1]).then_inc(sink_done.sem, 1)
                        act.activation(PR[:, j, 0:nk], BANK[j][:, 0:nk], ACT.Exp, bias=NM[:, j:j + 1],
                                       accum_out=RS[:, j:j + 1]).then_inc(exp_done.sem, 1)
                act.wait_ge(pv_done.sem, at(lambda p: s.pv + p))
                for jj in range(s.tper):
                    nb = s.nblk(jj % 2)
                    act.wait_ge(turned.sem, at(lambda p: s.tu + s.tper * p + jj + 1))
                    act.activation(PT[:, jj, 0:nb, :], B_T[jj % 2][:, 0:P * nb].rearrange("p (b n) -> p b n", n=P),
                                   ACT.Copy).then_inc(copied.sem, 1)
            each(act, 0, s.pairs, s.unroll, pair)

        for s in PLAN:
            if s.kind == "setup":
                setup()
            elif s.kind == "ada":
                flush()
            elif s.kind in ("mod", "ln", "rms"):
                if s.kind != "mod":
                    stats(s)
                if not s.last_ln:
                    modulate(s)
            elif s.kind == "qkv":
                qkv(s)
            elif s.kind == "ffn_in":
                ffn_in(s)
            elif s.kind == "proj":
                proj(s)
            elif s.kind == "sub_norm":
                sub_norm(s)
            elif s.kind == "forget_bias":
                forget_bias(s)
            elif s.kind == "qk_norm":
                qk_norm(s)
            elif s.kind == "attn":
                attn(s)
            elif s.kind == "finish":
                for b in (0, 2):
                    act.wait_ge(out_mm, b + 1)
                    act.activation(OUTR[:, b // 2, 0:512], BANK[b][:, :], ACT.Copy).then_inc(out_cp, 1)

    @block.vector
    def _(dve):
        chain = Chain(dve, dve_chain)
        late = [0, 1]
        one = At(None, 0, 1, 1)

        def split(at, f):
            p = f(at.u)
            ch = p.chunk
            dve.wait_ge(hi_done, at(lambda s: f(s).g + 1))
            dve.tensor_tensor(WL[:, p.g % 2, 0:p.kt * CW].rearrange("p (t n) -> p t n", n=CW),
                              raw_ap(ch.n, ch.kt, CW)[:, p.k0:p.k0 + p.kt, :],
                              WH[:, p.g % 2, 0:p.kt * CW].rearrange("p (t n) -> p t n", n=CW).bitcast(F32),
                              ALU.subtract).then_inc(lo_done, 1)

        def flush():
            while late:
                g = late.pop(0)
                split(one, lambda _: PIECES[g])

        def used(at, f):
            dve.wait_ge(piece_used.sem, at(lambda s: f(s).g + 3))

        def ada(at, f):
            ch = f(at.u)
            m = ch.order[0]
            nv = 1 if m < 2 else 2
            bias = (B1 if m < 2 else B2)[:, m % 2, :]
            col = at(lambda s: 2 * f(s).order[1])
            dve.wait_ge(ada_used, at(lambda s: f(s).raw_order + 1))
            b = bias[:, bass.ds(col, 2)]
            if nv == 2:
                b = b[:, :, None].broadcast_to([P, 2, 2])
                o, i = AD[m][:, bass.ds(col, 2), :], B_ADA[:, 0:4].rearrange("p (c v) -> p c v", v=2)
            else:
                o, i = AD[m][:, bass.ds(col, 2), 0], B_ADA[:, 0:2]
            dve.tensor_tensor(o, i, b, ALU.add).then_inc(ada_out.sem, 1)

        def setup():
            dve.memset(EPS[:, 0:1], LN_EPS)
            dve.memset(EPS[:, 1:2], NORM_EPS)
            dve.wait_ge(setup_mm, 1)
            at = 0
            b0 = BANK[0]
            dve.tensor_copy(C_COLS[:, :], b0[:, 0:24])
            dve.tensor_copy(B1[:, :, :], b0[:, 24:120].rearrange("p (l n) -> p l n", l=2))
            dve.tensor_copy(B2[:, :, :], b0[:, 120:264].rearrange("p (l n) -> p l n", l=2))
            dve.tensor_copy(G_COLS[:, :], b0[:, 264:376])
            chain.link(dve.tensor_copy(E_COLS[:, :], b0[:, 376:385]))
            for j in (1, 2, 4, 5):
                dve.tensor_scalar(B1[:, :, 8 * j:8 * j + 8], B1[:, :, 8 * j:8 * j + 8], 1.0, None, ALU.add)
            for j in (1, 4, 7):
                dve.tensor_scalar(B2[:, :, 8 * j:8 * j + 8], B2[:, :, 8 * j:8 * j + 8], 1.0, None, ALU.add)
            dve.tensor_scalar(E_COLS[:, 0:1], E_COLS[:, 0:1], 1.0 - LAMBDA_INIT, None, ALU.mult)
            for k in (1, 3, 5, 7):
                ins = dve.tensor_scalar(E_COLS[:, k:k + 1], E_COLS[:, k:k + 1], SCALE, None, ALU.mult)
            chain.link(ins)
            for k in range(4):
                dve.wait_ge(setup_mm, 6 + k)
                b = BANK[5 + k] if k < 3 else BANK[1]
                ins = dve.tensor_copy(X[:, 2 * k:2 * k + 2, T:2 * T], b[:, :].rearrange("p (t n) -> p t n", t=2))
            ins.then_inc(cols_done, 1)
            dve.wait_ge(setup_mm, 10)
            dve.tensor_tensor(T5ROW[:, :], BANK[2][0:N_T5, 0:BIAS_L], T5MASK[:, :], ALU.add).then_inc(t5_rows, 1)
            pairs = LROW[:, :, :].rearrange("p (a b) d -> p a b d", b=2)
            chain.link(dve.tensor_tensor(LPROD[:, :, :], pairs[:, :, 0, :], pairs[:, :, 1, :], ALU.mult))
            dve.tensor_reduce(LAM[:, 0:2], LPROD[:, :, :], AX.X, ALU.add).then_inc(lam_sum, 1)
            dve.wait_ge(lam_exp, 1)
            ins = dve.scalar_tensor_tensor(out=LAM[:, 4:5], in0=LAM[:, 3:4], scalar=LAMBDA_INIT, in1=LAM[:, 2:3],
                                           op0=ALU.subtract, op1=ALU.subtract)
            chain.link(ins)
            dve.sem_inc(region_free, 1)
            dve.wait_ge(setup_act, 4)

        def flat(ap):
            return ap.rearrange("p o n -> p (o n)")

        def norm(s):
            n, ad = s.n, AD[s.ada]
            rms = s.kind == "rms"
            if rms:
                g = G_COLS[:, s.gain:s.gain + 8][:, :, None].broadcast_to([P, 8, 2])
                chain.link(dve.tensor_tensor(GS[:, :, :], ad[:, 8 * s.scale:8 * s.scale + 8, :], g, ALU.mult))
            if s.kind == "ln":
                dve.wait_ge(mean_mm.sem, s.mean + 1)
                for t in range(NT):
                    dve.scalar_tensor_tensor(out=X[:, t, 0:n], in0=B_STAT[:, 0:n], scalar=-1.0 / D, in1=X[:, t, 0:n],
                                             op0=ALU.mult, op1=ALU.add).then_inc(centred.sem, 1)
                dve.wait_ge(centred.sem, s.cen + NT)
            if s.kind != "mod":
                dve.wait_ge(rstd_sq.sem, s.rstd + 1)
                chain.link(dve.reciprocal(RB[:, 0:n], RB[:, 0:n]))
            linked = s.kind == "ln"

            def tile(at):
                par, t = at.u % 2, at(lambda k: k)
                x = flat(X[:, bass.ds(t, 1), 0:n])
                if s.kind != "mod":
                    if not s.last_ln:
                        dve.wait_ge(mod_t2.sem, at(lambda k: s.t2 + k - 1))
                    ins = dve.tensor_tensor(T1[:, par, 0:n], x, RB[:, 0:n], ALU.mult)
                    if rms:
                        ins.then_inc(mod_src.sem, 1)
                    else:
                        chain.link(ins)
                        ins = dve.tensor_scalar(x, T1[:, par, 0:n],
                                                G_COLS[:, bass.ds(at(lambda k: s.gain + k), 1)],
                                                G_COLS[:, bass.ds(at(lambda k: s.gain_b + k), 1)], ALU.mult, ALU.add)
                        if s.last_ln:
                            return
                        ins.then_inc(mod_src.sem, 1)
                    dve.wait_ge(mod_src.sem, at(lambda k: s.src + k + 1))
                for v in range(n // T):
                    cols = slice(v * T, v * T + T)
                    src = T1[:, par, cols] if rms else flat(X[:, bass.ds(t, 1), cols])
                    sc = GS[:, bass.ds(t, 1), v] if rms else ad[:, bass.ds(at(lambda k: 8 * s.scale + k), 1), v]
                    sh = ad[:, bass.ds(at(lambda k: 8 * s.shift + k), 1), v]
                    ins = dve.tensor_scalar(flat(HH[:, bass.ds(t, 1), cols]), src, sc, sh, ALU.mult, ALU.add)
                ins.then_inc(mod_hi.sem, 1)
            each(dve, 0, 8, 2, tile, chain if linked else None, 2)
            if s.kind == "ln":
                dve.drain().then_inc(x_ready.sem, 1)

        def ffn_in(s):
            n = s.n

            def step(at):
                for i in range(2):
                    ahead(at, lambda k: s.steps[k].g.pieces[i], split, late)
                if s.host:
                    ada(at, lambda k: s.steps[k].hosts[0])
                for i in range(2):
                    ahead(at, lambda k: s.steps[k].u.pieces[i], split, late)
                used(at, lambda k: s.steps[k].u.pieces[-1])
                dve.wait_ge(silu_g.sem, at(lambda k: s.silu + k + 1))
                dve.wait_ge(act_ready.sem, at(lambda k: s.ready + k))
                pair = PAIR[s.steps[at.u].ug.n % 2]
                for j in range(2):
                    ins = dve.tensor_tensor(T2[:, j, 0:n], T1[:, j, 0:n], pair[j][:, 0:n], ALU.mult)
                ins.then_inc(act32.sem, 1)
                dve.wait_ge(act32.sem, at(lambda k: s.a32 + k + 1))
                dve.sem_inc(ev_dve.sem, 1)
                if s.host:
                    ada(at, lambda k: s.steps[k].hosts[1])
            each(dve, 0, 10, 1 if s.host else 2, step)
            step(At(None, 10, 1, 1))

        def proj(s):
            n, ad = s.n, AD[s.ada]
            for m, g in enumerate(s.groups):
                for ch in g.chunks:
                    for p in ch.pieces:
                        ahead(one, lambda _: p, split, late)
                used(one, lambda _: g.chunks[-1].pieces[-1])
                pair = PAIR[g.grp.n % 2]
                if m == 0 and s.half:
                    chain.link(dve.tensor_scalar(GS[:, :, :], ad[:, 8 * s.gate:8 * s.gate + 8, :], 0.5, None, ALU.mult))
                if s.first:
                    for j in range(2):
                        t = 2 * m + j
                        ins = dve.tensor_scalar(T2[:, j, 0:n], pair[j][:, 0:n], ad[:, 8 * s.gate + t, :], None, ALU.mult)
                    chain.link(ins)
                    ins = dve.scalar_tensor_tensor(out=X[:, 2 * m:2 * m + 2, 0:n], in0=X[:, 2 * m:2 * m + 2, 0:n],
                                                   scalar=ALPHA, in1=T2[:, :, 0:n], op0=ALU.mult, op1=ALU.add)
                else:
                    for j in range(2):
                        t = 2 * m + j
                        for v in range(n // T):
                            cols = slice(v * T, v * T + T)
                            gate = GS[:, t, v:v + 1] if s.half else ad[:, 8 * s.gate + t, v:v + 1]
                            ins = dve.scalar_tensor_tensor(out=X[:, t, cols], in0=pair[j][:, cols], scalar=gate,
                                                           in1=X[:, t, cols], op0=ALU.mult, op1=ALU.add)
                chain.link(ins)
                dve.sem_inc(g.grp.tally.sem, 1)
                if g.host:
                    ada(one, lambda _: g.host)
            dve.sem_inc(x_ready.sem, 1)

        def sub_norm():
            for t in range(4):
                dve.wait_ge(sub_rt, t + 1)
                o, r = OF[:, t, :], T2[:, t % 2, 0:T]
                chain.link(dve.reciprocal(r, r))
                chain.link(dve.scalar_tensor_tensor(out=o, in0=o, scalar=E_COLS[:, 0:1], in1=r, op0=ALU.mult,
                                                    op1=ALU.mult))
                chain.link(dve.tensor_copy(HH[:, t, 0:T], o))
                dve.tensor_tensor(HL[:, t, 0:T], o, HH[:, t, 0:T].bitcast(F32), ALU.subtract).then_inc(sub_out, 1)

        def forget_bias(s):
            dve.wait_ge(fg_x, 1)
            dve.scalar_tensor_tensor(out=FD_ABS, in0=FD, scalar=-1.0, in1=FD, op0=ALU.mult, op1=ALU.max
                                     ).then_inc(fg_abs, 1)
            dve.tensor_scalar(FD_MIN, FD, 0.0, None, ALU.min)
            dve.memset(FD_ONE, 1.0)
            dve.wait_ge(fg_exp, 1)
            chain.link(dve.drain())
            chain.link(dve.tensor_tensor(FD_MIN, FD_MIN, FD_ABS, ALU.subtract))
            dve.tensor_tensor_scan(CUM, FD_ONE.rearrange("p a b -> p (a b)"), FD_MIN, 0.0, ALU.mult, ALU.add
                                   ).then_inc(fg_cum, 1)
            dve.wait_ge(fg_mm, 1)
            chain.link(dve.tensor_copy(CUMT[:, :, :], B_T[0][:, 0:16].rearrange("p (q h) -> p q h", q=2)))
            dve.wait_ge(bias_in.sem, s.bias_in)
            for h in range(8):
                dve.wait_ge(fg_mm, h + 2)
                for q in range(2):
                    nk = P * (q + 1)
                    ins = dve.scalar_tensor_tensor(out=BT[:, 512 * h + T * q:512 * h + T * q + nk],
                                                   in0=BANK[h % 2][:, 0:nk], scalar=CUMT[:, q, h:h + 1],
                                                   in1=CAUSAL[:, T - nk:T], op0=ALU.add, op1=ALU.add)
                ins.then_inc(fg_free, 1)
            dve.wait_ge(fg_free, 8)

        def qk_norm(s):
            dve.wait_ge(bias_in.sem, s.bias_in)
            blocks = BT[:, :].rearrange("p (b k) -> p b k", k=T)
            chain.link(dve.tensor_tensor(blocks, blocks, NEIGH[:, None, :].broadcast_to([P, 16, T]), ALU.add))

            def segment(lo, hi, gain):
                tb, off = (QB, 0) if lo < 8 else (KB, 8)

                def tile(at):
                    par = at.u % 2
                    dve.wait_ge(qn_rt.sem, at(lambda i: s.rt + i + 1))
                    chain.link(dve.reciprocal(T2[:, par, :], T2[:, par, :]))
                    x = flat(tb[:, bass.ds(at(lambda i: i - off), 1), :])
                    dve.scalar_tensor_tensor(out=x, in0=x, scalar=gain, in1=T2[:, par, :], op0=ALU.mult,
                                             op1=ALU.mult).then_inc(qn_out.sem, 1)
                each(dve, lo, hi, 2, tile, chain, 2)
            for (lo, hi), g in (((0, 4), 0), ((4, 8), 2), ((8, 12), 1), ((12, 13), 3)):
                k = 1 + 4 * s.layer + g
                segment(lo, hi, E_COLS[:, k:k + 1])
            dve.wait_ge(qn_out.sem, s.out + 13)
            for r in range(5):
                x = QB[:, 4 + r, 0:T] if r < 4 else KB[:, 4, 0:T]
                dve.wait_ge(rope_mm.sem, s.rmm + r + 1)
                dve.tensor_tensor(T1[:, 0, 0:T], B_STAT[:, 0:T], SIN[:, :], ALU.mult)
                chain.link(dve.tensor_tensor(x, x, COS[:, :], ALU.mult))
                chain.link(dve.tensor_tensor(x, x, T1[:, 0, 0:T], ALU.add))
                dve.sem_inc(rope_out.sem, 1)
            for kv in range(2):
                dve.wait_ge(rope_mm.sem, s.rmm + 6 + kv)
                dve.tensor_copy(KB[:, 5 + kv, :], BANK[kv][:, :]).then_inc(rope_out.sem, 1)

        def attn(s):
            dve.wait_ge(bias_in.sem, s.bias_in)
            links = 0

            def pair(at):
                k0 = chain.k
                for hh in range(2):
                    for qt in range(2):
                        j, nk = 2 * hh + qt, P * s.nblk(qt)
                        dve.wait_ge(scores.sem, at(lambda p: s.sc + 4 * p + j + 1))
                        if s.bias:
                            where, _, w = s.bias(at.u, hh, qt)
                            b = WINDOW[:, qt, :] if where == "window" else \
                                BT[:, bass.ds(at(lambda p: s.bias(p, hh, qt)[1]), w)]
                            chain.link(dve.tensor_tensor(BANK[j][:, 0:w], BANK[j][:, 0:w], b, ALU.add))
                        ins = dve.tensor_reduce(NM[:, j:j + 1], BANK[j][:, 0:nk], AX.X, ALU.max, negate=True)
                        if s.sink:
                            chain.link(ins)
                            col = SINK[:, bass.ds(at(lambda p: s.sink(p, hh)), 1)]
                            ins = dve.scalar_tensor_tensor(out=NM[:, j:j + 1], in0=col, scalar=-1.0,
                                                           in1=NM[:, j:j + 1], op0=ALU.mult, op1=ALU.min)
                        ins.then_inc(nmax.sem, 1)
                for hh in range(2):
                    for qt in range(2):
                        j, nk = 2 * hh + qt, P * s.nblk(qt)
                        if s.diff and hh == 0:
                            continue
                        for jj in ((qt, j) if s.diff else (j,)):
                            dve.wait_ge(exp_done.sem, at(lambda p: s.ex + 4 * p + jj + 1))
                            if s.sink:
                                dve.wait_ge(sink_done.sem, at(lambda p: s.sk + 4 * p + jj + 1))
                                chain.link(dve.tensor_tensor(RS[:, jj:jj + 1], RS[:, jj:jj + 1], ES[:, jj:jj + 1],
                                                             ALU.add))
                            chain.link(dve.reciprocal(RI[:, jj:jj + 1], RS[:, jj:jj + 1]))
                        p1 = PR[:, j, 0:nk]
                        if s.diff:
                            p0 = PR[:, qt, 0:nk]
                            chain.link(dve.tensor_scalar(p1, p1, RI[:, j:j + 1], LAM[:, 4:5], ALU.mult, ALU.mult))
                            ins = dve.scalar_tensor_tensor(out=p0, in0=p0, scalar=RI[:, qt:qt + 1], in1=p1,
                                                           op0=ALU.mult, op1=ALU.add)
                        else:
                            ins = dve.tensor_scalar(p1, p1, RI[:, j:j + 1], None, ALU.mult)
                        ins.then_inc(probs.sem, 1)
                dve.wait_ge(pv_done.sem, at(lambda p: s.pv + p + 1))
                if s.diff:
                    dve.tensor_copy(OF[:, at.u, :] if at.reg is None else
                                    flat(OF[:, bass.ds(at(lambda p: p), 1), :]), B_STAT[:, 0:T]
                                    ).then_inc(o_done.sem, 1)
                else:
                    t = at(s.out)
                    hi = flat(HH[:, bass.ds(t, 1), s.qoff:s.qoff + T])
                    lo = flat(HL[:, bass.ds(t, 1), s.qoff:s.qoff + T])
                    chain.link(dve.tensor_copy(hi, B_STAT[:, 0:T]))
                    dve.tensor_tensor(lo, B_STAT[:, 0:T], hi.bitcast(F32), ALU.subtract).then_inc(o_done.sem, 1)
            per = (4 if s.bias else 0) + (4 if s.sink else 0) + 4 + (4 if s.sink else 0) + (2 if s.diff else 1)
            each(dve, 0, s.pairs, s.unroll, pair, chain, per * s.unroll)

        for s in PLAN:
            if s.kind == "setup":
                setup()
            elif s.kind == "ada":
                for ch in s.chunks:
                    ada(one, lambda _, ch=ch: ch)
                flush()
            elif s.kind in ("mod", "ln", "rms"):
                if s.kind == "mod" or s.ada in ada_ready:
                    dve.wait_ge(ada_out.sem, s.a_out)
                norm(s)
            elif s.kind == "qkv":
                for it in s.items:
                    for p in it.chunk.pieces:
                        ahead(one, lambda _: p, split, late)
            elif s.kind == "ffn_in":
                ffn_in(s)
            elif s.kind == "proj":
                proj(s)
            elif s.kind == "sub_norm":
                sub_norm()
            elif s.kind == "forget_bias":
                forget_bias(s)
            elif s.kind == "qk_norm":
                qk_norm(s)
            elif s.kind == "attn":
                attn(s)
            elif s.kind == "finish":
                for b in (1, 3):
                    dve.wait_ge(out_mm, b + 1)
                    dve.tensor_copy(OUTR[:, b // 2, 512:1024], BANK[b][:, :]).then_inc(out_cp, 1)


_INS = ["x", "c", "rel_bias", "w_ada", "b_ada", "ln_g", "ln_b", "w_in_ab", "diff_lambda", "diff_subln_g",
        "w_in_cd", "forget_b", "w_o", "w_ffn_in", "w_ffn_out", "c_2", "ctx_2", "c_ctx_2", "w_ada_2", "b_ada_2",
        "norm_g_2", "w_ffn_up_2", "w_ffn_down_2", "w_in_2", "w_out_2", "qk_norm_g_2", "na_rpb_2", "wa_sink_2"]


def kernel(**inputs):
    import concourse.bacc as _bacc
    from concourse.bass_utils import run_bass_kernel_spmd as _run

    nc = _bacc.Bacc("TRN2", target_bir_lowering=False, num_devices=1)
    arrays, a, c = {}, {}, {}
    for name in _INS:
        v = np.ascontiguousarray(inputs[name])
        arrays[f"in_{name}_dram"] = v
        a[name] = nc.dram_tensor(f"in_{name}_dram", v.shape, mybir.dt.from_np(v.dtype), kind="ExternalInput").ap()
    for name, v in shape_constants().items():
        v = np.ascontiguousarray(v, dtype=np.float32)
        arrays[f"const_{name}_dram"] = v
        c[name] = nc.dram_tensor(f"const_{name}_dram", v.shape, F32, kind="ExternalInput").ap()
    out = nc.dram_tensor("out_0_dram", (1, T, D), F32, kind="ExternalOutput").ap()
    build(nc, a, c, out)
    r = _run(nc, [arrays], core_ids=[0])
    return r.results[0]["out_0_dram"]
```

```python
from contextlib import ExitStack

import numpy as np

import concourse.bass as bass
from concourse import mybir

F32 = mybir.dt.float32
F32R = mybir.dt.float32r
ALU = mybir.AluOpType
ACT = mybir.ActivationFunctionType
AX = mybir.AxisListType

P = 128
D = 1024
NT = D // P
T = 256
DFF = 2816
NF = DFF // P
DEPTH = 2
HD = 64
CW = 256
KC = 8
PIECE = 2
SPLIT = 4
RAW = 4
ALPHA = (2 * DEPTH) ** 0.25
LN_EPS, NORM_EPS = 1e-5, 1e-6
SCALE = HD ** -0.5
LAMBDA_INIT = 0.8 - 0.6
NA_H = 8
RPB_H, RPB_W = 15, 31
NEG = -1e30
BIAS_L = 384
N_T5 = 20
NA_ROWS, NA_WIDTH = 7, 128


def shape_constants():
    f = np.float32
    c = {}
    c["ident"] = np.eye(P, dtype=f)
    c["ones"] = np.ones((P, P), f)
    half = np.arange(P) // HD
    c["head_cols"] = (half[:, None] + 24 == np.arange(50)[None, :]).astype(f)
    c["head_rows"] = (np.arange(26)[:, None] == (2 * np.arange(13)[:, None] + half[None, :]).reshape(1, -1)).astype(f)
    for kv in range(2):
        m = np.zeros((P, P), f)
        m[kv * HD + np.arange(P) % HD, np.arange(P)] = 1
        c[f"dup{kv}"] = m
    quarter = (np.arange(P) // 16) % 2
    m = np.zeros((P, P), f)
    for o in range(P):
        m[o + 16 if quarter[o] == 0 else o - 16, o] = -1 if quarter[o] == 0 else 1
    c["rotate"] = m
    inv = (f(10000.0) ** (-np.arange(0, 32, 2, dtype=f) / f(32))).astype(f)
    t = np.arange(T)
    pos = np.stack([(t // 64).astype(f), (t % 64).astype(f)])
    axis = (np.arange(P) // 32) % 2
    ang = (pos[axis] * inv[np.arange(P) % 16][:, None]).astype(f)
    c["cos"], c["sin"] = np.cos(ang).astype(f), np.sin(ang).astype(f)
    d = 255 - np.arange(BIAS_L)
    n = np.maximum(d, 0)
    nf = np.maximum(n, 1).astype(f)
    large = 16 + (np.log(nf / f(16)) / f(np.log(8.0)) * f(16)).astype(np.int32)
    bucket = np.where(n < 16, n, np.minimum(large, 31))
    c["bucket_onehot"] = (np.arange(32)[:, None] == bucket[None, :]).astype(f)
    count = (d <= 128).astype(int) + (d % 4 == 0) + (d % 16 == 0)
    dil = np.where((d >= 0) & (count > 0), np.log(np.maximum(count, 1)), NEG).astype(f)
    causal = np.where(d >= 0, 0, NEG).astype(f)
    c["t5_mask"] = np.stack([causal] * 4 + [dil] * 8 + [causal] * 8).astype(f)
    i, j = np.arange(P)[:, None], np.arange(T)[None, :]
    c["causal"] = np.where(P + i - j >= 0, 0, NEG).astype(f)
    col, kcol = (i % 64), (j % 64)
    c0 = np.clip(col - 8, 0, 48)
    c["neighbour"] = np.where((kcol >= c0) & (kcol < c0 + 16), 0, NEG).astype(f)
    c["window"] = np.concatenate([np.where(np.abs(P * q + i - j) <= 128, 0, NEG) for q in range(2)],
                                 axis=1).astype(f)
    neg = np.zeros((8, 8, P), f)
    for h in range(8):
        neg[h, h] = -1
    c["neg_select"] = neg.reshape(8, 8 * P)
    return c


class Tally:

    def __init__(self, sem, credit=0):
        self.sem, self.total, self.credit = sem, credit, credit

    def take(self, n):
        at = self.total
        self.total += n
        return at


class At:

    def __init__(self, reg, u, unroll, n):
        self.reg, self.u, self.unroll, self.n = reg, u, unroll, n

    def __call__(self, f):
        first = f(self.u)
        if self.reg is None:
            return first
        steps = [f(self.u + self.unroll * k) for k in range(self.n)]
        by = steps[1] - steps[0]
        assert all(b - a == by for a, b in zip(steps, steps[1:])), steps
        return self.reg * by + first if by else first


def each(eng, lo, hi, unroll, body, chain=None, links=0):
    n = (hi - lo) // unroll
    if n < 2:
        for s in range(lo, hi):
            body(At(None, s, 1, 1))
        return
    with eng.Fori(0, n) as reg:
        if chain:
            chain.enter(reg, links)
        for u in range(unroll):
            body(At(reg, lo + u, unroll, n))
        if chain:
            chain.leave(n)
    for s in range(lo + n * unroll, hi):
        body(At(None, s, 1, 1))


class Chain:

    def __init__(self, eng, sem):
        self.eng, self.sem, self.k, self.reg, self.per = eng, sem, 0, None, 0

    def enter(self, reg, per):
        self.reg, self.per, self.start = reg, per, self.k

    def leave(self, n):
        assert self.k - self.start == self.per, (self.k - self.start, self.per)
        self.k, self.reg = self.start + n * self.per, None

    def link(self, ins):
        self.k += 1
        ins.then_inc(self.sem, 1)
        self.eng.wait_ge(self.sem, self.reg * self.per + self.k if self.reg is not None else self.k)


class Chunk:
    def __init__(self, n, kind, weight, k0, kt, c0, cw, order):
        self.n, self.kind, self.weight = n, kind, weight
        self.k0, self.kt, self.c0, self.cw, self.order = k0, kt, c0, cw, order
        self.pieces = []


class Piece:
    def __init__(self, g, chunk, k0, kt):
        self.g, self.chunk, self.k0, self.kt = g, chunk, k0, kt


class Stage:

    def __init__(self, kind, *, a_out=None, ada=None, bias=None, bias_in=None, chunks=None, diff=None,
                 first=None, gain=None, gain_b=None, gate=None, groups=None, h_wait=None, half=None, hidden=None,
                 hi=None, host=None, items=None, koff=None, ktile=None, last_ln=None, layer=None, hosted=None,
                 mm=None, n=None, name=None, nblk=None, normed=None, o_wait=None, out=None, pairs=None,
                 q_in=None, qoff=None, qtile=None, ready=None, rmm=None, ro=None, root=None, rows=None, sums=None, scale=None,
                 shift=None, silu=None, sink=None, sq=None, steps=None, take=None, unroll=None, vblk=None,
                 vcol=None, vrow=None, vw=None, what=None, x=None, x_out=None, a32=None):
        self.kind, self.a_out, self.ada, self.bias, self.bias_in = kind, a_out, ada, bias, bias_in
        self.chunks, self.diff, self.first, self.gain, self.gain_b = chunks, diff, first, gain, gain_b
        self.gate, self.groups, self.h_wait, self.half, self.hidden = gate, groups, h_wait, half, hidden
        self.hi, self.host, self.items, self.koff, self.ktile = hi, host, items, koff, ktile
        self.last_ln, self.layer, self.hosted, self.mm, self.n = last_ln, layer, hosted, mm, n
        self.name, self.nblk, self.normed, self.o_wait, self.out = name, nblk, normed, o_wait, out
        self.pairs, self.q_in, self.qoff, self.qtile, self.ready = pairs, q_in, qoff, qtile, ready
        self.rmm, self.ro, self.root, self.rows, self.sums, self.scale = rmm, ro, root, rows, sums, scale
        self.shift, self.silu, self.sink, self.sq, self.steps = shift, silu, sink, sq, steps
        self.take, self.unroll, self.vblk, self.vcol, self.vrow = take, unroll, vblk, vcol, vrow
        self.vw, self.what, self.x, self.x_out, self.a32 = vw, what, x, x_out, a32


class Group:

    def __init__(self, n, tally, done):
        self.n, self.tally, self.done = n, tally, done


class Item:

    def __init__(self, what, chunk, grp, host, n):
        self.what, self.chunk, self.grp, self.host, self.n = what, chunk, grp, host, n


class Rows:

    def __init__(self, chunks, host, grp):
        self.chunks, self.host, self.grp = chunks, host, grp


class Step:

    def __init__(self, g, u, hosts, gg, ug):
        self.g, self.u, self.hosts, self.gg, self.ug = g, u, hosts, gg, ug


def build(nc, a, c, out):
    ctx = ExitStack()
    with ctx:
        _build(nc, ctx, a, c, out)


def _build(nc, ctx, a, c, out):
    def sem(name):
        return ctx.enter_context(nc.semaphore(name))

    def sb(name, shape, dt=F32):
        return ctx.enter_context(nc.sbuf_tensor(name, shape, dt))

    X = sb("X", [P, NT, 2 * T])
    HH = sb("H_hi", [P, NT, 2 * T], F32R)
    HL = sb("H_lo", [P, NT, 2 * T], F32R)
    RAWS = sb("raw_weights", [P, RAW, KC * CW])
    WH = sb("weight_hi", [P, SPLIT, PIECE * CW], F32R)
    WL = sb("weight_lo", [P, SPLIT, PIECE * CW], F32R)
    T1 = sb("tmp1", [P, 2, 2 * T])
    T2 = sb("tmp2", [P, 2, 2 * T])
    RB = sb("rstd", [P, 2 * T])
    ident = sb("ident", [P, P])
    ones = sb("ones", [P, P])
    head_cols = sb("head_cols", [P, 50])
    rotate = sb("rotate", [P, P])
    dup = [sb(f"dup{k}", [P, P]) for k in range(2)]
    SILU_C = sb("silu_c", [P, 24])
    C_COLS = sb("c_cols", [P, 24])
    B1 = sb("b_ada_cols", [P, 2, 48])
    B2 = sb("b_ada2_cols", [P, 2, 72])
    G_COLS = sb("gain_cols", [P, 112])
    E_COLS = sb("head_gain_cols", [P, 9])
    AD = [sb("ada0", [P, 48, 1]), sb("ada1", [P, 48, 1]), sb("ada2", [P, 72, 2]), sb("ada3", [P, 72, 2])]
    GS = sb("gain_scale", [P, NT, 2])
    ACC = sb("ada_partial", [P, 2, 2, CW])
    EPS = sb("eps", [P, 2])
    SINK = sb("sink", [P, 16])
    LAM = sb("lam", [P, 8])
    FB = sb("forget_bias", [8, 1])
    NM = sb("neg_max", [P, 4])
    RS = sb("row_sum", [P, 4])
    ES = sb("sink_exp", [P, 4])
    RI = sb("row_scale", [P, 4])
    CUMT = sb("cum_cols", [P, 2, 8])

    base = (nc.sbuf_base + 63) // 64 * 64
    used = {"at": base}

    def region(name, shape, dt=F32, at=None):
        size = 4 * int(np.prod(shape[1:]))
        if at is None:
            at = used["at"]
            used["at"] = at + (size + 31) // 32 * 32
        return nc.alloc_sbuf_tensor_at(name, shape, dt, offset=at)

    AH = region("hidden_hi", [P, NF, 2 * T], F32R)
    AL = region("hidden_lo", [P, NF, 2 * T], F32R)
    used["at"] = base
    QB = region("q", [P, 8, 2 * T])
    KB = region("k", [P, 8, 2 * T])
    VB = region("v", [P, 4 * 640])
    PR = region("probs", [P, 4, 512])
    PT = region("probs_turned", [P, 4, 4, P])
    BT = region("bias", [P, 4096])
    OF = region("o_diff", [P, 4, T])
    QS = region("q_pair", [P, T])
    KS = region("k_pair", [P, 2 * T])
    VS = region("v_pair", [P, 4, P])
    COS = region("cos", [P, T])
    SIN = region("sin", [P, T])
    CAUSAL = region("causal", [P, T])
    NEIGH = region("neighbour", [P, T])
    WINDOW = region("window", [P, 2, T])
    assert used["at"] <= nc.sbuf_usable_end and base + 2 * NF * 2 * T * 4 <= nc.sbuf_usable_end
    used["at"] = base
    XIN = region("x_rows", [P, 2, D])
    CIN = region("ctx_rows", [P, 2, D])
    ROWS = [region(f"rows{k}", [n, P]) for k, n in enumerate((120, 72, 72, 112, 9))]
    ONEHOT = region("onehot", [32, BIAS_L])
    TABLE = region("table", [32, N_T5])
    T5MASK = region("t5_mask", [N_T5, BIAS_L])
    T5ROW = region("t5_rows", [N_T5, BIAS_L])
    RPB = region("rpb_rows", [NA_H, 2, NA_ROWS, NA_WIDTH])
    LROW = region("lambda_rows", [P, 4, HD])
    LPROD = region("lambda_prod", [P, 2, HD])
    assert used["at"] <= nc.sbuf_usable_end
    OUTR = XIN
    HEAD_ROWS = PR[0:26, :, :].rearrange("p j n -> p (j n)")
    FD = PR[0:8, 0, 0:T]
    FD_ABS = PR[0:8, 0, T:2 * T]
    FD_MIN = PR[0:8, 1, 0:T]
    CUM = PR[0:8, 1, T:2 * T]
    FD_ONE = PT[0:8, 0, 0:2, :]
    NEGSEL = PT[0:8, 1:3, :, :]

    BANK = [ctx.enter_context(nc.psum_tensor(f"bank{b}", [P, 512], F32)) for b in range(8)]
    PAIR = [(BANK[0], BANK[1]), (BANK[2], BANK[3])]
    B_T, B_STAT, B_ADA = (BANK[4], BANK[5]), BANK[6], BANK[7]

    t5_dram = nc.dram_tensor("t5_skew", (N_T5, P, BIAS_L), F32, kind="Internal").ap()
    na_dram = nc.dram_tensor("na_skew", (2, NA_H, 64, NA_ROWS * NA_WIDTH), F32, kind="Internal").ap()

    landed = [sem(f"chunk_landed{i}") for i in range(RAW)]
    hi_done, lo_done = sem("hi_done"), sem("lo_done")
    piece_used = Tally(sem("piece_used"), SPLIT)
    ada_used, ada_sum, ada_out = sem("ada_used"), sem("ada_sum"), sem("ada_out")
    forget_used = sem("forget_chunk_used")
    ev_act, ev_dve = Tally(sem("evac_act"), 2), Tally(sem("evac_dve"), 2)
    const_in, rows_in, setup_mm = sem("const_in"), sem("rows_in"), sem("setup_mm")
    setup_act, t5_rows, region_free = sem("x_turned"), sem("t5_rows_ready"), sem("lambda_done")
    skew_out, skew_src = sem("skew_out"), sem("skew_src")
    silu_done, cols_done = sem("silu_done"), sem("cols_done")
    lam_sum, lam_exp = sem("lambda_sums"), sem("lambda_exp")
    h_ready = Tally(sem("h_ready"), 2)
    mod_src, mod_hi, mod_t2 = Tally(sem("mod_src")), Tally(sem("mod_hi")), Tally(sem("mod_t2"), 2)
    centred = Tally(sem("centred"))
    stat_in, stat_mm = Tally(sem("stat_in")), Tally(sem("stat_mm"), 2)
    rstd_sq, mean_mm, x_ready = Tally(sem("rstd_sqrt")), Tally(sem("mean_mm")), Tally(sem("x_ready"))
    silu_g, act32, act_hi = Tally(sem("silu_g")), Tally(sem("act32"), 1), Tally(sem("act_hi"))
    act_ready = Tally(sem("act_ready"), 1)
    bias_in = Tally(sem("bias_in"))
    fg_x, fg_abs, fg_exp = sem("forget_logit"), sem("forget_abs"), sem("forget_exp")
    fg_cum, fg_sel, fg_mm, fg_free = sem("forget_cum"), sem("forget_select"), sem("forget_mm"), sem("forget_free")
    qn_sq, qn_sums, qn_root = Tally(sem("qknorm_sq")), Tally(sem("qknorm_sums")), Tally(sem("qknorm_root"))
    qn_mm, qn_out, qn_rstd = Tally(sem("qknorm_spread")), Tally(sem("qknorm_out")), sem("qknorm_rstd")
    rope_mm, rope_out = Tally(sem("rope_mm")), Tally(sem("rope_out"))
    q_staged, v_staged = Tally(sem("q_staged")), Tally(sem("v_staged"))
    scores, nmax = Tally(sem("scores"), 4), Tally(sem("neg_max_ready"))
    sink_done = Tally(sem("sink_exp_done"))
    exp_done, probs = Tally(sem("exp_done"), 4), Tally(sem("probs_ready"))
    turned, copied = Tally(sem("probs_turned"), 4), Tally(sem("turned_copied"), 2)
    pv_done, o_done = Tally(sem("pv_done"), 1), Tally(sem("o_done"), 1)
    sub_sq, sub_mm, sub_rt, sub_out = sem("sub_sq"), sem("sub_mm"), sem("sub_root"), sem("sub_out")
    dve_chain, act_chain, pool_chain = sem("dve_chain"), sem("act_chain"), sem("pool_chain")
    out_mm, out_cp, out_dma = sem("out_mm"), sem("out_cp"), sem("out_dma")
    credited = [piece_used, ev_act, ev_dve, h_ready, mod_t2, act32, stat_mm, act_ready,
                 scores, exp_done, turned, copied, pv_done, o_done]

    CHUNKS, PIECES, GROUPS, ADA = [], [], [], []
    W = {"ada": [a["w_ada"][0], a["w_ada"][1], a["w_ada_2"][0], a["w_ada_2"][1]]}
    counts = {"a": 0, "f": 0}

    def view(w):
        return w.rearrange("(t p) n -> p t n", p=P)

    def chunk(kind, w, k0, kt, c0, cw=CW, order=None):
        ch = Chunk(len(CHUNKS), kind, w, k0, kt, c0, cw, order)
        CHUNKS.append(ch)
        if kind == "g":
            for k in range(0, kt, PIECE):
                pc = Piece(len(PIECES), ch, k, min(PIECE, kt - k))
                PIECES.append(pc)
                ch.pieces.append(pc)
        else:
            ch.raw_order = counts[kind]
            counts[kind] += 1
        return ch

    def group(engine):
        tally = ev_act if engine == "act" else ev_dve
        g = Group(n=len(GROUPS), tally=tally, done=tally.take(1) + 1)
        GROUPS.append(g)
        return g

    ada_at = {"m": 0, "c": 0}
    ADA_CHUNKS = [24, 24, 36, 36]

    def ada_chunk():
        m, k = ada_at["m"], ada_at["c"]
        ch = chunk("a", view(W["ada"][m]), 0, KC, CW * k, order=(m, k))
        ADA.append(ch)
        ada_at["c"] += 1
        if ada_at["c"] == ADA_CHUNKS[m]:
            ada_at.update(m=m + 1, c=0)
        return ch

    PLAN = []
    state = {"q_in": 0, "normed": None}
    def add(kind, **k):
        now = dict(h_wait=h_ready.total, o_wait=o_done.total, a_out=len(ADA), x=x_ready.total,
                   bias_in=bias_in.total, last_ln=False)
        PLAN.append(Stage(kind, **{**now, **k}))
        return PLAN[-1]

    def ada_run(n):
        add("ada", chunks=[ada_chunk() for _ in range(n)])

    def mod(kind, ada, shift, scale, n, gain=None, gain_b=None, last_ln=False):
        s = add(kind, ada=ada, shift=shift, scale=scale, n=n, gain=gain, gain_b=gain_b, last_ln=last_ln)
        if kind != "mod":
            s.x = x_ready.total
            s.stat_in, s.stat = stat_in.take(8), stat_mm.take(8)
            s.rstd = rstd_sq.take(1)
            if kind == "ln":
                s.mean, s.cen = mean_mm.take(1), centred.take(8)
        if kind == "ln":
            s.x_out = x_ready.take(1)
        if not last_ln:
            s.src = mod_src.take(8) if kind != "mod" else None
            s.hi, s.t2, s.h = (t.take(8) for t in (mod_hi, mod_t2, h_ready))

    def ffn(w_in, w_out, n, ada, gate, half, hosted, first):
        steps, host, before = [], hosted, len(ADA)
        for s in range(NF // 2):
            g = chunk("g", view(w_in), 0, KC, CW * s)
            h1 = ada_chunk() if host else None
            u = chunk("g", view(w_in), 0, KC, DFF + CW * s)
            h2 = ada_chunk() if host else None
            steps.append(Step(g=g, u=u, hosts=[h1, h2] if host else [None, None],
                               gg=group("act"), ug=group("dve")))
        add("ffn_in", n=n, steps=steps, silu=silu_g.take(11), a32=act32.take(11), hi=act_hi.take(11),
            ready=act_ready.take(11), host=host, a_out=before)
        groups, before = [], len(ADA)
        for m in range(4):
            cs = [chunk("g", view(w_out), k, min(KC, NF - k), CW * m) for k in range(0, NF, KC)]
            groups.append(Rows(chunks=cs, host=ada_chunk() if host and ada_at["m"] < 4 else None,
                               grp=group("dve")))
        add("proj", n=n, groups=groups, ada=ada, gate=gate, half=half, hidden=True, first=first,
            ready=act_ready.total, x_out=x_ready.take(1), a_out=before)

    def w_out(w, n, ada, gate, first, hosted):
        before = len(ADA)
        groups = [Rows(chunks=[chunk("g", view(w), 0, KC, CW * m)], host=ada_chunk() if hosted else None,
                       grp=group("dve")) for m in range(4)]
        add("proj", n=n, groups=groups, ada=ada, gate=gate, half=False, hidden=False, first=first,
            ready=o_done.total, x_out=x_ready.take(1), a_out=before)

    def qkv(w, items, n, every, q_n):
        st = add("qkv", n=n, items=[], ready=h_ready.total, first=n == T)
        for c0, what in items:
            if what[0] == "forget":
                st.items.append(Item(what=what, chunk=chunk("f", view(w), 0, KC, c0, 8), grp=None, host=None, n=n))
            else:
                ch = chunk("g", view(w), 0, KC, c0)
                host = ada_chunk() if every and len(st.items) % every == every - 1 else None
                st.items.append(Item(what=what, chunk=ch, grp=group("act"), host=host,
                                     n=q_n if what[0] == "q" else n))
        st.done = ev_act.total
        state.update(q_in=st.done, normed=None)

    def attention(name, pairs, unroll, **k):
        s = add("attn", name=name, pairs=pairs, unroll=unroll, **state, **k)
        s.tper = 2 if s.diff else 4
        s.units, s.bias_in = 4 * pairs, bias_in.total
        s.q, s.v = q_staged.take(pairs), v_staged.take(pairs)
        s.sc, s.mx, s.ex = scores.take(s.units), nmax.take(s.units), exp_done.take(s.units)
        s.sk = sink_done.take(s.units) if s.sink else None
        s.pb, s.tu, s.cp = (t.take(s.tper * pairs) for t in (probs, turned, copied))
        s.pv, s.o = pv_done.take(pairs), o_done.take(pairs)

    def causal_heads(name, q, k, vcol, out_tile, bias, diff=False):
        attention(name, 4, 1, diff=diff, sink=None, qtile=lambda p: q + p, ktile=lambda p: k + p,
                  vcol=lambda p: vcol + P * p, vw=P, vblk=0, vrow=D, nblk=lambda qt: qt + 1, qoff=0, koff=0,
                  bias=bias, out=lambda p: out_tile + p)

    def t5(h0):
        def bias(p, hh, qt):
            return "bias", T * (h0(p, hh)) + (P if qt == 0 else 0), P * (qt + 1)
        return bias

    add("setup")
    ada_run(8)
    mod("mod", 0, 0, 1, T)
    qkv(a["w_in_ab"][0],
        [(0, ("q", 0)), (256, ("q", 2)), (512, ("k", 0)), (768, ("k", 2)), (1024, ("v", 0)), (1280, ("v", 256)),
         (1536, ("q", 4)), (1792, ("q", 6)), (2048, ("k", 4)), (2304, ("k", 6)), (2560, ("v", 512)),
         (2816, ("v", 768))], T, 1, T)
    add("bias", what="t5", rows=(0, 12), take=bias_in.take(32))
    causal_heads("differential", 0, 0, 0, 0, t5(lambda p, hh: p), diff=True)
    add("sub_norm")
    causal_heads("dilated", 4, 4, 512, 4, t5(lambda p, hh: 4 + 2 * p + hh))
    w_out(a["w_o"][0], T, 0, 2, True, True)
    mod("ln", 0, 3, 4, T, gain=0, gain_b=32)
    ffn(a["w_ffn_in"][0], a["w_ffn_out"][0], T, 0, 5, False, True, True)
    mod("ln", 1, 0, 1, T, gain=8, gain_b=40)
    qkv(a["w_in_cd"][0],
        [(0, ("q", 0)), (256, ("q", 2)), (512, ("k", 0)), (768, ("k", 2)), (1024, ("v", 0)), (1280, ("v", 256)),
         (1536, ("q", 4)), (1792, ("q", 6)), (2048, ("k", 4)), (2304, ("k", 6)), (2560, ("v", 512)),
         (2816, ("v", 768)), (3072, ("forget",))], T, 2, T)
    add("bias", what="t5", rows=(12, 8), take=bias_in.take(32))
    causal_heads("moba", 0, 0, 0, 0, t5(lambda p, hh: 2 * p + hh))
    add("forget_bias")
    causal_heads("forget", 4, 4, 512, 4,
                 lambda p, hh, qt: ("bias", 512 * (2 * p + hh) + T * qt, P * (qt + 1)))
    w_out(a["w_o"][1], T, 1, 2, True, False)
    mod("ln", 1, 3, 4, T, gain=16, gain_b=48)
    ffn(a["w_ffn_in"][1], a["w_ffn_out"][1], T, 1, 5, False, False, True)
    mod("ln", 1, 0, 0, T, gain=24, gain_b=56, last_ln=True)
    for l in range(DEPTH):
        last = l == DEPTH - 1
        n = 2 * T
        mod("rms", 2 + l, 0, 1, n, gain=64 + 24 * l)
        ffn(a["w_ffn_up_2"][l, 0], a["w_ffn_down_2"][l, 0], n, 2 + l, 2, True, not last, False)
        mod("rms", 2 + l, 3, 4, n, gain=64 + 24 * l + 8)
        qkv(a["w_in_2"][l],
            [(0, ("q", 0)), (256, ("q", 2)), (512, ("q", 4)), (768, ("q", 6)), (1024, ("k", 0)),
             (1280, ("k", 2)), (1536, ("v", 0)), (1792, ("v", 256)), (2048, ("kv",))], n, 0 if last else 1, T if last else n)
        add("bias", what="na", layer=l, take=bias_in.take(16 * 37))
        tiles = [(i, 2 * T) for i in (12, 8, 9, 10, 11)] + [(i, T if last else n) for i in (4, 5, 6, 7, 0, 1, 2, 3)]
        add("qk_norm", layer=l, items=tiles, sq=qn_sq.take(13), sums=qn_sums.take(13), mm=qn_mm.take(13),
            root=qn_root.take(1), out=qn_out.take(13), rmm=rope_mm.take(7), ro=rope_out.take(7),
            q_in=state["q_in"], bias_in=bias_in.total)
        state["normed"] = (qn_out.total, rope_out.total)
        two = dict(diff=False, nblk=lambda qt: 4, qoff=0, koff=0, vblk=0, vrow=640)
        attention("neighbourhood", 4, 1, sink=None, qtile=lambda p: p, ktile=lambda p: p,
                  vcol=lambda p: P * p, vw=P,
                  bias=lambda p, hh, qt: ("bias", 512 * (2 * p + hh) + T * qt, T), out=lambda p: p, **two)
        attention("window", 4, 2, sink=(lambda p, hh: 8 * l + 2 * p + hh) if l == 0 else
                  (lambda p, hh: 8 + 2 * p + hh), qtile=lambda p: 4 + p, ktile=lambda p: 5 + p // 2,
                  vcol=lambda p: 512 + HD * (p // 2), vw=HD,
                  bias=lambda p, hh, qt: ("window", qt, T), out=lambda p: 4 + p, **two)
        if not last:
            one = dict(diff=False, nblk=lambda qt: 2, qoff=T, koff=T, vblk=2, vrow=640, bias=None)
            attention("context_a", 4, 1, sink=None, qtile=lambda p: p, ktile=lambda p: p,
                      vcol=lambda p: P * p, vw=P, out=lambda p: p, **one)
            attention("context_b", 4, 2, sink=lambda p, hh: 2 * p + hh, qtile=lambda p: 4 + p,
                      ktile=lambda p: 5 + p // 2, vcol=lambda p: 512 + HD * (p // 2), vw=HD,
                      out=lambda p: 4 + p, **one)
        n2 = T if last else 2 * T
        w_out(a["w_out_2"][l], n2, 2 + l, 5, False, not last)
        mod("rms", 2 + l, 6, 7, n2, gain=64 + 24 * l + 16)
        ffn(a["w_ffn_up_2"][l, 1], a["w_ffn_down_2"][l, 1], n2, 2 + l, 8, True, not last, False)
    add("finish")
    assert len(ADA) == sum(ADA_CHUNKS), len(ADA)
    for s, after in zip(PLAN, PLAN[1:] + [None]):
        s.hosted = after.a_out if after else len(ADA)

    def raw_ap(n, kt, cw):
        return RAWS[:, n % RAW, 0:kt * cw].rearrange("p (t n) -> p t n", t=kt)

    def wait_landed(eng, at, f):
        eng.wait_ge(landed[f(at.u).n % RAW], at(lambda s: 16 * (f(s).n // RAW + 1)))

    def wait_slot(eng, at, f):
        if f(at.u).n < RAW:
            return
        before = lambda s: CHUNKS[f(s).n - RAW]
        if before(at.u).kind == "g":
            eng.wait_ge(lo_done, at(lambda s: before(s).pieces[-1].g + 1))
        else:
            eng.wait_ge(ada_used if before(at.u).kind == "a" else forget_used,
                        at(lambda s: before(s).raw_order + 1))

    act_waited, pool_waited = sem("act_waited"), sem("pool_waited")

    def wait_apart(eng, on, value, count):
        eng.wait_ge(on, value)
        eng.sem_inc(count, 1)

    block = ctx.enter_context(nc.Block())

    @block.sync
    def _(sp):
        def load(at, f):
            ch = f(at.u)
            wait_slot(sp, at, f)
            src = ch.weight[:, ch.k0:ch.k0 + ch.kt, bass.ds(at(lambda s: f(s).c0), ch.cw)]
            sp.dma_start(raw_ap(ch.n, ch.kt, ch.cw), src).then_inc(landed[ch.n % RAW], 16)

        def load_one(ch):
            load(At(None, 0, 1, 1), lambda s: ch)

        def ffn_in(s):
            parts = 2 if not s.host else 4

            def step(at):
                load(at, lambda k: s.steps[k].g)
                if s.host:
                    load(at, lambda k: s.steps[k].hosts[0])
                load(at, lambda k: s.steps[k].u)
                if s.host:
                    load(at, lambda k: s.steps[k].hosts[1])
            step(At(None, 0, 1, 1))
            if not s.host:
                step(At(None, 1, 1, 1))
                each(sp, 2, 10, 2, step)
                step(At(None, 10, 1, 1))
            else:
                each(sp, 1, 11, RAW // parts, step)

        for s in PLAN:
            if s.kind == "ada":
                for ch in s.chunks:
                    load_one(ch)
            elif s.kind == "qkv":
                for it in s.items:
                    load_one(it.chunk)
                    if it.host:
                        load_one(it.host)
            elif s.kind == "ffn_in":
                ffn_in(s)
            elif s.kind == "proj":
                for g in s.groups:
                    for ch in g.chunks:
                        load_one(ch)
                    if g.host:
                        load_one(g.host)
        sp.wait_ge(out_cp, 4)
        sp.dma_start(out.rearrange("a (q p) d -> p (a q) d", p=P), OUTR[:, :, :]).then_inc(out_dma, 16)
        sp.wait_ge(out_dma, 16)

    @block.gpsimd
    def _(pool):
        chain = Chain(pool, pool_chain)

        def const(dst, src):
            pool.dma_start(dst, src).then_inc(const_in, 16)

        def setup():
            for t in credited:
                pool.sem_inc(t.sem, t.credit)
            const(head_cols[:, :], c["head_cols"])
            const(rotate[:, :], c["rotate"])
            for k in range(2):
                const(dup[k][:, :], c[f"dup{k}"])
            const(ONEHOT[:, :], c["bucket_onehot"])
            const(T5MASK[:, :], c["t5_mask"])
            const(TABLE[:, 0:12], a["rel_bias"])
            const(TABLE[:, 12:20], a["rel_bias"][:, 0:8])
            const(SINK[:, :], a["wa_sink_2"].rearrange("l h -> (l h)").rearrange("(o n) -> o n", o=1)
                  .broadcast_to([P, 16]))
            const(FB[:, :], a["forget_b"].rearrange("l h -> h l"))
            const(LROW[:, :, :], a["diff_lambda"].broadcast_to([P, 4, HD]))
            chain.link(pool.memset(RPB[:, :, :, :], 0.0))
            for l in range(2):
                pool.dma_start(RPB[:, l, :, 48:48 + RPB_W],
                               a["na_rpb_2"][l, :, 4:4 + NA_ROWS, :]).then_inc(skew_src, 16)
            pool.wait_ge(skew_src, 32)
            for l in range(2):
                src = RPB[:, l, :, :].rearrange("h i w -> h (i w)")
                pool.dma_start(na_dram[l], src[:, None, :].broadcast_to([NA_H, 64, NA_ROWS * NA_WIDTH])
                               ).then_inc(skew_out, 16)
            pool.wait_ge(t5_rows, 1)
            pool.dma_start(t5_dram, T5ROW[:, None, :].broadcast_to([N_T5, P, BIAS_L])).then_inc(skew_out, 16)
            pool.wait_ge(skew_out, 48)

        def bias(s):
            pool.wait_ge(region_free, 1)
            pool.wait_ge(h_ready.sem, s.h_wait)
            if s.what == "t5":
                h0, n = s.rows
                src = bass.AP(t5_dram.tensor, h0 * P * BIAS_L + P - 1,
                              [[BIAS_L - 1, P], [P * BIAS_L, n], [1, T]])
                pool.dma_start(BT[:, 0:n * T].rearrange("p (h k) -> p h k", h=n), src).then_inc(bias_in.sem, 16)
                pool.dma_start(CAUSAL[:, :], c["causal"]).then_inc(bias_in.sem, 16)
            else:
                row = NA_ROWS * NA_WIDTH
                for q in range(4):
                    half, qt = q % 2, q // 2
                    for h in range(NA_H):
                        src = bass.AP(na_dram.tensor, (s.layer * NA_H + h) * 64 * row + (3 - q) * NA_WIDTH + 63,
                                      [[row - 1, 64], [NA_WIDTH, 4], [1, 64]])
                        dst = BT[64 * half:64 * half + 64, 512 * h + T * qt:512 * h + T * qt + T]
                        pool.dma_start(dst.rearrange("p (i k) -> p i k", i=4), src).then_inc(bias_in.sem, 16)
                pool.dma_start(HEAD_ROWS[:, 0:13 * P], c["head_rows"]).then_inc(bias_in.sem, 16)
                for d, nm in ((COS, "cos"), (SIN, "sin"), (NEIGH, "neighbour")):
                    pool.dma_start(d[:, :], c[nm]).then_inc(bias_in.sem, 16)
                pool.dma_start(WINDOW[:, :, :].rearrange("p q k -> p (q k)"), c["window"]
                               ).then_inc(bias_in.sem, 16)

        def low(s):
            def tile(at):
                par = at.u % 2
                t = at(lambda k: k)
                pool.wait_ge(mod_hi.sem, at(lambda k: s.hi + k + 1))
                pool.wait_ge(mod_t2.sem, at(lambda k: s.t2 + k + 1))
                pool.tensor_tensor(HL[:, bass.ds(t, 1), 0:s.n], T2[:, par:par + 1, 0:s.n],
                                   HH[:, bass.ds(t, 1), 0:s.n].bitcast(F32), ALU.subtract
                                   ).then_inc(h_ready.sem, 1)
            each(pool, 0, 8, 2, tile)

        def ffn_in(s):
            def step(at):
                t = at(lambda k: 2 * k)
                pool.wait_ge(act_hi.sem, at(lambda k: s.hi + k + 1))
                pool.tensor_tensor(AL[:, bass.ds(t, 2), 0:s.n], T2[:, :, 0:s.n],
                                   AH[:, bass.ds(t, 2), 0:s.n].bitcast(F32), ALU.subtract
                                   ).then_inc(act_ready.sem, 1)
            each(pool, 0, 11, 1, step)

        def attn(s):
            vb = VB[:, 0:4 * s.vrow if s.vrow == 640 else 2 * s.vrow].rearrange("p (b n) -> p b n", n=s.vrow)
            nb = s.nblk(1)

            def pair(at):
                wait_apart(pool, scores.sem, at(lambda p: s.sc + 4 * p), pool_waited)
                pool.tensor_copy(QS[:, :], QB[:, bass.ds(at(s.qtile), 1), s.qoff:s.qoff + T]
                                 .rearrange("p o t -> p (o t)"))
                nk = P * nb
                pool.tensor_copy(KS[:, 0:nk], KB[:, bass.ds(at(s.ktile), 1), s.koff:s.koff + nk]
                                 .rearrange("p o t -> p (o t)")).then_inc(q_staged.sem, 1)
                wait_apart(pool, pv_done.sem, at(lambda p: s.pv + p), pool_waited)
                pool.tensor_copy(VS[:, 0:nb, 0:s.vw], vb[:, s.vblk:s.vblk + nb, bass.ds(at(s.vcol), s.vw)]
                                 ).then_inc(v_staged.sem, 1)
            pool.wait_ge(ev_act.sem, s.q_in)
            if s.normed:
                pool.wait_ge(qn_out.sem, s.normed[0])
                pool.wait_ge(rope_out.sem, s.normed[1])
            each(pool, 0, s.pairs, s.unroll, pair)

        for s in PLAN:
            if s.kind == "setup":
                setup()
            elif s.kind in ("mod", "ln", "rms") and not s.last_ln:
                low(s)
            elif s.kind == "ffn_in":
                ffn_in(s)
            elif s.kind == "bias":
                bias(s)
            elif s.kind == "forget_bias":
                pool.wait_ge(o_done.sem, s.o_wait)
                pool.dma_start(NEGSEL, c["neg_select"].rearrange("h (a b p) -> h a b p", a=2, b=4)
                               ).then_inc(fg_sel, 16)
            elif s.kind == "attn":
                attn(s)


    @block.tensor
    def _(pe):
        closed, one = {"at": 0}, At(None, 0, 1, 1)

        def mm(o, w, x, start, stop):
            return pe.matmul(o, w, x, start=start, stop=stop, skip_group_check=True)

        def product(o, kt, wh, wl, xh, xl, start, stop):
            mm(o, wh, xh, start, False)
            mm(o, wh, xl, False, False)
            return mm(o, wl, xh, False, stop)

        def ada(at, f):
            if f(at.u).raw_order > closed["at"]:
                sum_rows(at, lambda s: ADA[f(s).raw_order - 1])

        def close(a):
            if a > closed["at"]:
                sum_rows(one, lambda _: ADA[a - 1])
                closed["at"] = a

        def sum_rows(at, f):
            ch = f(at.u)
            nv = 1 if ch.order[0] < 2 else 2
            pe.wait_ge(ada_used, at(lambda s: f(s).raw_order + 1))
            if ch.raw_order > 0:
                pe.wait_ge(ada_out, at(lambda s: f(s).raw_order))
            for j in range(2):
                for v in range(nv):
                    ins = mm(B_ADA[:, j * nv + v:j * nv + v + 1],
                             ACC[:, ch.raw_order % 2, v, j * P:(j + 1) * P], ones[:, 0:1], True, True)
            ins.then_inc(ada_sum, 1)

        def wait_bank(at, f):
            g = f(at.u)
            if g.n >= 2:
                before = lambda s: GROUPS[f(s).n - 2]
                pe.wait_ge(before(at.u).tally.sem, at(lambda s: before(s).done))

        def features(at, f, grp, kt_all, k_base, xh, xl, n, width=2, left=None, ready=None):
            ch = f(at.u)
            for i, pc in enumerate(ch.pieces):
                pe.wait_ge(lo_done, at(lambda s: f(s).pieces[i].g + 1))
                wh = WH[:, pc.g % SPLIT, :].rearrange("p (t n) -> p t n", n=CW)
                wl = WL[:, pc.g % SPLIT, :].rearrange("p (t n) -> p t n", n=CW)
                for k in range(pc.kt):
                    kk = k_base + pc.k0 + k
                    if ready:
                        ready(kk)
                    for j in range(width):
                        ins = product(PAIR[grp.n % 2][j][:, 0:n], kk, wh[:, k, j * P:(j + 1) * P],
                                      wl[:, k, j * P:(j + 1) * P], xh[:, kk, 0:n], xl[:, kk, 0:n],
                                      kk == 0, kk == kt_all - 1)
                    if left:
                        ins = left(wh, wl, k, kk)
                ins.then_inc(piece_used.sem, 1)

        def tokens(ch, grp, n, col, cw, bank_of, at_col):
            def part(wh, wl, k, kk):
                for tt in range(n // P):
                    o = bank_of(tt)[:, at_col(tt):at_col(tt) + cw]
                    first = kk == 0 and at_col(tt) == 0
                    h, lo = HH[:, kk, tt * P:(tt + 1) * P], HL[:, kk, tt * P:(tt + 1) * P]
                    mm(o, h, wh[:, k, col:col + cw], first, False)
                    mm(o, h, wl[:, k, col:col + cw], False, False)
                    ins = mm(o, lo, wh[:, k, col:col + cw], False, kk == KC - 1)
                return ins
            return part

        def modulated(last):
            return lambda kk: pe.wait_ge(h_ready.sem, last - NT + kk + 1)

        def qkv(s):
            for it in s.items:
                ch, grp = it.chunk, it.grp
                ready = modulated(s.ready) if it is s.items[0] else None
                if it.what[0] == "forget":
                    close(s.hosted)
                    wait_landed(pe, one, lambda _: ch)
                    pe.wait_ge(ada_out, s.hosted)
                    w = raw_ap(ch.n, KC, 8)
                    for k in range(KC):
                        mm(B_ADA[0:8, 0:T], w[:, k, :], HH[:, k, 0:T].bitcast(F32), k == 0, False)
                        ins = mm(B_ADA[0:8, 0:T], w[:, k, :], HL[:, k, 0:T].bitcast(F32), False, k == KC - 1)
                    ins.then_inc(forget_used, 1)
                    continue
                wait_bank(one, lambda _: grp)
                pair = PAIR[grp.n % 2]
                if it.what[0] == "v":
                    part = tokens(ch, grp, s.n, 0, CW, lambda tt: pair[tt // 2], lambda tt: CW * (tt % 2))
                    features(one, lambda _: ch, grp, KC, 0, HH, HL, s.n, 0, part)
                elif it.what[0] == "kv":
                    part = tokens(ch, grp, s.n, P, P, lambda tt: pair[1], lambda tt: P * tt)
                    features(one, lambda _: ch, grp, KC, 0, HH, HL, s.n, 1, part)
                else:
                    features(one, lambda _: ch, grp, KC, 0, HH, HL, it.n, ready=ready)
                if it.host:
                    ada(one, lambda _: it.host)
            close(s.hosted)

        def ffn_in(s):
            def step(at, ready=None):
                wait_bank(at, lambda k: s.steps[k].gg)
                features(at, lambda k: s.steps[k].g, s.steps[at.u].gg, KC, 0, HH, HL, s.n, ready=ready)
                if s.host:
                    ada(at, lambda k: s.steps[k].hosts[0])
                wait_bank(at, lambda k: s.steps[k].ug)
                features(at, lambda k: s.steps[k].u, s.steps[at.u].ug, KC, 0, HH, HL, s.n)
                if s.host:
                    ada(at, lambda k: s.steps[k].hosts[1])
            step(At(None, 0, 1, 1), modulated(s.h_wait))
            each(pe, 1, 11, 1, step)
            close(s.hosted)

        def proj(s):
            xh, xl, kt = (AH, AL, NF) if s.hidden else (HH, HL, NT)
            if not s.hidden:
                pe.wait_ge(o_done.sem, s.ready)

            def hidden(kk):
                if kk % 2 == 0:
                    pe.wait_ge(act_ready.sem, s.ready - NF // 2 + kk // 2 + 1)

            def two(at):
                for b in range(2):
                    grp = lambda k: s.groups[2 * k + b]
                    wait_bank(at, lambda k: grp(k).grp)
                    for j in range(len(grp(0).chunks)):
                        features(at, lambda k: grp(k).chunks[j], grp(at.u).grp, kt, KC * j, xh, xl, s.n,
                                 ready=hidden if s.hidden and at.u == 0 and b == 0 else None)
                    if grp(at.u).host:
                        ada(at, lambda k: grp(k).host)
            for k in range(2):
                two(At(None, k, 1, 1))
            close(s.hosted)

        def setup():
            pe.wait_ge(rows_in, 16 * 16)
            at = 0
            for r in ROWS:
                n = r.shape[0]
                ins = pe.transpose(BANK[0][:, at:at + n], r[:, :], ident[0:n, 0:n])
                at += n
            ins.then_inc(setup_mm, 1)

            def turn(src, b, k):
                for t in range(2):
                    for q in range(2):
                        ins = pe.transpose(b[:, T * t + P * q:T * t + P * q + P],
                                           src[:, q, P * (2 * k + t):P * (2 * k + t + 1)], ident[:, :])
                ins.then_inc(setup_mm, 1)
            for k in range(4):
                turn(XIN, BANK[1 + k], k)
            for k in range(3):
                turn(CIN, BANK[5 + k], k)
            pe.wait_ge(setup_act, 1)
            turn(CIN, BANK[1], 3)
            pe.wait_ge(const_in, 16 * 11)
            pe.wait_ge(setup_act, 2)
            mm(BANK[2][0:N_T5, 0:BIAS_L], TABLE[:, :], ONEHOT[:, :], True, True).then_inc(setup_mm, 1)
            pe.wait_ge(cols_done, 1)

        def stats(s):
            if s.kind == "ln":
                pe.wait_ge(x_ready.sem, s.x)
                for t in range(NT):
                    ins = mm(B_STAT[:, 0:s.n], ones[:, :], X[:, t, 0:s.n], t == 0, t == NT - 1)
                ins.then_inc(mean_mm.sem, 1)
            bank = B_T[0] if s.kind == "ln" else B_STAT
            for t in range(NT):
                pe.wait_ge(stat_in.sem, s.stat_in + t + 1)
                mm(bank[:, 0:s.n], ones[:, :], T1[:, t % 2, 0:s.n], t == 0, t == NT - 1).then_inc(stat_mm.sem, 1)

        def sub_norm():
            for t in range(4):
                pe.wait_ge(sub_sq, t + 1)
                if t >= 2:
                    pe.wait_ge(sub_rt, t - 1)
                mm(B_T[t % 2][:, 0:T], ones[:, :], T1[:, t % 2, 0:T], True, True).then_inc(sub_mm, 1)

        def forget_bias(s):
            pe.wait_ge(fg_cum, 1)
            for q in range(2):
                ins = pe.transpose(B_T[0][:, 8 * q:8 * q + 8], CUM[:, P * q:P * q + P], ident[0:8, 0:8])
            ins.then_inc(fg_mm, 1)
            pe.wait_ge(fg_sel, 16)
            for h in range(8):
                if h >= 2:
                    pe.wait_ge(fg_free, h - 1)
                sel = NEGSEL[:, h // 4, h % 4, :]
                mm(BANK[h % 2][:, 0:T], sel, CUM, True, True).then_inc(fg_mm, 1)
            pe.wait_ge(fg_free, 8)

        def qk_norm(s):
            for i, (t, w) in enumerate(s.items):
                pe.wait_ge(qn_sq.sem, s.sq + i + 1)
                mm(B_STAT[0:26, 0:w], head_cols[:, 24 - 2 * t:50 - 2 * t], T1[:, i % 2, 0:w], i == 0, i == 12
                   ).then_inc(qn_sums.sem, 1)
            pe.wait_ge(bias_in.sem, s.bias_in)
            pe.wait_ge(qn_rstd, s.layer + 1)
            for i, (t, w) in enumerate(s.items):
                if i >= 2:
                    pe.wait_ge(qn_out.sem, s.out + i - 1)
                mm(B_T[i % 2][:, 0:w], HEAD_ROWS[:, P * t:P * t + P], RB[0:26, 0:w], True, True).then_inc(qn_mm.sem, 1)
            for r in range(5):
                pe.wait_ge(qn_out.sem, s.out + (1, 6, 7, 8, 9)[r])
                if r >= 2:
                    pe.wait_ge(rope_out.sem, s.ro + r - 1)
                src = QB[:, 3 + r, 0:T] if r else KB[:, 4, 0:T]
                mm(BANK[2 + r % 2][:, 0:T], rotate[:, :], src, True, True).then_inc(rope_mm.sem, 1)
            pe.wait_ge(rope_out.sem, s.ro + 1)
            for kv in range(2):
                mm(BANK[kv][:, :], dup[kv][:, :], KB[:, 4, :], True, True).then_inc(rope_mm.sem, 1)

        def attn(s):
            def pair(at):
                pe.wait_ge(q_staged.sem, at(lambda p: s.q + p + 1))
                for hh in range(2):
                    for qt in range(2):
                        j, nk = 2 * hh + qt, P * s.nblk(qt)
                        pe.wait_ge(exp_done.sem, at(lambda p: s.ex + 4 * p + j - 3))
                        mm(BANK[j][:, 0:nk], QS[HD * hh:HD * hh + HD, P * qt:P * qt + P],
                           KS[HD * hh:HD * hh + HD, 0:nk], True, True).then_inc(scores.sem, 1)
                for jj in range(s.tper):
                    nb = s.nblk(jj % 2)
                    pe.wait_ge(probs.sem, at(lambda p: s.pb + s.tper * p + jj + 1))
                    pe.wait_ge(copied.sem, at(lambda p: s.cp + s.tper * p + jj - 1))
                    for b in range(nb):
                        ins = pe.transpose(B_T[jj % 2][:, P * b:P * b + P], PR[:, jj, P * b:P * b + P],
                                           ident[:, :])
                    ins.then_inc(turned.sem, 1)
                pe.wait_ge(v_staged.sem, at(lambda p: s.v + p + 1))
                pe.wait_ge(copied.sem, at(lambda p: s.cp + s.tper * (p + 1)))
                pe.wait_ge(o_done.sem, at(lambda p: s.o + p))
                for jj in range(s.tper):
                    hh, qt = jj // 2, jj % 2
                    nb = s.nblk(qt)
                    vc = 0 if s.diff or s.vw == HD else HD * hh
                    w = P if s.diff else HD
                    o = B_STAT[:, P * qt:P * qt + P] if s.diff else B_STAT[HD * hh:HD * hh + HD, P * qt:P * qt + P]
                    for b in range(nb):
                        ins = mm(o, VS[:, b, vc:vc + w], PT[:, jj, b, :], b == 0, b == nb - 1)
                ins.then_inc(pv_done.sem, 1)
            each(pe, 0, s.pairs, s.unroll, pair)

        def finish(s):
            pe.wait_ge(x_ready.sem, s.x)
            for b in range(4):
                q, f0 = b // 2, 4 * (b % 2)
                for t in range(4):
                    ins = pe.transpose(BANK[b][:, P * t:P * t + P], X[:, f0 + t, P * q:P * q + P], ident[:, :])
                ins.then_inc(out_mm, 1)

        for s in PLAN:
            if s.kind == "setup":
                setup()
            elif s.kind == "ada":
                for ch in s.chunks:
                    ada(one, lambda _, ch=ch: ch)
                close(s.hosted)
            elif s.kind in ("ln", "rms"):
                stats(s)
            elif s.kind == "qkv":
                qkv(s)
            elif s.kind == "ffn_in":
                ffn_in(s)
            elif s.kind == "proj":
                proj(s)
            elif s.kind == "sub_norm":
                sub_norm()
            elif s.kind == "forget_bias":
                forget_bias(s)
            elif s.kind == "qk_norm":
                qk_norm(s)
            elif s.kind == "attn":
                attn(s)
            elif s.kind == "finish":
                finish(s)

    def ahead(at, f, split, late):
        p = f(at.u)
        if p.g + SPLIT >= len(PIECES):
            return
        if PIECES[p.g + SPLIT].chunk.n - p.chunk.n > RAW:
            late.append(p.g + SPLIT)
        else:
            split(at, lambda s: PIECES[f(s).g + SPLIT])

    @block.scalar
    def _(act):
        chain = Chain(act, act_chain)
        late = list(range(SPLIT))
        one = At(None, 0, 1, 1)

        def split(at, f):
            p = f(at.u)
            ch = p.chunk
            wait_landed(act, at, lambda s: f(s).chunk)
            act.wait_ge(piece_used.sem, at(lambda s: f(s).g + 1))
            act.activation(WH[:, p.g % SPLIT, 0:p.kt * CW].rearrange("p (t n) -> p t n", n=CW),
                           raw_ap(ch.n, ch.kt, CW)[:, p.k0:p.k0 + p.kt, :], ACT.Copy).then_inc(hi_done, 1)

        def flush():
            while late:
                g = late.pop(0)
                split(one, lambda _: PIECES[g])

        def used(at, f):
            act.wait_ge(piece_used.sem, at(lambda s: f(s).g + SPLIT + 1))

        def rows(dst, src):
            act.dma_start(dst, src).then_inc(rows_in, 16)

        def setup():
            rows(ROWS[0][0:8, :], a["c"].rearrange("a (t p) -> (a t) p", p=P))
            rows(ROWS[0][8:16, :], a["c_2"].rearrange("a (t p) -> (a t) p", p=P))
            rows(ROWS[0][16:24, :], a["c_ctx_2"].rearrange("(t p) -> t p", p=P))
            rows(ROWS[0][24:120, :], a["b_ada"].rearrange("l (t p) -> (l t) p", p=P))
            rows(ident[:, :], c["ident"])
            rows(ones[:, :], c["ones"])
            for l in range(2):
                rows(ROWS[1 + l][:, :], a["b_ada_2"][l].rearrange("(t p) -> t p", p=P))
            rows(ROWS[3][0:32, :], a["ln_g"].rearrange("l j (t p) -> (l j t) p", p=P))
            rows(ROWS[3][32:64, :], a["ln_b"].rearrange("l j (t p) -> (l j t) p", p=P))
            rows(ROWS[3][64:112, :], a["norm_g_2"].rearrange("l j (t p) -> (l j t) p", p=P))
            rows(ROWS[4][0:1, :], a["diff_subln_g"])
            for hf in range(2):
                rows(ROWS[4][1:9, hf * HD:(hf + 1) * HD], a["qk_norm_g_2"].rearrange("l j d -> (l j) d"))
            rows(XIN[:, :, :], a["x"].rearrange("a (q p) d -> p (a q) d", p=P))
            rows(CIN[:, :, :], a["ctx_2"].rearrange("a (q p) d -> p (a q) d", p=P))
            for k in range(4):
                act.wait_ge(setup_mm, 2 + k)
                act.activation(X[:, 2 * k:2 * k + 2, 0:T], BANK[1 + k][:, :].rearrange("p (t n) -> p t n", t=2),
                               ACT.Copy).then_inc(setup_act, 1)
            act.wait_ge(cols_done, 1)
            act.activation(SILU_C[:, 0:8], C_COLS[:, 0:8], ACT.Silu)
            pairs = SILU_C[:, 8:24].rearrange("p (t v) -> p t v", v=2)
            for v in range(2):
                ins = act.activation(pairs[:, :, v], C_COLS[:, 8 + 8 * v:16 + 8 * v], ACT.Silu)
            ins.then_inc(silu_done, 1)
            act.wait_ge(lam_sum, 1)
            act.activation(LAM[:, 2:4], LAM[:, 0:2], ACT.Exp).then_inc(lam_exp, 1)

        def stats(s):
            act.wait_ge(x_ready.sem, s.x)
            for t in range(NT):
                if s.kind == "ln":
                    act.wait_ge(centred.sem, s.cen + t + 1)
                act.wait_ge(stat_mm.sem, s.stat + t - 1)
                act.activation(T1[:, t % 2, 0:s.n], X[:, t, 0:s.n], ACT.Square).then_inc(stat_in.sem, 1)
            act.wait_ge(stat_mm.sem, s.stat + NT)
            bank, eps = (B_T[0], EPS[:, 0:1]) if s.kind == "ln" else (B_STAT, EPS[:, 1:2])
            act.activation(RB[:, 0:s.n], bank[:, 0:s.n], ACT.Sqrt, bias=eps, scale=1.0 / D).then_inc(rstd_sq.sem, 1)

        def modulate(s):
            act.wait_ge(ada_out, s.a_out)
            ad = AD[s.ada]

            def tile(at):
                par, t = at.u % 2, at(lambda k: k)
                if s.kind != "mod":
                    act.wait_ge(mod_src.sem, at(lambda k: s.src + k + 1))
                wait_apart(act, h_ready.sem, at(lambda k: s.h + k - 1), act_waited)
                for v in range(s.n // T):
                    cols = slice(v * T, v * T + T)
                    src = T1[:, par, cols] if s.kind == "rms" else \
                        X[:, bass.ds(t, 1), cols].rearrange("p o n -> p (o n)")
                    sc = GS[:, bass.ds(t, 1), v] if s.kind == "rms" else ad[:, bass.ds(at(lambda k: 8 * s.scale + k), 1), v]
                    sh = ad[:, bass.ds(at(lambda k: 8 * s.shift + k), 1), v]
                    ins = act.activation(T2[:, par, cols], src, ACT.Identity, bias=sh, scale=sc)
                ins.then_inc(mod_t2.sem, 1)
            each(act, 0, 8, 2, tile)

        def qkv(s):
            for it in s.items:
                if it.what[0] == "forget":
                    continue
                for p in it.chunk.pieces:
                    ahead(one, lambda _: p, split, late)
                used(one, lambda _: it.chunk.pieces[-1])
                pair, kind, n = PAIR[it.grp.n % 2], it.what[0], it.n
                if kind in "qk":
                    dst, t = (QB if kind == "q" else KB), it.what[1]
                    for j in range(2):
                        ins = act.activation(dst[:, t + j, 0:n], pair[j][:, 0:n], ACT.Copy,
                                             scale=SCALE if s.first and kind == "q" else 1.0)
                elif kind == "v":
                    row = D if s.first else 640
                    v = VB[:, 0:n // P * row].rearrange("p (b n) -> p b n", n=row)
                    for j in range(n // T):
                        ins = act.activation(v[:, 2 * j:2 * j + 2, it.what[1]:it.what[1] + CW],
                                             pair[j][:, :].rearrange("p (b n) -> p b n", b=2), ACT.Copy)
                else:
                    v = VB[:, :].rearrange("p (b n) -> p b n", n=640)
                    act.activation(KB[:, 4, :], pair[0][:, :], ACT.Copy)
                    ins = act.activation(v[:, :, 512:640], pair[1][:, :].rearrange("p (b n) -> p b n", b=4),
                                         ACT.Copy)
                ins.then_inc(ev_act.sem, 1)

        def ffn_in(s):
            n = s.n

            def hidden_hi(at):
                t = at(lambda k: 2 * k)
                wait_apart(act, act32.sem, at(lambda k: s.a32 + k + 1), act_waited)
                act.activation(AH[:, bass.ds(t, 2), 0:n], T2[:, :, 0:n], ACT.Copy).then_inc(act_hi.sem, 1)

            def step(at):
                gg = s.steps[at.u].gg
                for i in range(KC // PIECE):
                    ahead(at, lambda k: s.steps[k].g.pieces[i], split, late)
                used(at, lambda k: s.steps[k].g.pieces[-1])
                act.wait_ge(act32.sem, at(lambda k: s.a32 + k))
                act.activation(T1[:, 0, 0:n], PAIR[gg.n % 2][0][:, 0:n], ACT.Silu)
                act.activation(T1[:, 1, 0:n], PAIR[gg.n % 2][1][:, 0:n], ACT.Silu).then_inc(silu_g.sem, 1)
                act.wait_ge(silu_g.sem, at(lambda k: s.silu + k + 1))
                act.sem_inc(ev_act.sem, 1)
                for i in range(KC // PIECE):
                    ahead(at, lambda k: s.steps[k].u.pieces[i], split, late)
                hidden_hi(at)
            each(act, 0, 10, 1 if s.host else 2, step)
            step(At(None, 10, 1, 1))

        def proj(s):
            for g in s.groups:
                for ch in g.chunks:
                    for p in ch.pieces:
                        ahead(one, lambda _: p, split, late)

        def sub_norm(s):
            act.wait_ge(o_done.sem, s.o_wait)
            for t in range(4):
                if t >= 2:
                    act.wait_ge(sub_mm, t - 1)
                act.activation(T1[:, t % 2, 0:T], OF[:, t, :], ACT.Square).then_inc(sub_sq, 1)
                act.wait_ge(sub_mm, t + 1)
                if t >= 2:
                    act.wait_ge(sub_out, t - 1)
                act.activation(T2[:, t % 2, 0:T], B_T[t % 2][:, 0:T], ACT.Sqrt, bias=EPS[:, 0:1], scale=1.0 / P
                               ).then_inc(sub_rt, 1)

        def forget_bias(s):
            act.wait_ge(o_done.sem, s.o_wait)
            act.wait_ge(forget_used, 1)
            act.activation(FD, B_ADA[0:8, 0:T], ACT.Identity, bias=FB[:, 0:1]).then_inc(fg_x, 1)
            act.wait_ge(fg_abs, 1)
            chain.link(act.activation(FD_ABS, FD_ABS, ACT.Exp, scale=-1.0))
            act.activation(FD_ABS, FD_ABS, ACT.Ln, bias=1.0).then_inc(fg_exp, 1)

        def qk_norm(s):
            act.wait_ge(ev_act.sem, s.q_in)

            for i, (t, w) in enumerate(s.items):
                if i >= 2:
                    act.wait_ge(qn_sums.sem, s.sums + i - 1)
                src = QB[:, t, 0:w] if t < 8 else KB[:, t - 8, 0:w]
                act.activation(T1[:, i % 2, 0:w], src, ACT.Square).then_inc(qn_sq.sem, 1)
            act.wait_ge(qn_sums.sem, s.sums + 13)
            act.activation(RB[0:26, :], B_STAT[0:26, :], ACT.Sqrt, bias=EPS[0:26, 1:2], scale=1.0 / HD
                           ).then_inc(qn_root.sem, 1)

        def attn(s):
            def pair(at):
                for hh in range(2):
                    for qt in range(2):
                        j, nk = 2 * hh + qt, P * s.nblk(qt)
                        back = j % 2 if s.diff else j
                        act.wait_ge(nmax.sem, at(lambda p: s.mx + 4 * p + j + 1))
                        wait_apart(act, turned.sem, at(lambda p: s.tu + s.tper * (p - 1) + back + 1), act_waited)
                        if s.sink:
                            act.activation(ES[:, j:j + 1], SINK[:, bass.ds(at(lambda p: s.sink(p, hh)), 1)],
                                           ACT.Exp, bias=NM[:, j:j + 1]).then_inc(sink_done.sem, 1)
                        act.activation(PR[:, j, 0:nk], BANK[j][:, 0:nk], ACT.Exp, bias=NM[:, j:j + 1],
                                       accum_out=RS[:, j:j + 1]).then_inc(exp_done.sem, 1)
                act.wait_ge(pv_done.sem, at(lambda p: s.pv + p))
                for jj in range(s.tper):
                    nb = s.nblk(jj % 2)
                    act.wait_ge(turned.sem, at(lambda p: s.tu + s.tper * p + jj + 1))
                    act.activation(PT[:, jj, 0:nb, :], B_T[jj % 2][:, 0:P * nb].rearrange("p (b n) -> p b n", n=P),
                                   ACT.Copy).then_inc(copied.sem, 1)
            each(act, 0, s.pairs, s.unroll, pair)

        for s in PLAN:
            if s.kind == "setup":
                setup()
            elif s.kind == "ada":
                flush()
            elif s.kind in ("mod", "ln", "rms"):
                if s.kind != "mod":
                    stats(s)
                if not s.last_ln:
                    modulate(s)
            elif s.kind == "qkv":
                qkv(s)
            elif s.kind == "ffn_in":
                ffn_in(s)
            elif s.kind == "proj":
                proj(s)
            elif s.kind == "sub_norm":
                sub_norm(s)
            elif s.kind == "forget_bias":
                forget_bias(s)
            elif s.kind == "qk_norm":
                qk_norm(s)
            elif s.kind == "attn":
                attn(s)
            elif s.kind == "finish":
                for b in (0, 2):
                    act.wait_ge(out_mm, b + 1)
                    act.activation(OUTR[:, b // 2, 0:512], BANK[b][:, :], ACT.Copy).then_inc(out_cp, 1)

    @block.vector
    def _(dve):
        chain = Chain(dve, dve_chain)
        late = list(range(SPLIT))
        closed = {"at": 0, "read": 0}
        one = At(None, 0, 1, 1)

        def split(at, f):
            p = f(at.u)
            ch = p.chunk
            dve.wait_ge(hi_done, at(lambda s: f(s).g + 1))
            dve.tensor_tensor(WL[:, p.g % SPLIT, 0:p.kt * CW].rearrange("p (t n) -> p t n", n=CW),
                              raw_ap(ch.n, ch.kt, CW)[:, p.k0:p.k0 + p.kt, :],
                              WH[:, p.g % SPLIT, 0:p.kt * CW].rearrange("p (t n) -> p t n", n=CW).bitcast(F32),
                              ALU.subtract).then_inc(lo_done, 1)

        def flush():
            while late:
                g = late.pop(0)
                split(one, lambda _: PIECES[g])

        def used(at, f):
            dve.wait_ge(piece_used.sem, at(lambda s: f(s).g + SPLIT + 1))

        def ada(at, f):
            ch = f(at.u)
            nv = 1 if ch.order[0] < 2 else 2
            if ch.raw_order > closed["at"] + 1:
                columns(at, lambda s: ADA[f(s).raw_order - 2])
            wait_landed(dve, at, f)
            w = raw_ap(ch.n, KC, CW)
            if ch.raw_order >= 2:
                dve.wait_ge(ada_sum, at(lambda s: f(s).raw_order - 1))
            for k in range(KC):
                for v in range(nv):
                    acc = ACC[:, ch.raw_order % 2, v, :]
                    i = k if ch.order[0] < 2 else 8 + 2 * k + v
                    if k == 0:
                        ins = dve.tensor_scalar(acc, w[:, k, :], SILU_C[:, i:i + 1], None, ALU.mult)
                    else:
                        ins = dve.scalar_tensor_tensor(out=acc, in0=w[:, k, :], scalar=SILU_C[:, i:i + 1], in1=acc,
                                                       op0=ALU.mult, op1=ALU.add)
                if k < KC - 1:
                    chain.link(ins)
            ins.then_inc(ada_used, 1)

        def ahead_of(at, f, host=None):
            for i in range(len(f(at.u).pieces)):
                if host and i == len(f(at.u).pieces) - 2:
                    ada(at, host)
                ahead(at, lambda k: f(k).pieces[i], split, late)

        def close(a):
            while closed["read"] < a:
                columns(one, lambda _: ADA[closed["read"]])
            closed["at"] = a

        def columns(at, f):
            ch = f(at.u)
            m = ch.order[0]
            nv = 1 if m < 2 else 2
            bias = (B1 if m < 2 else B2)[:, m % 2, :]
            col = at(lambda s: 2 * f(s).order[1])
            dve.wait_ge(ada_sum, at(lambda s: f(s).raw_order + 1))
            b = bias[:, bass.ds(col, 2)]
            if nv == 2:
                b = b[:, :, None].broadcast_to([P, 2, 2])
                o, i = AD[m][:, bass.ds(col, 2), :], B_ADA[:, 0:4].rearrange("p (c v) -> p c v", v=2)
            else:
                o, i = AD[m][:, bass.ds(col, 2), 0], B_ADA[:, 0:2]
            dve.tensor_tensor(o, i, b, ALU.add).then_inc(ada_out, 1)
            closed["read"] = max(closed["read"], f(at.u + at.unroll * (at.n - 1)).raw_order + 1)

        def setup():
            dve.memset(EPS[:, 0:1], LN_EPS)
            dve.memset(EPS[:, 1:2], NORM_EPS)
            dve.wait_ge(setup_mm, 1)
            at = 0
            b0 = BANK[0]
            dve.tensor_copy(C_COLS[:, :], b0[:, 0:24])
            dve.tensor_copy(B1[:, :, :], b0[:, 24:120].rearrange("p (l n) -> p l n", l=2))
            dve.tensor_copy(B2[:, :, :], b0[:, 120:264].rearrange("p (l n) -> p l n", l=2))
            dve.tensor_copy(G_COLS[:, :], b0[:, 264:376])
            chain.link(dve.tensor_copy(E_COLS[:, :], b0[:, 376:385]))
            for j in (1, 2, 4, 5):
                dve.tensor_scalar(B1[:, :, 8 * j:8 * j + 8], B1[:, :, 8 * j:8 * j + 8], 1.0, None, ALU.add)
            for j in (1, 4, 7):
                dve.tensor_scalar(B2[:, :, 8 * j:8 * j + 8], B2[:, :, 8 * j:8 * j + 8], 1.0, None, ALU.add)
            dve.tensor_scalar(E_COLS[:, 0:1], E_COLS[:, 0:1], 1.0 - LAMBDA_INIT, None, ALU.mult)
            for k in (1, 3, 5, 7):
                ins = dve.tensor_scalar(E_COLS[:, k:k + 1], E_COLS[:, k:k + 1], SCALE, None, ALU.mult)
            chain.link(ins)
            for k in range(4):
                dve.wait_ge(setup_mm, 6 + k)
                b = BANK[5 + k] if k < 3 else BANK[1]
                ins = dve.tensor_copy(X[:, 2 * k:2 * k + 2, T:2 * T], b[:, :].rearrange("p (t n) -> p t n", t=2))
            ins.then_inc(cols_done, 1)
            dve.wait_ge(setup_mm, 10)
            dve.tensor_tensor(T5ROW[:, :], BANK[2][0:N_T5, 0:BIAS_L], T5MASK[:, :], ALU.add).then_inc(t5_rows, 1)
            pairs = LROW[:, :, :].rearrange("p (a b) d -> p a b d", b=2)
            chain.link(dve.tensor_tensor(LPROD[:, :, :], pairs[:, :, 0, :], pairs[:, :, 1, :], ALU.mult))
            dve.tensor_reduce(LAM[:, 0:2], LPROD[:, :, :], AX.X, ALU.add).then_inc(lam_sum, 1)
            dve.wait_ge(lam_exp, 1)
            ins = dve.scalar_tensor_tensor(out=LAM[:, 4:5], in0=LAM[:, 3:4], scalar=LAMBDA_INIT, in1=LAM[:, 2:3],
                                           op0=ALU.subtract, op1=ALU.subtract)
            chain.link(ins)
            dve.sem_inc(region_free, 1)
            dve.wait_ge(setup_act, 4)
            dve.wait_ge(silu_done, 1)

        def flat(ap):
            return ap.rearrange("p o n -> p (o n)")

        def norm(s):
            n, ad = s.n, AD[s.ada]
            rms = s.kind == "rms"
            if rms:
                g = G_COLS[:, s.gain:s.gain + 8][:, :, None].broadcast_to([P, 8, 2])
                chain.link(dve.tensor_tensor(GS[:, :, :], ad[:, 8 * s.scale:8 * s.scale + 8, :], g, ALU.mult))
            if s.kind == "ln":
                dve.wait_ge(mean_mm.sem, s.mean + 1)
                for t in range(NT):
                    dve.scalar_tensor_tensor(out=X[:, t, 0:n], in0=B_STAT[:, 0:n], scalar=-1.0 / D, in1=X[:, t, 0:n],
                                             op0=ALU.mult, op1=ALU.add).then_inc(centred.sem, 1)
                dve.wait_ge(centred.sem, s.cen + NT)
            if s.kind != "mod":
                dve.wait_ge(rstd_sq.sem, s.rstd + 1)
                chain.link(dve.reciprocal(RB[:, 0:n], RB[:, 0:n]))
            linked = s.kind == "ln"

            def tile(at):
                par, t = at.u % 2, at(lambda k: k)
                x = flat(X[:, bass.ds(t, 1), 0:n])
                if s.kind != "mod":
                    if not s.last_ln:
                        dve.wait_ge(mod_t2.sem, at(lambda k: s.t2 + k - 1))
                    ins = dve.tensor_tensor(T1[:, par, 0:n], x, RB[:, 0:n], ALU.mult)
                    if rms:
                        ins.then_inc(mod_src.sem, 1)
                    else:
                        chain.link(ins)
                        ins = dve.tensor_scalar(x, T1[:, par, 0:n],
                                                G_COLS[:, bass.ds(at(lambda k: s.gain + k), 1)],
                                                G_COLS[:, bass.ds(at(lambda k: s.gain_b + k), 1)], ALU.mult, ALU.add)
                        if s.last_ln:
                            return
                        ins.then_inc(mod_src.sem, 1)
                    dve.wait_ge(mod_src.sem, at(lambda k: s.src + k + 1))
                for v in range(n // T):
                    cols = slice(v * T, v * T + T)
                    src = T1[:, par, cols] if rms else flat(X[:, bass.ds(t, 1), cols])
                    sc = GS[:, bass.ds(t, 1), v] if rms else ad[:, bass.ds(at(lambda k: 8 * s.scale + k), 1), v]
                    sh = ad[:, bass.ds(at(lambda k: 8 * s.shift + k), 1), v]
                    ins = dve.tensor_scalar(flat(HH[:, bass.ds(t, 1), cols]), src, sc, sh, ALU.mult, ALU.add)
                ins.then_inc(mod_hi.sem, 1)
            each(dve, 0, 8, 2, tile, chain if linked else None, 2)
            if s.kind == "ln":
                dve.drain().then_inc(x_ready.sem, 1)

        def ffn_in(s):
            n = s.n

            def step(at):
                ahead_of(at, lambda k: s.steps[k].g, (lambda k: s.steps[k].hosts[0]) if s.host else None)
                ahead_of(at, lambda k: s.steps[k].u, (lambda k: s.steps[k].hosts[1]) if s.host else None)
                used(at, lambda k: s.steps[k].u.pieces[-1])
                dve.wait_ge(silu_g.sem, at(lambda k: s.silu + k + 1))
                dve.wait_ge(act_ready.sem, at(lambda k: s.ready + k))
                pair = PAIR[s.steps[at.u].ug.n % 2]
                for j in range(2):
                    ins = dve.tensor_tensor(T2[:, j, 0:n], T1[:, j, 0:n], pair[j][:, 0:n], ALU.mult)
                ins.then_inc(act32.sem, 1)
                dve.wait_ge(act32.sem, at(lambda k: s.a32 + k + 1))
                dve.sem_inc(ev_dve.sem, 1)
            if s.host:
                step(At(None, 0, 1, 1))
                each(dve, 1, 10, 1, step, chain, 2 * (KC - 1))
            else:
                each(dve, 0, 10, 2, step)
            step(At(None, 10, 1, 1))
            close(s.hosted)

        def proj(s):
            n, ad = s.n, AD[s.ada]
            for m, g in enumerate(s.groups):
                for ch in g.chunks:
                    ahead_of(one, lambda _: ch, (lambda _: g.host) if g.host and ch is g.chunks[-1] else None)
                used(one, lambda _: g.chunks[-1].pieces[-1])
                pair = PAIR[g.grp.n % 2]
                if m == 0 and s.half:
                    chain.link(dve.tensor_scalar(GS[:, :, :], ad[:, 8 * s.gate:8 * s.gate + 8, :], 0.5, None, ALU.mult))
                if s.first:
                    for j in range(2):
                        t = 2 * m + j
                        ins = dve.tensor_scalar(T2[:, j, 0:n], pair[j][:, 0:n], ad[:, 8 * s.gate + t, :], None, ALU.mult)
                    chain.link(ins)
                    ins = dve.scalar_tensor_tensor(out=X[:, 2 * m:2 * m + 2, 0:n], in0=X[:, 2 * m:2 * m + 2, 0:n],
                                                   scalar=ALPHA, in1=T2[:, :, 0:n], op0=ALU.mult, op1=ALU.add)
                else:
                    for j in range(2):
                        t = 2 * m + j
                        for v in range(n // T):
                            cols = slice(v * T, v * T + T)
                            gate = GS[:, t, v:v + 1] if s.half else ad[:, 8 * s.gate + t, v:v + 1]
                            ins = dve.scalar_tensor_tensor(out=X[:, t, cols], in0=pair[j][:, cols], scalar=gate,
                                                           in1=X[:, t, cols], op0=ALU.mult, op1=ALU.add)
                chain.link(ins)
                dve.sem_inc(g.grp.tally.sem, 1)
            dve.sem_inc(x_ready.sem, 1)
            close(s.hosted)

        def sub_norm():
            for t in range(4):
                dve.wait_ge(sub_rt, t + 1)
                o, r = OF[:, t, :], T2[:, t % 2, 0:T]
                chain.link(dve.reciprocal(r, r))
                chain.link(dve.scalar_tensor_tensor(out=o, in0=o, scalar=E_COLS[:, 0:1], in1=r, op0=ALU.mult,
                                                    op1=ALU.mult))
                chain.link(dve.tensor_copy(HH[:, t, 0:T], o))
                dve.tensor_tensor(HL[:, t, 0:T], o, HH[:, t, 0:T].bitcast(F32), ALU.subtract).then_inc(sub_out, 1)

        def forget_bias(s):
            dve.wait_ge(fg_x, 1)
            dve.scalar_tensor_tensor(out=FD_ABS, in0=FD, scalar=-1.0, in1=FD, op0=ALU.mult, op1=ALU.max
                                     ).then_inc(fg_abs, 1)
            dve.tensor_scalar(FD_MIN, FD, 0.0, None, ALU.min)
            dve.memset(FD_ONE, 1.0)
            dve.wait_ge(fg_exp, 1)
            chain.link(dve.drain())
            chain.link(dve.tensor_tensor(FD_MIN, FD_MIN, FD_ABS, ALU.subtract))
            dve.tensor_tensor_scan(CUM, FD_ONE.rearrange("p a b -> p (a b)"), FD_MIN, 0.0, ALU.mult, ALU.add
                                   ).then_inc(fg_cum, 1)
            dve.wait_ge(fg_mm, 1)
            chain.link(dve.tensor_copy(CUMT[:, :, :], B_T[0][:, 0:16].rearrange("p (q h) -> p q h", q=2)))
            dve.wait_ge(bias_in.sem, s.bias_in)
            for h in range(8):
                dve.wait_ge(fg_mm, h + 2)
                for q in range(2):
                    nk = P * (q + 1)
                    ins = dve.scalar_tensor_tensor(out=BT[:, 512 * h + T * q:512 * h + T * q + nk],
                                                   in0=BANK[h % 2][:, 0:nk], scalar=CUMT[:, q, h:h + 1],
                                                   in1=CAUSAL[:, T - nk:T], op0=ALU.add, op1=ALU.add)
                ins.then_inc(fg_free, 1)
            dve.wait_ge(fg_free, 8)

        def qk_norm(s):
            dve.wait_ge(bias_in.sem, s.bias_in)
            blocks = BT[:, :].rearrange("p (b k) -> p b k", k=T)
            chain.link(dve.tensor_tensor(blocks, blocks, NEIGH[:, None, :].broadcast_to([P, 16, T]), ALU.add))

            dve.wait_ge(qn_root.sem, s.root + 1)
            dve.reciprocal(RB[0:26, :], RB[0:26, :]).then_inc(qn_rstd, 1)
            for i, (t, w) in enumerate(s.items):
                x = QB[:, t, 0:w] if t < 8 else KB[:, t - 8, 0:w]
                k = 1 + 4 * s.layer + (0 if t < 4 else 2 if t < 8 else 1 if t < 12 else 3)
                dve.wait_ge(qn_mm.sem, s.mm + i + 1)
                dve.scalar_tensor_tensor(out=x, in0=x, scalar=E_COLS[:, k:k + 1], in1=B_T[i % 2][:, 0:w],
                                         op0=ALU.mult, op1=ALU.mult).then_inc(qn_out.sem, 1)
            dve.wait_ge(qn_out.sem, s.out + 13)
            for r in range(5):
                x = QB[:, 3 + r, 0:T] if r else KB[:, 4, 0:T]
                dve.wait_ge(rope_mm.sem, s.rmm + r + 1)
                dve.tensor_tensor(T1[:, r % 2, 0:T], BANK[2 + r % 2][:, 0:T], SIN[:, :], ALU.mult)
                chain.link(dve.tensor_tensor(x, x, COS[:, :], ALU.mult))
                dve.tensor_tensor(x, x, T1[:, r % 2, 0:T], ALU.add).then_inc(rope_out.sem, 1)
            for kv in range(2):
                dve.wait_ge(rope_mm.sem, s.rmm + 6 + kv)
                dve.tensor_copy(KB[:, 5 + kv, :], BANK[kv][:, :]).then_inc(rope_out.sem, 1)

        def attn(s):
            dve.wait_ge(bias_in.sem, s.bias_in)
            links = 0

            def pair(at):
                k0 = chain.k
                for hh in range(2):
                    for qt in range(2):
                        j, nk = 2 * hh + qt, P * s.nblk(qt)
                        dve.wait_ge(scores.sem, at(lambda p: s.sc + 4 * p + j + 1))
                        if s.bias:
                            where, _, w = s.bias(at.u, hh, qt)
                            b = WINDOW[:, qt, :] if where == "window" else \
                                BT[:, bass.ds(at(lambda p: s.bias(p, hh, qt)[1]), w)]
                            chain.link(dve.tensor_tensor(BANK[j][:, 0:w], BANK[j][:, 0:w], b, ALU.add))
                        ins = dve.tensor_reduce(NM[:, j:j + 1], BANK[j][:, 0:nk], AX.X, ALU.max, negate=True)
                        if s.sink:
                            chain.link(ins)
                            col = SINK[:, bass.ds(at(lambda p: s.sink(p, hh)), 1)]
                            ins = dve.scalar_tensor_tensor(out=NM[:, j:j + 1], in0=col, scalar=-1.0,
                                                           in1=NM[:, j:j + 1], op0=ALU.mult, op1=ALU.min)
                        ins.then_inc(nmax.sem, 1)
                for hh in range(2):
                    for qt in range(2):
                        j, nk = 2 * hh + qt, P * s.nblk(qt)
                        if s.diff and hh == 0:
                            continue
                        for jj in ((qt, j) if s.diff else (j,)):
                            dve.wait_ge(exp_done.sem, at(lambda p: s.ex + 4 * p + jj + 1))
                            if s.sink:
                                dve.wait_ge(sink_done.sem, at(lambda p: s.sk + 4 * p + jj + 1))
                                chain.link(dve.tensor_tensor(RS[:, jj:jj + 1], RS[:, jj:jj + 1], ES[:, jj:jj + 1],
                                                             ALU.add))
                            chain.link(dve.reciprocal(RI[:, jj:jj + 1], RS[:, jj:jj + 1]))
                        p1 = PR[:, j, 0:nk]
                        if s.diff:
                            p0 = PR[:, qt, 0:nk]
                            chain.link(dve.tensor_scalar(p1, p1, RI[:, j:j + 1], LAM[:, 4:5], ALU.mult, ALU.mult))
                            ins = dve.scalar_tensor_tensor(out=p0, in0=p0, scalar=RI[:, qt:qt + 1], in1=p1,
                                                           op0=ALU.mult, op1=ALU.add)
                        else:
                            ins = dve.tensor_scalar(p1, p1, RI[:, j:j + 1], None, ALU.mult)
                        ins.then_inc(probs.sem, 1)
                dve.wait_ge(pv_done.sem, at(lambda p: s.pv + p + 1))
                if s.diff:
                    dve.tensor_copy(OF[:, at.u, :] if at.reg is None else
                                    flat(OF[:, bass.ds(at(lambda p: p), 1), :]), B_STAT[:, 0:T]
                                    ).then_inc(o_done.sem, 1)
                else:
                    t = at(s.out)
                    hi = flat(HH[:, bass.ds(t, 1), s.qoff:s.qoff + T])
                    lo = flat(HL[:, bass.ds(t, 1), s.qoff:s.qoff + T])
                    chain.link(dve.tensor_copy(hi, B_STAT[:, 0:T]))
                    dve.tensor_tensor(lo, B_STAT[:, 0:T], hi.bitcast(F32), ALU.subtract).then_inc(o_done.sem, 1)
            per = (4 if s.bias else 0) + (4 if s.sink else 0) + 4 + (4 if s.sink else 0) + (2 if s.diff else 1)
            each(dve, 0, s.pairs, s.unroll, pair, chain, per * s.unroll)

        for s in PLAN:
            if s.kind == "setup":
                setup()
            elif s.kind == "ada":
                for ch in s.chunks:
                    ada(one, lambda _, ch=ch: ch)
                close(s.hosted)
                flush()
            elif s.kind in ("mod", "ln", "rms"):
                dve.wait_ge(ada_out, s.a_out)
                norm(s)
            elif s.kind == "qkv":
                for it in s.items:
                    ahead_of(one, lambda _: it.chunk, (lambda _: it.host) if it.host else None)
                    if it is s.items[-2] and s.items[-1].grp is None:
                        close(s.hosted)
                close(s.hosted)
            elif s.kind == "ffn_in":
                ffn_in(s)
            elif s.kind == "proj":
                proj(s)
            elif s.kind == "sub_norm":
                sub_norm()
            elif s.kind == "forget_bias":
                forget_bias(s)
            elif s.kind == "qk_norm":
                qk_norm(s)
            elif s.kind == "attn":
                attn(s)
            elif s.kind == "finish":
                for b in (1, 3):
                    dve.wait_ge(out_mm, b + 1)
                    dve.tensor_copy(OUTR[:, b // 2, 512:1024], BANK[b][:, :]).then_inc(out_cp, 1)


_INS = ["x", "c", "rel_bias", "w_ada", "b_ada", "ln_g", "ln_b", "w_in_ab", "diff_lambda", "diff_subln_g",
        "w_in_cd", "forget_b", "w_o", "w_ffn_in", "w_ffn_out", "c_2", "ctx_2", "c_ctx_2", "w_ada_2", "b_ada_2",
        "norm_g_2", "w_ffn_up_2", "w_ffn_down_2", "w_in_2", "w_out_2", "qk_norm_g_2", "na_rpb_2", "wa_sink_2"]


def kernel(**inputs):
    import concourse.bacc as _bacc
    from concourse.bass_utils import run_bass_kernel_spmd as _run

    nc = _bacc.Bacc("TRN2", target_bir_lowering=False, num_devices=1)
    arrays, a, c = {}, {}, {}
    for name in _INS:
        v = np.ascontiguousarray(inputs[name])
        arrays[f"in_{name}_dram"] = v
        a[name] = nc.dram_tensor(f"in_{name}_dram", v.shape, mybir.dt.from_np(v.dtype), kind="ExternalInput").ap()
    for name, v in shape_constants().items():
        v = np.ascontiguousarray(v, dtype=np.float32)
        arrays[f"const_{name}_dram"] = v
        c[name] = nc.dram_tensor(f"const_{name}_dram", v.shape, F32, kind="ExternalInput").ap()
    out = nc.dram_tensor("out_0_dram", (1, T, D), F32, kind="ExternalOutput").ap()
    build(nc, a, c, out)
    r = _run(nc, [arrays], core_ids=[0])
    return r.results[0]["out_0_dram"]
```

```python
from contextlib import ExitStack

import numpy as np

import concourse.bass as bass
from concourse import mybir

F32 = mybir.dt.float32
F32R = mybir.dt.float32r
ALU = mybir.AluOpType
ACT = mybir.ActivationFunctionType
AX = mybir.AxisListType

P = 128
D = 1024
NT = D // P
T = 256
DFF = 2816
NF = DFF // P
DEPTH = 2
HD = 64
CW = 256
KC = 8
PIECE = 2
SPLIT = 4
RAW = 4
ALPHA = (2 * DEPTH) ** 0.25
LN_EPS, NORM_EPS = 1e-5, 1e-6
SCALE = HD ** -0.5
LAMBDA_INIT = 0.8 - 0.6
NA_H = 8
RPB_H, RPB_W = 15, 31
NEG = -1e30
BIAS_L = 384
N_T5 = 20
NA_ROWS, NA_WIDTH = 7, 128


def shape_constants():
    f = np.float32
    c = {}
    c["ident"] = np.eye(P, dtype=f)
    c["ones"] = np.ones((P, P), f)
    half = np.arange(P) // HD
    c["head_cols"] = (half[:, None] + 24 == np.arange(50)[None, :]).astype(f)
    c["head_rows"] = (np.arange(26)[:, None] == (2 * np.arange(13)[:, None] + half[None, :]).reshape(1, -1)).astype(f)
    for kv in range(2):
        m = np.zeros((P, P), f)
        m[kv * HD + np.arange(P) % HD, np.arange(P)] = 1
        c[f"dup{kv}"] = m
    quarter = (np.arange(P) // 16) % 2
    m = np.zeros((P, P), f)
    for o in range(P):
        m[o + 16 if quarter[o] == 0 else o - 16, o] = -1 if quarter[o] == 0 else 1
    c["rotate"] = m
    inv = (f(10000.0) ** (-np.arange(0, 32, 2, dtype=f) / f(32))).astype(f)
    t = np.arange(T)
    pos = np.stack([(t // 64).astype(f), (t % 64).astype(f)])
    axis = (np.arange(P) // 32) % 2
    ang = (pos[axis] * inv[np.arange(P) % 16][:, None]).astype(f)
    c["cos"], c["sin"] = np.cos(ang).astype(f), np.sin(ang).astype(f)
    d = 255 - np.arange(BIAS_L)
    n = np.maximum(d, 0)
    nf = np.maximum(n, 1).astype(f)
    large = 16 + (np.log(nf / f(16)) / f(np.log(8.0)) * f(16)).astype(np.int32)
    bucket = np.where(n < 16, n, np.minimum(large, 31))
    c["bucket_onehot"] = (np.arange(32)[:, None] == bucket[None, :]).astype(f)
    count = (d <= 128).astype(int) + (d % 4 == 0) + (d % 16 == 0)
    dil = np.where((d >= 0) & (count > 0), np.log(np.maximum(count, 1)), NEG).astype(f)
    causal = np.where(d >= 0, 0, NEG).astype(f)
    c["t5_mask"] = np.stack([causal] * 4 + [dil] * 8 + [causal] * 8).astype(f)
    i, j = np.arange(P)[:, None], np.arange(T)[None, :]
    c["causal"] = np.where(P + i - j >= 0, 0, NEG).astype(f)
    col, kcol = (i % 64), (j % 64)
    c0 = np.clip(col - 8, 0, 48)
    c["neighbour"] = np.where((kcol >= c0) & (kcol < c0 + 16), 0, NEG).astype(f)
    c["window"] = np.concatenate([np.where(np.abs(P * q + i - j) <= 128, 0, NEG) for q in range(2)],
                                 axis=1).astype(f)
    neg = np.zeros((8, 8, P), f)
    for h in range(8):
        neg[h, h] = -1
    c["neg_select"] = neg.reshape(8, 8 * P)
    return c


class Tally:

    def __init__(self, sem, credit=0):
        self.sem, self.total, self.credit = sem, credit, credit

    def take(self, n):
        at = self.total
        self.total += n
        return at


class At:

    def __init__(self, reg, u, unroll, n):
        self.reg, self.u, self.unroll, self.n = reg, u, unroll, n

    def __call__(self, f):
        first = f(self.u)
        if self.reg is None:
            return first
        steps = [f(self.u + self.unroll * k) for k in range(self.n)]
        by = steps[1] - steps[0]
        assert all(b - a == by for a, b in zip(steps, steps[1:])), steps
        return self.reg * by + first if by else first


def each(eng, lo, hi, unroll, body, chain=None, links=0):
    n = (hi - lo) // unroll
    if n < 2:
        for s in range(lo, hi):
            body(At(None, s, 1, 1))
        return
    with eng.Fori(0, n) as reg:
        if chain:
            chain.enter(reg, links)
        for u in range(unroll):
            body(At(reg, lo + u, unroll, n))
        if chain:
            chain.leave(n)
    for s in range(lo + n * unroll, hi):
        body(At(None, s, 1, 1))


class Chain:

    def __init__(self, eng, sem):
        self.eng, self.sem, self.k, self.reg, self.per = eng, sem, 0, None, 0

    def enter(self, reg, per):
        self.reg, self.per, self.start = reg, per, self.k

    def leave(self, n):
        assert self.k - self.start == self.per, (self.k - self.start, self.per)
        self.k, self.reg = self.start + n * self.per, None

    def mark(self, ins):
        self.k += 1
        ins.then_inc(self.sem, 1)
        return self.k

    def wait(self, k):
        self.eng.wait_ge(self.sem, self.reg * self.per + k if self.reg is not None else k)

    def link(self, ins):
        self.wait(self.mark(ins))


class Chunk:
    def __init__(self, n, kind, weight, k0, kt, c0, cw, order):
        self.n, self.kind, self.weight = n, kind, weight
        self.k0, self.kt, self.c0, self.cw, self.order = k0, kt, c0, cw, order
        self.pieces = []


class Piece:
    def __init__(self, g, chunk, k0, kt):
        self.g, self.chunk, self.k0, self.kt = g, chunk, k0, kt


class Stage:

    def __init__(self, kind, *, ada=None, bias=None, bias_in=None, chunks=None, diff=None,
                 first=None, gain=None, gain_b=None, gate=None, groups=None, h_wait=None, half=None, hidden=None,
                 hi=None, host=None, items=None, koff=None, ktile=None, last_ln=None, layer=None, hosted=None,
                 mm=None, n=None, name=None, nblk=None, need=None, normed=None, o_wait=None, out=None, pairs=None,
                 q_in=None, qoff=None, qtile=None, ready=None, rmm=None, ro=None, root=None, rows=None, sums=None, scale=None,
                 shift=None, silu=None, sink=None, sq=None, steps=None, take=None, unroll=None, vblk=None,
                 vcol=None, vrow=None, vw=None, what=None, x=None, x_out=None, a32=None):
        self.kind, self.ada, self.bias, self.bias_in = kind, ada, bias, bias_in
        self.chunks, self.diff, self.first, self.gain, self.gain_b = chunks, diff, first, gain, gain_b
        self.gate, self.groups, self.h_wait, self.half, self.hidden = gate, groups, h_wait, half, hidden
        self.hi, self.host, self.items, self.koff, self.ktile = hi, host, items, koff, ktile
        self.last_ln, self.layer, self.hosted, self.mm, self.n = last_ln, layer, hosted, mm, n
        self.name, self.nblk, self.need, self.normed, self.o_wait, self.out = name, nblk, need, normed, o_wait, out
        self.pairs, self.q_in, self.qoff, self.qtile, self.ready = pairs, q_in, qoff, qtile, ready
        self.rmm, self.ro, self.root, self.rows, self.sums, self.scale = rmm, ro, root, rows, sums, scale
        self.shift, self.silu, self.sink, self.sq, self.steps = shift, silu, sink, sq, steps
        self.take, self.unroll, self.vblk, self.vcol, self.vrow = take, unroll, vblk, vcol, vrow
        self.vw, self.what, self.x, self.x_out, self.a32 = vw, what, x, x_out, a32


class Group:

    def __init__(self, n, tally, done):
        self.n, self.tally, self.done = n, tally, done


class Item:

    def __init__(self, what, chunk, grp, host, n):
        self.what, self.chunk, self.grp, self.host, self.n = what, chunk, grp, host, n


class Rows:

    def __init__(self, chunks, host, grp):
        self.chunks, self.host, self.grp = chunks, host, grp


class Step:

    def __init__(self, g, u, host, gg, ug):
        self.g, self.u, self.host, self.gg, self.ug = g, u, host, gg, ug


def build(nc, a, c, out):
    ctx = ExitStack()
    with ctx:
        _build(nc, ctx, a, c, out)


def _build(nc, ctx, a, c, out):
    def sem(name):
        return ctx.enter_context(nc.semaphore(name))

    def sb(name, shape, dt=F32):
        return ctx.enter_context(nc.sbuf_tensor(name, shape, dt))

    X = sb("X", [P, NT, 2 * T])
    HH = sb("H_hi", [P, NT, 2 * T], F32R)
    HL = sb("H_lo", [P, NT, 2 * T], F32R)
    RAWS = sb("raw_weights", [P, RAW, KC * CW])
    WH = sb("weight_hi", [P, SPLIT, PIECE * CW], F32R)
    WL = sb("weight_lo", [P, SPLIT, PIECE * CW], F32R)
    T1 = sb("tmp1", [P, 2, 2 * T])
    T2 = sb("tmp2", [P, 2, 2 * T])
    RB = sb("rstd", [P, 2 * T])
    ident = sb("ident", [P, P])
    ones = sb("ones", [P, P])
    head_cols = sb("head_cols", [P, 50])
    rotate = sb("rotate", [P, P])
    dup = [sb(f"dup{k}", [P, P]) for k in range(2)]
    SILU_C = sb("silu_c", [P, 24])
    C_COLS = sb("c_cols", [P, 24])
    B1 = sb("b_ada_cols", [P, 2, 48])
    B2 = sb("b_ada2_cols", [P, 2, 72])
    G_COLS = sb("gain_cols", [P, 112])
    E_COLS = sb("head_gain_cols", [P, 9])
    AD = [sb("ada0", [P, 48, 1]), sb("ada1", [P, 48, 1]), sb("ada2", [P, 72, 2]), sb("ada3", [P, 72, 2])]
    GS = sb("gain_scale", [P, NT, 2])
    ACC = sb("ada_partial", [P, 2, 2, CW])
    EPS = sb("eps", [P, 2])
    SINK = sb("sink", [P, 16])
    LAM = sb("lam", [P, 8])
    FB = sb("forget_bias", [8, 1])
    NM = sb("neg_max", [P, 4])
    RS = sb("row_sum", [P, 4])
    ES = sb("sink_exp", [P, 4])
    RI = sb("row_scale", [P, 4])
    CUMT = sb("cum_cols", [P, 2, 8])

    base = (nc.sbuf_base + 63) // 64 * 64
    used = {"at": base}

    def region(name, shape, dt=F32, at=None):
        size = 4 * int(np.prod(shape[1:]))
        if at is None:
            at = used["at"]
            used["at"] = at + (size + 31) // 32 * 32
        return nc.alloc_sbuf_tensor_at(name, shape, dt, offset=at)

    AH = region("hidden_hi", [P, NF, 2 * T], F32R)
    AL = region("hidden_lo", [P, NF, 2 * T], F32R)
    used["at"] = base
    QB = region("q", [P, 8, 2 * T])
    KB = region("k", [P, 8, 2 * T])
    VB = region("v", [P, 4 * 640])
    PR = region("probs", [P, 4, 512])
    PT = region("probs_turned", [P, 4, 4, P])
    BT = region("bias", [P, 4096])
    OF = region("o_diff", [P, 4, T])
    QS = region("q_pair", [P, T])
    KS = region("k_pair", [P, 2 * T])
    VS = region("v_pair", [P, 4, P])
    COS = region("cos", [P, T])
    SIN = region("sin", [P, T])
    CAUSAL = region("causal", [P, T])
    NEIGH = region("neighbour", [P, T])
    WINDOW = region("window", [P, 2, T])
    assert used["at"] <= nc.sbuf_usable_end and base + 2 * NF * 2 * T * 4 <= nc.sbuf_usable_end
    used["at"] = base
    XIN = region("x_rows", [P, 2, D])
    CIN = region("ctx_rows", [P, 2, D])
    ROWS = [region(f"rows{k}", [n, P]) for k, n in enumerate((120, 72, 72, 112, 9))]
    ONEHOT = region("onehot", [32, BIAS_L])
    TABLE = region("table", [32, N_T5])
    T5MASK = region("t5_mask", [N_T5, BIAS_L])
    T5ROW = region("t5_rows", [N_T5, BIAS_L])
    RPB = region("rpb_rows", [NA_H, 2, NA_ROWS, NA_WIDTH])
    LROW = region("lambda_rows", [P, 4, HD])
    LPROD = region("lambda_prod", [P, 2, HD])
    assert used["at"] <= nc.sbuf_usable_end
    OUTR = XIN
    HEAD_ROWS = PR[0:26, :, :].rearrange("p j n -> p (j n)")
    FD = PR[0:8, 0, 0:T]
    FD_ABS = PR[0:8, 0, T:2 * T]
    FD_MIN = PR[0:8, 1, 0:T]
    CUM = PR[0:8, 1, T:2 * T]
    FD_ONE = PT[0:8, 0, 0:2, :]
    NEGSEL = PT[0:8, 1:3, :, :]

    BANK = [ctx.enter_context(nc.psum_tensor(f"bank{b}", [P, 512], F32)) for b in range(8)]
    PAIR = [(BANK[0], BANK[1]), (BANK[2], BANK[3])]
    B_T, B_STAT, B_ADA = (BANK[4], BANK[5]), BANK[6], BANK[7]

    t5_dram = nc.dram_tensor("t5_skew", (N_T5, P, BIAS_L), F32, kind="Internal").ap()
    na_dram = nc.dram_tensor("na_skew", (2, NA_H, 64, NA_ROWS * NA_WIDTH), F32, kind="Internal").ap()

    landed = [sem(f"chunk_landed{i}") for i in range(RAW)]
    hi_done = sem("hi_done")
    lo_done = (sem("lo_done_even"), sem("lo_done_odd"))
    piece_used = Tally(sem("piece_used"), SPLIT)
    ada_used, ada_sum, ada_out = sem("ada_used"), sem("ada_sum"), sem("ada_out")
    forget_used = sem("forget_chunk_used")
    ev_act, ev_dve = Tally(sem("evac_act"), 2), Tally(sem("evac_dve"), 2)
    const_in, rows_in, setup_mm = sem("const_in"), sem("rows_in"), sem("setup_mm")
    tokens_in = sem("tokens_in")
    TURN_BANKS = (3, 4, 5, 6, 1, 0, 3, 4)
    setup_act, t5_rows, region_free = sem("x_turned"), sem("t5_rows_ready"), sem("lambda_done")
    skew_out, skew_src = sem("skew_out"), sem("skew_src")
    silu_done, cols_done = sem("silu_done"), sem("cols_done")
    lam_sum, lam_exp = sem("lambda_sums"), sem("lambda_exp")
    h_ready = Tally(sem("h_ready"), 2)
    mod_src, mod_hi, mod_t2 = Tally(sem("mod_src")), Tally(sem("mod_hi")), Tally(sem("mod_t2"), 2)
    centred = Tally(sem("centred"))
    stat_in, stat_mm = Tally(sem("stat_in")), Tally(sem("stat_mm"), 2)
    rstd_sq, mean_mm, x_ready = Tally(sem("rstd_sqrt")), Tally(sem("mean_mm")), Tally(sem("x_ready"))
    silu_g, act32, act_hi = Tally(sem("silu_g")), Tally(sem("act32"), 1), Tally(sem("act_hi"))
    act_ready = Tally(sem("act_ready"), 1)
    bias_in = Tally(sem("bias_in"))
    fg_x, fg_abs, fg_exp = sem("forget_logit"), sem("forget_abs"), sem("forget_exp")
    fg_cum, fg_sel, fg_mm, fg_free = sem("forget_cum"), sem("forget_select"), sem("forget_mm"), sem("forget_free")
    qn_sq, qn_sums, qn_root = Tally(sem("qknorm_sq")), Tally(sem("qknorm_sums")), Tally(sem("qknorm_root"))
    qn_mm, qn_out, qn_rstd = Tally(sem("qknorm_spread")), Tally(sem("qknorm_out")), sem("qknorm_rstd")
    rope_mm, rope_out = Tally(sem("rope_mm")), Tally(sem("rope_out"))
    q_staged, v_staged = Tally(sem("q_staged")), Tally(sem("v_staged"))
    scores, nmax = Tally(sem("scores"), 4), Tally(sem("neg_max_ready"))
    sink_done = Tally(sem("sink_exp_done"))
    exp_done, probs = Tally(sem("exp_done"), 4), Tally(sem("probs_ready"))
    turned, copied = Tally(sem("probs_turned"), 4), Tally(sem("turned_copied"), 2)
    pv_done, o_done = Tally(sem("pv_done"), 1), Tally(sem("o_done"), 1)
    sub_sq, sub_mm, sub_rt, sub_out = sem("sub_sq"), sem("sub_mm"), sem("sub_root"), sem("sub_out")
    dve_chain, act_chain, pool_chain = sem("dve_chain"), sem("act_chain"), sem("pool_chain")
    out_mm, out_cp, out_dma = sem("out_mm"), sem("out_cp"), sem("out_dma")
    credited = [piece_used, ev_act, ev_dve, h_ready, mod_t2, act32, stat_mm, act_ready,
                 scores, exp_done, turned, copied, pv_done, o_done]

    CHUNKS, PIECES, GROUPS, ADA = [], [], [], []
    W = {"ada": [a["w_ada"][0], a["w_ada"][1], a["w_ada_2"][0], a["w_ada_2"][1]]}
    counts = {"a": 0, "f": 0}

    def view(w):
        return w.rearrange("(t p) n -> p t n", p=P)

    def chunk(kind, w, k0, kt, c0, cw=CW, order=None):
        ch = Chunk(len(CHUNKS), kind, w, k0, kt, c0, cw, order)
        CHUNKS.append(ch)
        if kind == "g":
            for k in range(0, kt, PIECE):
                pc = Piece(len(PIECES), ch, k, min(PIECE, kt - k))
                PIECES.append(pc)
                ch.pieces.append(pc)
        else:
            ch.raw_order = counts[kind]
            counts[kind] += 1
        return ch

    def group(engine):
        tally = ev_act if engine == "act" else ev_dve
        g = Group(n=len(GROUPS), tally=tally, done=tally.take(1) + 1)
        GROUPS.append(g)
        return g

    ada_at = {"m": 0, "c": 0}
    ADA_CHUNKS = [24, 24, 36, 36]

    def ada_chunk():
        m, k = ada_at["m"], ada_at["c"]
        ch = chunk("a", view(W["ada"][m]), 0, KC, CW * k, order=(m, k))
        ADA.append(ch)
        ada_at["c"] += 1
        if ada_at["c"] == ADA_CHUNKS[m]:
            ada_at.update(m=m + 1, c=0)
        return ch

    PLAN = []
    state = {"q_in": 0, "normed": None}
    def add(kind, **k):
        now = dict(h_wait=h_ready.total, o_wait=o_done.total, x=x_ready.total,
                   bias_in=bias_in.total, last_ln=False)
        PLAN.append(Stage(kind, **{**now, **k}))
        return PLAN[-1]

    def ada_run(n):
        add("ada", chunks=[ada_chunk() for _ in range(n)], hosted=len(ADA))

    def need(ada, last):
        n = sum(ADA_CHUNKS[:ada]) + D // CW * (last + 1)
        assert n <= len(ADA), (n, len(ADA))
        return n

    def mod(kind, ada, shift, scale, n, gain=None, gain_b=None, last_ln=False):
        s = add(kind, ada=ada, shift=shift, scale=scale, n=n, gain=gain, gain_b=gain_b, last_ln=last_ln,
                need=None if last_ln else need(ada, max(shift, scale)))
        if kind != "mod":
            s.x = x_ready.total
            s.stat_in, s.stat = stat_in.take(8), stat_mm.take(8)
            s.rstd = rstd_sq.take(1)
            if kind == "ln":
                s.mean, s.cen = mean_mm.take(1), centred.take(8)
        if kind == "ln":
            s.x_out = x_ready.take(1)
        if not last_ln:
            s.src = mod_src.take(8) if kind != "mod" else None
            s.hi, s.t2, s.h = (t.take(8) for t in (mod_hi, mod_t2, h_ready))

    def ffn(w_in, w_out, n, ada, gate, half, hosted, first):
        steps, host = [], hosted
        for s in range(NF // 2):
            g = chunk("g", view(w_in), 0, KC, CW * s)
            a1 = ada_chunk() if host else None
            u = chunk("g", view(w_in), 0, KC, DFF + CW * s)
            steps.append(Step(g=g, u=u, host=a1, gg=group("act"), ug=group("dve")))
        add("ffn_in", n=n, steps=steps, silu=silu_g.take(11), a32=act32.take(11), hi=act_hi.take(11),
            ready=act_ready.take(11), host=host)
        groups = []
        for m in range(4):
            cs = [chunk("g", view(w_out), k, min(KC, NF - k), CW * m) for k in range(0, NF, KC)]
            groups.append(Rows(chunks=cs, host=ada_chunk() if host and m < 3 else None,
                               grp=group("dve")))
        add("proj", n=n, groups=groups, ada=ada, gate=gate, half=half, hidden=True, first=first,
            ready=act_ready.total, x_out=x_ready.take(1),
            need=need(ada, gate))

    def w_out(w, n, ada, gate, first, hosted):
        groups = [Rows(chunks=[chunk("g", view(w), 0, KC, CW * m)], host=ada_chunk() if m < hosted else None,
                       grp=group("dve")) for m in range(4)]
        add("proj", n=n, groups=groups, ada=ada, gate=gate, half=False, hidden=False, first=first,
            ready=o_done.total, x_out=x_ready.take(1),
            need=need(ada, gate))

    def qkv(w, items, n, hosted, q_n):
        st = add("qkv", n=n, items=[], ready=h_ready.total, first=n == T)
        for c0, what in items:
            if what[0] == "forget":
                st.items.append(Item(what=what, chunk=chunk("f", view(w), 0, KC, c0, 8), grp=None, host=None, n=n))
            else:
                ch = chunk("g", view(w), 0, KC, c0)
                host = ada_chunk() if len(st.items) < hosted else None
                st.items.append(Item(what=what, chunk=ch, grp=group("act"), host=host,
                                     n=q_n if what[0] == "q" else n))
        st.done = ev_act.total
        st.hosted = len(ADA) if len(ADA) == sum(ADA_CHUNKS) or st.items[-1].grp is None else None
        state.update(q_in=st.done, normed=None)

    def attention(name, pairs, unroll, **k):
        s = add("attn", name=name, pairs=pairs, unroll=unroll, **state, **k)
        s.tper = 2 if s.diff else 4
        s.units, s.bias_in = 4 * pairs, bias_in.total
        s.q, s.v = q_staged.take(pairs), v_staged.take(pairs)
        s.sc, s.mx, s.ex = scores.take(s.units), nmax.take(s.units), exp_done.take(s.units)
        s.sk = sink_done.take(s.units) if s.sink else None
        s.pb, s.tu, s.cp = (t.take(s.tper * pairs) for t in (probs, turned, copied))
        s.pv, s.o = pv_done.take(pairs), o_done.take(pairs)

    def causal_heads(name, q, k, vcol, out_tile, bias, diff=False):
        attention(name, 4, 1, diff=diff, sink=None, qtile=lambda p: q + p, ktile=lambda p: k + p,
                  vcol=lambda p: vcol + P * p, vw=P, vblk=0, vrow=D, nblk=lambda qt: qt + 1, qoff=0, koff=0,
                  bias=bias, out=lambda p: out_tile + p)

    def t5(h0):
        def bias(p, hh, qt):
            return "bias", T * (h0(p, hh)) + (P if qt == 0 else 0), P * (qt + 1)
        return bias

    add("setup")
    ada_run(8)
    mod("mod", 0, 0, 1, T)
    qkv(a["w_in_ab"][0],
        [(0, ("q", 0)), (256, ("q", 2)), (512, ("k", 0)), (768, ("k", 2)), (1024, ("v", 0)), (1280, ("v", 256)),
         (1536, ("q", 4)), (1792, ("q", 6)), (2048, ("k", 4)), (2304, ("k", 6)), (2560, ("v", 512)),
         (2816, ("v", 768))], T, 12, T)
    add("bias", what="t5", rows=(0, 12), take=bias_in.take(32))
    causal_heads("differential", 0, 0, 0, 0, t5(lambda p, hh: p), diff=True)
    add("sub_norm")
    causal_heads("dilated", 4, 4, 512, 4, t5(lambda p, hh: 4 + 2 * p + hh))
    w_out(a["w_o"][0], T, 0, 2, True, 4)
    mod("ln", 0, 3, 4, T, gain=0, gain_b=32)
    ffn(a["w_ffn_in"][0], a["w_ffn_out"][0], T, 0, 5, False, True, True)
    mod("ln", 1, 0, 1, T, gain=8, gain_b=40)
    qkv(a["w_in_cd"][0],
        [(0, ("q", 0)), (256, ("q", 2)), (512, ("k", 0)), (768, ("k", 2)), (1024, ("v", 0)), (1280, ("v", 256)),
         (1536, ("q", 4)), (1792, ("q", 6)), (2048, ("k", 4)), (2304, ("k", 6)), (2560, ("v", 512)),
         (2816, ("v", 768)), (3072, ("forget",))], T, 7, T)
    add("bias", what="t5", rows=(12, 8), take=bias_in.take(32))
    causal_heads("moba", 0, 0, 0, 0, t5(lambda p, hh: 2 * p + hh))
    add("forget_bias")
    causal_heads("forget", 4, 4, 512, 4,
                 lambda p, hh, qt: ("bias", 512 * (2 * p + hh) + T * qt, P * (qt + 1)))
    w_out(a["w_o"][1], T, 1, 2, True, 3)
    mod("ln", 1, 3, 4, T, gain=16, gain_b=48)
    ffn(a["w_ffn_in"][1], a["w_ffn_out"][1], T, 1, 5, False, True, True)
    mod("ln", 1, 0, 0, T, gain=24, gain_b=56, last_ln=True)
    for l in range(DEPTH):
        last = l == DEPTH - 1
        n = 2 * T
        mod("rms", 2 + l, 0, 1, n, gain=64 + 24 * l)
        ffn(a["w_ffn_up_2"][l, 0], a["w_ffn_down_2"][l, 0], n, 2 + l, 2, True, True, False)
        mod("rms", 2 + l, 3, 4, n, gain=64 + 24 * l + 8)
        qkv(a["w_in_2"][l],
            [(0, ("q", 0)), (256, ("q", 2)), (512, ("q", 4)), (768, ("q", 6)), (1024, ("k", 0)),
             (1280, ("k", 2)), (1536, ("v", 0)), (1792, ("v", 256)), (2048, ("kv",))], n, 8, T if last else n)
        add("bias", what="na", layer=l, take=bias_in.take(16 * 37))
        tiles = [(i, 2 * T) for i in (12, 8, 9, 10, 11)] + [(i, T if last else n) for i in (4, 5, 6, 7, 0, 1, 2, 3)]
        add("qk_norm", layer=l, items=tiles, sq=qn_sq.take(13), sums=qn_sums.take(13), mm=qn_mm.take(13),
            root=qn_root.take(1), out=qn_out.take(13), rmm=rope_mm.take(7), ro=rope_out.take(7),
            q_in=state["q_in"], bias_in=bias_in.total)
        state["normed"] = (qn_out.total, rope_out.total)
        two = dict(diff=False, nblk=lambda qt: 4, qoff=0, koff=0, vblk=0, vrow=640)
        attention("neighbourhood", 4, 1, sink=None, qtile=lambda p: p, ktile=lambda p: p,
                  vcol=lambda p: P * p, vw=P,
                  bias=lambda p, hh, qt: ("bias", 512 * (2 * p + hh) + T * qt, T), out=lambda p: p, **two)
        attention("window", 4, 2, sink=(lambda p, hh: 8 * l + 2 * p + hh) if l == 0 else
                  (lambda p, hh: 8 + 2 * p + hh), qtile=lambda p: 4 + p, ktile=lambda p: 5 + p // 2,
                  vcol=lambda p: 512 + HD * (p // 2), vw=HD,
                  bias=lambda p, hh, qt: ("window", qt, T), out=lambda p: 4 + p, **two)
        if not last:
            one = dict(diff=False, nblk=lambda qt: 2, qoff=T, koff=T, vblk=2, vrow=640, bias=None)
            attention("context_a", 4, 1, sink=None, qtile=lambda p: p, ktile=lambda p: p,
                      vcol=lambda p: P * p, vw=P, out=lambda p: p, **one)
            attention("context_b", 4, 2, sink=lambda p, hh: 2 * p + hh, qtile=lambda p: 4 + p,
                      ktile=lambda p: 5 + p // 2, vcol=lambda p: 512 + HD * (p // 2), vw=HD,
                      out=lambda p: 4 + p, **one)
        n2 = T if last else 2 * T
        w_out(a["w_out_2"][l], n2, 2 + l, 5, False, 0)
        mod("rms", 2 + l, 6, 7, n2, gain=64 + 24 * l + 16)
        ffn(a["w_ffn_up_2"][l, 1], a["w_ffn_down_2"][l, 1], n2, 2 + l, 8, True, not last, False)
    add("finish")
    assert len(ADA) == sum(ADA_CHUNKS), len(ADA)

    def raw_ap(n, kt, cw):
        return RAWS[:, n % RAW, 0:kt * cw].rearrange("p (t n) -> p t n", t=kt)

    def wait_landed(eng, at, f):
        eng.wait_ge(landed[f(at.u).n % RAW], at(lambda s: 16 * (f(s).n // RAW + 1)))

    def wait_split(eng, at, f):
        eng.wait_ge(lo_done[f(at.u).g % 2], at(lambda s: f(s).g // 2 + 1))

    def split_low(eng, mine, at, f):
        p = f(at.u)
        ch = p.chunk
        if p.g % 2 != mine:
            return
        eng.wait_ge(hi_done, at(lambda s: f(s).g + 1))
        eng.tensor_tensor(WL[:, p.g % SPLIT, 0:p.kt * CW].rearrange("p (t n) -> p t n", n=CW),
                          raw_ap(ch.n, ch.kt, CW)[:, p.k0:p.k0 + p.kt, :],
                          WH[:, p.g % SPLIT, 0:p.kt * CW].rearrange("p (t n) -> p t n", n=CW).bitcast(F32),
                          ALU.subtract).then_inc(lo_done[mine], 1)

    def ahead(at, f, split, late):
        p = f(at.u)
        if p.g + SPLIT >= len(PIECES):
            return
        if PIECES[p.g + SPLIT].chunk.n - p.chunk.n > RAW:
            late.append(p.g + SPLIT)
        else:
            split(at, lambda s: PIECES[f(s).g + SPLIT])

    def wait_slot(eng, at, f):
        if f(at.u).n < RAW:
            return
        before = lambda s: CHUNKS[f(s).n - RAW]
        if before(at.u).kind == "g":
            wait_split(eng, at, lambda s: before(s).pieces[-2])
            if at.reg is not None:
                eng.sem_inc(sp_waited, 1)
            wait_split(eng, at, lambda s: before(s).pieces[-1])
        else:
            eng.wait_ge(ada_used if before(at.u).kind == "a" else forget_used,
                        at(lambda s: before(s).raw_order + 1))
        if at.reg is not None:
            eng.sem_inc(sp_waited, 1)

    def unroll(s):
        return 4 if s.host else 2

    act_waited, pool_waited, sp_waited = sem("act_waited"), sem("pool_waited"), sem("sp_waited")

    def wait_apart(eng, on, value, count):
        eng.wait_ge(on, value)
        eng.sem_inc(count, 1)

    block = ctx.enter_context(nc.Block())

    @block.sync
    def _(sp):
        def load(at, f):
            ch = f(at.u)
            wait_slot(sp, at, f)
            src = ch.weight[:, ch.k0:ch.k0 + ch.kt, bass.ds(at(lambda s: f(s).c0), ch.cw)]
            sp.dma_start(raw_ap(ch.n, ch.kt, ch.cw), src).then_inc(landed[ch.n % RAW], 16)

        def load_one(ch):
            load(At(None, 0, 1, 1), lambda s: ch)

        def ffn_in(s):
            def step(at):
                load(at, lambda k: s.steps[k].g)
                if s.host:
                    load(at, lambda k: s.steps[k].host)
                load(at, lambda k: s.steps[k].u)
            step(At(None, 0, 1, 1))
            step(At(None, 1, 1, 1))
            each(sp, 2, 10, unroll(s), step)
            step(At(None, 10, 1, 1))

        def bias(s, part, parts):
            if part == 0:
                sp.wait_ge(skew_out, 48)
                sp.wait_ge(region_free, 1)
                sp.wait_ge(h_ready.sem, s.h_wait)
            if s.what == "t5":
                h0, n = s.rows
                src = bass.AP(t5_dram.tensor, h0 * P * BIAS_L + P - 1,
                              [[BIAS_L - 1, P], [P * BIAS_L, n], [1, T]])
                tiles = [(BT[:, 0:n * T].rearrange("p (h k) -> p h k", h=n), src), (CAUSAL[:, :], c["causal"])]
            else:
                tiles, row = [], NA_ROWS * NA_WIDTH
                for q in range(4):
                    half, qt = q % 2, q // 2
                    for h in range(NA_H):
                        src = bass.AP(na_dram.tensor, (s.layer * NA_H + h) * 64 * row + (3 - q) * NA_WIDTH + 63,
                                      [[row - 1, 64], [NA_WIDTH, 4], [1, 64]])
                        dst = BT[64 * half:64 * half + 64, 512 * h + T * qt:512 * h + T * qt + T]
                        tiles.append((dst.rearrange("p (i k) -> p i k", i=4), src))
                tiles += [(HEAD_ROWS[:, 0:13 * P], c["head_rows"]), (COS[:, :], c["cos"]), (SIN[:, :], c["sin"]),
                          (NEIGH[:, :], c["neighbour"]), (WINDOW[:, :, :].rearrange("p q k -> p (q k)"), c["window"])]
            for dst, src in tiles[len(tiles) * part // parts:len(tiles) * (part + 1) // parts]:
                sp.dma_start(dst, src).then_inc(bias_in.sem, 16)

        for s, after in zip(PLAN, PLAN[1:] + [None]):
            if s.kind == "ada":
                for ch in s.chunks:
                    load_one(ch)
            elif s.kind == "qkv":
                for it in s.items:
                    load_one(it.chunk)
                    if 2 <= s.items.index(it) < 9:
                        bias(after, s.items.index(it) - 2, 7)
                    if it.host:
                        load_one(it.host)
            elif s.kind == "ffn_in":
                ffn_in(s)
            elif s.kind == "proj":
                for g in s.groups:
                    for ch in g.chunks:
                        load_one(ch)
                    if g.host:
                        load_one(g.host)
        sp.wait_ge(out_cp, 4)
        sp.dma_start(out.rearrange("a (q p) d -> p (a q) d", p=P), OUTR[:, :, :]).then_inc(out_dma, 16)
        sp.wait_ge(out_dma, 16)

    @block.gpsimd
    def _(pool):
        chain = Chain(pool, pool_chain)
        late = list(range(SPLIT))

        def const(dst, src):
            pool.dma_start(dst, src).then_inc(const_in, 16)

        def setup():
            for t in credited:
                pool.sem_inc(t.sem, t.credit)
            const(head_cols[:, :], c["head_cols"])
            const(rotate[:, :], c["rotate"])
            for k in range(2):
                const(dup[k][:, :], c[f"dup{k}"])
            const(ONEHOT[:, :], c["bucket_onehot"])
            const(T5MASK[:, :], c["t5_mask"])
            const(TABLE[:, 0:12], a["rel_bias"])
            const(TABLE[:, 12:20], a["rel_bias"][:, 0:8])
            const(SINK[:, :], a["wa_sink_2"].rearrange("l h -> (l h)").rearrange("(o n) -> o n", o=1)
                  .broadcast_to([P, 16]))
            const(FB[:, :], a["forget_b"].rearrange("l h -> h l"))
            const(LROW[:, :, :], a["diff_lambda"].broadcast_to([P, 4, HD]))
            chain.link(pool.memset(RPB[:, :, :, :], 0.0))
            for l in range(2):
                pool.dma_start(RPB[:, l, :, 48:48 + RPB_W],
                               a["na_rpb_2"][l, :, 4:4 + NA_ROWS, :]).then_inc(skew_src, 16)
            pool.wait_ge(skew_src, 32)
            for l in range(2):
                src = RPB[:, l, :, :].rearrange("h i w -> h (i w)")
                pool.dma_start(na_dram[l], src[:, None, :].broadcast_to([NA_H, 64, NA_ROWS * NA_WIDTH])
                               ).then_inc(skew_out, 16)
            pool.wait_ge(t5_rows, 1)
            pool.dma_start(t5_dram, T5ROW[:, None, :].broadcast_to([N_T5, P, BIAS_L])).then_inc(skew_out, 16)
        def split(at, f):
            split_low(pool, 1, at, f)

        def ahead_of(at, f):
            for i in range(len(f(at.u).pieces)):
                ahead(at, lambda k: f(k).pieces[i], split, late)

        def low(s):
            def tile(at):
                par = at.u % 2
                t = at(lambda k: k)
                pool.wait_ge(mod_hi.sem, at(lambda k: s.hi + k + 1))
                pool.wait_ge(mod_t2.sem, at(lambda k: s.t2 + k + 1))
                pool.tensor_tensor(HL[:, bass.ds(t, 1), 0:s.n], T2[:, par:par + 1, 0:s.n],
                                   HH[:, bass.ds(t, 1), 0:s.n].bitcast(F32), ALU.subtract
                                   ).then_inc(h_ready.sem, 1)
            each(pool, 0, 8, 2, tile)

        def ffn_in(s):
            def step(at):
                ahead_of(at, lambda k: s.steps[k].g)
                ahead_of(at, lambda k: s.steps[k].u)
                t = at(lambda k: 2 * k)
                pool.wait_ge(act_hi.sem, at(lambda k: s.hi + k + 1))
                pool.tensor_tensor(AL[:, bass.ds(t, 2), 0:s.n], T2[:, :, 0:s.n],
                                   AH[:, bass.ds(t, 2), 0:s.n].bitcast(F32), ALU.subtract
                                   ).then_inc(act_ready.sem, 1)
            each(pool, 0, 10, unroll(s), step)
            step(At(None, 10, 1, 1))

        def attn(s):
            vb = VB[:, 0:4 * s.vrow if s.vrow == 640 else 2 * s.vrow].rearrange("p (b n) -> p b n", n=s.vrow)
            nb = s.nblk(1)

            def pair(at):
                wait_apart(pool, scores.sem, at(lambda p: s.sc + 4 * p), pool_waited)
                pool.tensor_copy(QS[:, :], QB[:, bass.ds(at(s.qtile), 1), s.qoff:s.qoff + T]
                                 .rearrange("p o t -> p (o t)"))
                nk = P * nb
                pool.tensor_copy(KS[:, 0:nk], KB[:, bass.ds(at(s.ktile), 1), s.koff:s.koff + nk]
                                 .rearrange("p o t -> p (o t)")).then_inc(q_staged.sem, 1)
                wait_apart(pool, pv_done.sem, at(lambda p: s.pv + p), pool_waited)
                pool.tensor_copy(VS[:, 0:nb, 0:s.vw], vb[:, s.vblk:s.vblk + nb, bass.ds(at(s.vcol), s.vw)]
                                 ).then_inc(v_staged.sem, 1)
            pool.wait_ge(ev_act.sem, s.q_in)
            if s.normed:
                pool.wait_ge(qn_out.sem, s.normed[0])
                pool.wait_ge(rope_out.sem, s.normed[1])
            each(pool, 0, s.pairs, s.unroll, pair)

        for s in PLAN:
            if s.kind == "setup":
                setup()
            elif s.kind == "ada":
                for g in late:
                    split(At(None, 0, 1, 1), lambda _: PIECES[g])
                late.clear()
            elif s.kind in ("mod", "ln", "rms") and not s.last_ln:
                low(s)
            elif s.kind == "ffn_in":
                ffn_in(s)
            elif s.kind == "qkv":
                for it in s.items:
                    ahead_of(At(None, 0, 1, 1), lambda _: it.chunk)
            elif s.kind == "proj":
                for g in s.groups:
                    for ch in g.chunks:
                        ahead_of(At(None, 0, 1, 1), lambda _: ch)
            elif s.kind == "forget_bias":
                pool.wait_ge(o_done.sem, s.o_wait)
                pool.dma_start(NEGSEL, c["neg_select"].rearrange("h (a b p) -> h a b p", a=2, b=4)
                               ).then_inc(fg_sel, 16)
            elif s.kind == "attn":
                attn(s)


    @block.tensor
    def _(pe):
        closed, one = {"at": 0}, At(None, 0, 1, 1)

        def mm(o, w, x, start, stop):
            return pe.matmul(o, w, x, start=start, stop=stop, skip_group_check=True)

        def product(o, kt, wh, wl, xh, xl, start, stop):
            mm(o, wh, xh, start, False)
            mm(o, wh, xl, False, False)
            return mm(o, wl, xh, False, stop)

        def ada(at, f):
            if f(at.u).raw_order > closed["at"]:
                sum_rows(at, lambda s: ADA[f(s).raw_order - 1])

        def close(a):
            if a > closed["at"]:
                sum_rows(one, lambda _: ADA[a - 1])
                closed["at"] = a

        def sum_rows(at, f):
            ch = f(at.u)
            nv = 1 if ch.order[0] < 2 else 2
            pe.wait_ge(ada_used, at(lambda s: f(s).raw_order + 1))
            if ch.raw_order > 0:
                pe.wait_ge(ada_out, at(lambda s: f(s).raw_order))
            for j in range(2):
                for v in range(nv):
                    ins = mm(B_ADA[:, j * nv + v:j * nv + v + 1],
                             ACC[:, ch.raw_order % 2, v, j * P:(j + 1) * P], ones[:, 0:1], True, True)
            ins.then_inc(ada_sum, 1)

        def wait_bank(at, f):
            g = f(at.u)
            if g.n >= 2:
                before = lambda s: GROUPS[f(s).n - 2]
                pe.wait_ge(before(at.u).tally.sem, at(lambda s: before(s).done))

        def features(at, f, grp, kt_all, k_base, xh, xl, n, width=2, left=None, ready=None):
            ch = f(at.u)
            for i, pc in enumerate(ch.pieces):
                wait_split(pe, at, lambda s: f(s).pieces[i])
                wh = WH[:, pc.g % SPLIT, :].rearrange("p (t n) -> p t n", n=CW)
                wl = WL[:, pc.g % SPLIT, :].rearrange("p (t n) -> p t n", n=CW)
                for k in range(pc.kt):
                    kk = k_base + pc.k0 + k
                    if ready:
                        ready(kk)
                    for j in range(width):
                        ins = product(PAIR[grp.n % 2][j][:, 0:n], kk, wh[:, k, j * P:(j + 1) * P],
                                      wl[:, k, j * P:(j + 1) * P], xh[:, kk, 0:n], xl[:, kk, 0:n],
                                      kk == 0, kk == kt_all - 1)
                    if left:
                        ins = left(wh, wl, k, kk)
                ins.then_inc(piece_used.sem, 1)

        def tokens(ch, grp, n, col, cw, bank_of, at_col):
            def part(wh, wl, k, kk):
                for tt in range(n // P):
                    o = bank_of(tt)[:, at_col(tt):at_col(tt) + cw]
                    first = kk == 0 and at_col(tt) == 0
                    h, lo = HH[:, kk, tt * P:(tt + 1) * P], HL[:, kk, tt * P:(tt + 1) * P]
                    mm(o, h, wh[:, k, col:col + cw], first, False)
                    mm(o, h, wl[:, k, col:col + cw], False, False)
                    ins = mm(o, lo, wh[:, k, col:col + cw], False, kk == KC - 1)
                return ins
            return part

        def modulated(last):
            return lambda kk: pe.wait_ge(h_ready.sem, last - NT + kk + 1)

        def qkv(s):
            for it in s.items:
                ch, grp = it.chunk, it.grp
                ready = modulated(s.ready) if it is s.items[0] else None
                if it.what[0] == "forget":
                    close(s.hosted)
                    wait_landed(pe, one, lambda _: ch)
                    pe.wait_ge(ada_out, s.hosted)
                    w = raw_ap(ch.n, KC, 8)
                    for k in range(KC):
                        mm(B_ADA[0:8, 0:T], w[:, k, :], HH[:, k, 0:T].bitcast(F32), k == 0, False)
                        ins = mm(B_ADA[0:8, 0:T], w[:, k, :], HL[:, k, 0:T].bitcast(F32), False, k == KC - 1)
                    ins.then_inc(forget_used, 1)
                    continue
                wait_bank(one, lambda _: grp)
                pair = PAIR[grp.n % 2]
                if it.what[0] == "v":
                    part = tokens(ch, grp, s.n, 0, CW, lambda tt: pair[tt // 2], lambda tt: CW * (tt % 2))
                    features(one, lambda _: ch, grp, KC, 0, HH, HL, s.n, 0, part)
                elif it.what[0] == "kv":
                    part = tokens(ch, grp, s.n, P, P, lambda tt: pair[1], lambda tt: P * tt)
                    features(one, lambda _: ch, grp, KC, 0, HH, HL, s.n, 1, part)
                else:
                    features(one, lambda _: ch, grp, KC, 0, HH, HL, it.n, ready=ready)
                if it.host:
                    ada(one, lambda _: it.host)
            if s.hosted:
                close(s.hosted)

        def ffn_in(s):
            def step(at, ready=None):
                wait_bank(at, lambda k: s.steps[k].gg)
                features(at, lambda k: s.steps[k].g, s.steps[at.u].gg, KC, 0, HH, HL, s.n, ready=ready)
                if s.host:
                    ada(at, lambda k: s.steps[k].host)
                wait_bank(at, lambda k: s.steps[k].ug)
                features(at, lambda k: s.steps[k].u, s.steps[at.u].ug, KC, 0, HH, HL, s.n)
            step(At(None, 0, 1, 1), modulated(s.h_wait))
            each(pe, 1, 11, unroll(s), step)

        def proj(s, norm):
            xh, xl, kt = (AH, AL, NF) if s.hidden else (HH, HL, NT)
            if not s.hidden:
                pe.wait_ge(o_done.sem, s.ready)

            def hidden(kk):
                if kk % 2 == 0:
                    pe.wait_ge(act_ready.sem, s.ready - NF // 2 + kk // 2 + 1)

            def two(at):
                for b in range(2):
                    grp = lambda k: s.groups[2 * k + b]
                    wait_bank(at, lambda k: grp(k).grp)
                    for j in range(len(grp(0).chunks)):
                        features(at, lambda k: grp(k).chunks[j], grp(at.u).grp, kt, KC * j, xh, xl, s.n,
                                 ready=hidden if s.hidden and at.u == 0 and b == 0 else None)
                    if grp(at.u).host:
                        ada(at, lambda k: grp(k).host)
                    if b or at.u:
                        sums(norm, 2 * at.u + b - 1, s.groups[2 * at.u + b - 1].grp.done)
            for k in range(2):
                two(At(None, k, 1, 1))

        def setup():
            pe.wait_ge(rows_in, 16 * 14)
            at = 0
            for r in ROWS:
                n = r.shape[0]
                ins = pe.transpose(BANK[0][:, at:at + n], r[:, :], ident[0:n, 0:n])
                at += n
            ins.then_inc(setup_mm, 1)
            pe.wait_ge(const_in, 16 * 11)
            mm(BANK[2][0:N_T5, 0:BIAS_L], TABLE[:, :], ONEHOT[:, :], True, True).then_inc(setup_mm, 1)
            pe.wait_ge(tokens_in, 32)
            for i, b in enumerate(TURN_BANKS):
                src, k = (XIN, CIN)[i // 4], i % 4
                if i >= 4:
                    pe.wait_ge(setup_act, i - 3)
                for t in range(2):
                    for q in range(2):
                        ins = pe.transpose(BANK[b][:, T * t + P * q:T * t + P * q + P],
                                           src[:, q, P * (2 * k + t):P * (2 * k + t + 1)], ident[:, :])
                ins.then_inc(setup_mm, 1)

        def sums(s, m, done=None):
            for t in (2 * m, 2 * m + 1):
                if s.kind == "ln":
                    if done:
                        pe.wait_ge(ev_dve.sem, done)
                    ins = mm(B_STAT[:, 0:s.n], ones[:, :], X[:, t, 0:s.n], t == 0, t == NT - 1)
                    if t == NT - 1:
                        ins.then_inc(mean_mm.sem, 1)
                elif s.kind == "rms":
                    squares(s, t, B_STAT)

        def squares(s, t, bank):
            pe.wait_ge(stat_in.sem, s.stat_in + t + 1)
            mm(bank[:, 0:s.n], ones[:, :], T1[:, t % 2, 0:s.n], t == 0, t == NT - 1).then_inc(stat_mm.sem, 1)

        def stats(s, before):
            pe.wait_ge(x_ready.sem, s.x)
            for m in range(3 if before.kind == "proj" else 0, 4):
                sums(s, m)
            if s.kind == "ln":
                for t in range(NT):
                    squares(s, t, B_T[0])

        def sub_norm():
            for t in range(4):
                pe.wait_ge(sub_sq, t + 1)
                if t >= 2:
                    pe.wait_ge(sub_rt, t - 1)
                mm(B_T[t % 2][:, 0:T], ones[:, :], T1[:, t % 2, 0:T], True, True).then_inc(sub_mm, 1)

        def forget_bias(s):
            pe.wait_ge(fg_cum, 1)
            for q in range(2):
                ins = pe.transpose(B_T[0][:, 8 * q:8 * q + 8], CUM[:, P * q:P * q + P], ident[0:8, 0:8])
            ins.then_inc(fg_mm, 1)
            pe.wait_ge(fg_sel, 16)
            for h in range(8):
                if h >= 2:
                    pe.wait_ge(fg_free, h - 1)
                sel = NEGSEL[:, h // 4, h % 4, :]
                mm(BANK[h % 2][:, 0:T], sel, CUM, True, True).then_inc(fg_mm, 1)
            pe.wait_ge(fg_free, 8)

        def qk_norm(s):
            for i, (t, w) in enumerate(s.items):
                pe.wait_ge(qn_sq.sem, s.sq + i + 1)
                mm(B_STAT[0:26, 0:w], head_cols[:, 24 - 2 * t:50 - 2 * t], T1[:, i % 2, 0:w], i == 0, i == 12
                   ).then_inc(qn_sums.sem, 1)
            pe.wait_ge(bias_in.sem, s.bias_in)
            pe.wait_ge(qn_rstd, s.layer + 1)
            for i, (t, w) in enumerate(s.items):
                if i >= 2:
                    pe.wait_ge(qn_out.sem, s.out + i - 1)
                mm(B_T[i % 2][:, 0:w], HEAD_ROWS[:, P * t:P * t + P], RB[0:26, 0:w], True, True).then_inc(qn_mm.sem, 1)
            for r in range(5):
                pe.wait_ge(qn_out.sem, s.out + (1, 6, 7, 8, 9)[r])
                if r >= 2:
                    pe.wait_ge(rope_out.sem, s.ro + r - 1)
                src = QB[:, 3 + r, 0:T] if r else KB[:, 4, 0:T]
                mm(BANK[2 + r % 2][:, 0:T], rotate[:, :], src, True, True).then_inc(rope_mm.sem, 1)
            pe.wait_ge(rope_out.sem, s.ro + 1)
            for kv in range(2):
                mm(BANK[kv][:, :], dup[kv][:, :], KB[:, 4, :], True, True).then_inc(rope_mm.sem, 1)

        def attn(s):
            def score(at):
                pe.wait_ge(q_staged.sem, at(lambda p: s.q + p + 1))
                for hh in range(2):
                    for qt in range(2):
                        j, nk = 2 * hh + qt, P * s.nblk(qt)
                        pe.wait_ge(exp_done.sem, at(lambda p: s.ex + 4 * p + j - 3))
                        mm(BANK[j][:, 0:nk], QS[HD * hh:HD * hh + HD, P * qt:P * qt + P],
                           KS[HD * hh:HD * hh + HD, 0:nk], True, True).then_inc(scores.sem, 1)

            def turn(at):
                for jj in range(s.tper):
                    nb = s.nblk(jj % 2)
                    pe.wait_ge(probs.sem, at(lambda p: s.pb + s.tper * p + jj + 1))
                    pe.wait_ge(copied.sem, at(lambda p: s.cp + s.tper * p + jj - 1))
                    for b in range(nb):
                        ins = pe.transpose(B_T[jj % 2][:, P * b:P * b + P], PR[:, jj, P * b:P * b + P],
                                           ident[:, :])
                    ins.then_inc(turned.sem, 1)

            def values(at):
                pe.wait_ge(v_staged.sem, at(lambda p: s.v + p + 1))
                pe.wait_ge(copied.sem, at(lambda p: s.cp + s.tper * (p + 1)))
                pe.wait_ge(o_done.sem, at(lambda p: s.o + p))
                for jj in range(s.tper):
                    hh, qt = jj // 2, jj % 2
                    nb = s.nblk(qt)
                    vc = 0 if s.diff or s.vw == HD else HD * hh
                    w = P if s.diff else HD
                    o = B_STAT[:, P * qt:P * qt + P] if s.diff else B_STAT[HD * hh:HD * hh + HD, P * qt:P * qt + P]
                    for b in range(nb):
                        ins = mm(o, VS[:, b, vc:vc + w], PT[:, jj, b, :], b == 0, b == nb - 1)
                ins.then_inc(pv_done.sem, 1)
            score(one)

            def body(at):
                turn(at)
                score(At(at.reg, at.u + 1, at.unroll, at.n))
                values(at)
            each(pe, 0, s.pairs - 1, 1, body)
            last = At(None, s.pairs - 1, 1, 1)
            turn(last)
            values(last)

        def finish(s):
            pe.wait_ge(x_ready.sem, s.x)
            for b in range(4):
                q, f0 = b // 2, 4 * (b % 2)
                for t in range(4):
                    ins = pe.transpose(BANK[b][:, P * t:P * t + P], X[:, f0 + t, P * q:P * q + P], ident[:, :])
                ins.then_inc(out_mm, 1)

        for before, s, after in zip([None] + PLAN, PLAN, PLAN[1:] + [None]):
            if s.kind == "setup":
                setup()
            elif s.kind == "ada":
                for ch in s.chunks:
                    ada(one, lambda _, ch=ch: ch)
                close(s.hosted)
            elif s.kind in ("ln", "rms"):
                stats(s, before)
            elif s.kind == "qkv":
                qkv(s)
            elif s.kind == "ffn_in":
                ffn_in(s)
            elif s.kind == "proj":
                proj(s, after)
            elif s.kind == "sub_norm":
                sub_norm()
            elif s.kind == "forget_bias":
                forget_bias(s)
            elif s.kind == "qk_norm":
                qk_norm(s)
            elif s.kind == "attn":
                attn(s)
            elif s.kind == "finish":
                finish(s)

    @block.scalar
    def _(act):
        chain = Chain(act, act_chain)
        late = list(range(SPLIT))
        one = At(None, 0, 1, 1)

        def split(at, f):
            p = f(at.u)
            ch = p.chunk
            wait_landed(act, at, lambda s: f(s).chunk)
            act.wait_ge(piece_used.sem, at(lambda s: f(s).g + 1))
            act.activation(WH[:, p.g % SPLIT, 0:p.kt * CW].rearrange("p (t n) -> p t n", n=CW),
                           raw_ap(ch.n, ch.kt, CW)[:, p.k0:p.k0 + p.kt, :], ACT.Copy).then_inc(hi_done, 1)

        def flush():
            while late:
                g = late.pop(0)
                split(one, lambda _: PIECES[g])

        def used(at, f):
            act.wait_ge(piece_used.sem, at(lambda s: f(s).g + SPLIT + 1))

        def rows(dst, src):
            act.dma_start(dst, src).then_inc(rows_in, 16)

        def setup():
            rows(ROWS[0][0:8, :], a["c"].rearrange("a (t p) -> (a t) p", p=P))
            rows(ROWS[0][8:16, :], a["c_2"].rearrange("a (t p) -> (a t) p", p=P))
            rows(ROWS[0][16:24, :], a["c_ctx_2"].rearrange("(t p) -> t p", p=P))
            rows(ROWS[0][24:120, :], a["b_ada"].rearrange("l (t p) -> (l t) p", p=P))
            rows(ident[:, :], c["ident"])
            rows(ones[:, :], c["ones"])
            for l in range(2):
                rows(ROWS[1 + l][:, :], a["b_ada_2"][l].rearrange("(t p) -> t p", p=P))
            rows(ROWS[3][0:32, :], a["ln_g"].rearrange("l j (t p) -> (l j t) p", p=P))
            rows(ROWS[3][32:64, :], a["ln_b"].rearrange("l j (t p) -> (l j t) p", p=P))
            rows(ROWS[3][64:112, :], a["norm_g_2"].rearrange("l j (t p) -> (l j t) p", p=P))
            rows(ROWS[4][0:1, :], a["diff_subln_g"])
            for hf in range(2):
                rows(ROWS[4][1:9, hf * HD:(hf + 1) * HD], a["qk_norm_g_2"].rearrange("l j d -> (l j) d"))
            for dst, src in ((XIN, a["x"]), (CIN, a["ctx_2"])):
                act.dma_start(dst[:, :, :], src.rearrange("a (q p) d -> p (a q) d", p=P)).then_inc(tokens_in, 16)
            act.wait_ge(cols_done, 1)
            act.activation(SILU_C[:, 0:8], C_COLS[:, 0:8], ACT.Silu)
            pairs = SILU_C[:, 8:24].rearrange("p (t v) -> p t v", v=2)
            for v in range(2):
                ins = act.activation(pairs[:, :, v], C_COLS[:, 8 + 8 * v:16 + 8 * v], ACT.Silu)
            ins.then_inc(silu_done, 1)
            for i, b in enumerate(TURN_BANKS):
                act.wait_ge(setup_mm, 3 + i)
                half = (i // 4) * T
                act.activation(X[:, 2 * (i % 4):2 * (i % 4) + 2, half:half + T],
                               BANK[b][:, :].rearrange("p (t n) -> p t n", t=2), ACT.Copy).then_inc(setup_act, 1)
            act.wait_ge(lam_sum, 1)
            act.activation(LAM[:, 2:4], LAM[:, 0:2], ACT.Exp).then_inc(lam_exp, 1)

        def square(s, t):
            act.wait_ge(stat_mm.sem, s.stat + t - 1)
            act.activation(T1[:, t % 2, 0:s.n], X[:, t, 0:s.n], ACT.Square).then_inc(stat_in.sem, 1)

        def squares(s, m, done):
            if s.kind == "rms":
                act.wait_ge(ev_dve.sem, done)
                for t in (2 * m, 2 * m + 1):
                    square(s, t)

        def stats(s, before):
            act.wait_ge(x_ready.sem, s.x)
            for t in range(6 if s.kind == "rms" and before.kind == "proj" else 0, NT):
                if s.kind == "ln":
                    act.wait_ge(centred.sem, s.cen + t + 1)
                square(s, t)
            act.wait_ge(stat_mm.sem, s.stat + NT)
            bank, eps = (B_T[0], EPS[:, 0:1]) if s.kind == "ln" else (B_STAT, EPS[:, 1:2])
            act.activation(RB[:, 0:s.n], bank[:, 0:s.n], ACT.Sqrt, bias=eps, scale=1.0 / D).then_inc(rstd_sq.sem, 1)

        def modulate(s):
            act.wait_ge(ada_out, s.need)
            ad = AD[s.ada]

            def tile(at):
                par, t = at.u % 2, at(lambda k: k)
                if s.kind != "mod":
                    act.wait_ge(mod_src.sem, at(lambda k: s.src + k + 1))
                wait_apart(act, h_ready.sem, at(lambda k: s.h + k - 1), act_waited)
                for v in range(s.n // T):
                    cols = slice(v * T, v * T + T)
                    src = T1[:, par, cols] if s.kind == "rms" else \
                        X[:, bass.ds(t, 1), cols].rearrange("p o n -> p (o n)")
                    sc = GS[:, bass.ds(t, 1), v] if s.kind == "rms" else ad[:, bass.ds(at(lambda k: 8 * s.scale + k), 1), v]
                    sh = ad[:, bass.ds(at(lambda k: 8 * s.shift + k), 1), v]
                    ins = act.activation(T2[:, par, cols], src, ACT.Identity, bias=sh, scale=sc)
                ins.then_inc(mod_t2.sem, 1)
            each(act, 0, 8, 2, tile)

        def qkv(s):
            if not s.hosted and s.first:
                act.wait_ge(skew_out, 48)
            for it in s.items:
                if it.what[0] == "forget":
                    continue
                for p in it.chunk.pieces:
                    ahead(one, lambda _: p, split, late)
                used(one, lambda _: it.chunk.pieces[-1])
                pair, kind, n = PAIR[it.grp.n % 2], it.what[0], it.n
                if kind in "qk":
                    dst, t = (QB if kind == "q" else KB), it.what[1]
                    for j in range(2):
                        ins = act.activation(dst[:, t + j, 0:n], pair[j][:, 0:n], ACT.Copy,
                                             scale=SCALE if s.first and kind == "q" else 1.0)
                elif kind == "v":
                    row = D if s.first else 640
                    v = VB[:, 0:n // P * row].rearrange("p (b n) -> p b n", n=row)
                    for j in range(n // T):
                        ins = act.activation(v[:, 2 * j:2 * j + 2, it.what[1]:it.what[1] + CW],
                                             pair[j][:, :].rearrange("p (b n) -> p b n", b=2), ACT.Copy)
                else:
                    v = VB[:, :].rearrange("p (b n) -> p b n", n=640)
                    act.activation(KB[:, 4, :], pair[0][:, :], ACT.Copy)
                    ins = act.activation(v[:, :, 512:640], pair[1][:, :].rearrange("p (b n) -> p b n", b=4),
                                         ACT.Copy)
                ins.then_inc(ev_act.sem, 1)

        def ffn_in(s):
            n = s.n

            def hidden_hi(at):
                t = at(lambda k: 2 * k)
                wait_apart(act, act32.sem, at(lambda k: s.a32 + k + 1), act_waited)
                act.activation(AH[:, bass.ds(t, 2), 0:n], T2[:, :, 0:n], ACT.Copy).then_inc(act_hi.sem, 1)

            def step(at):
                gg = s.steps[at.u].gg
                for i in range(KC // PIECE):
                    ahead(at, lambda k: s.steps[k].g.pieces[i], split, late)
                used(at, lambda k: s.steps[k].g.pieces[-1])
                act.wait_ge(act32.sem, at(lambda k: s.a32 + k))
                act.activation(T1[:, 0, 0:n], PAIR[gg.n % 2][0][:, 0:n], ACT.Silu)
                act.activation(T1[:, 1, 0:n], PAIR[gg.n % 2][1][:, 0:n], ACT.Silu).then_inc(silu_g.sem, 1)
                act.wait_ge(silu_g.sem, at(lambda k: s.silu + k + 1))
                act.sem_inc(ev_act.sem, 1)
                for i in range(KC // PIECE):
                    ahead(at, lambda k: s.steps[k].u.pieces[i], split, late)
                hidden_hi(at)
            each(act, 0, 10, unroll(s), step)
            step(At(None, 10, 1, 1))

        def proj(s, norm):
            for m, g in enumerate(s.groups):
                for ch in g.chunks:
                    for p in ch.pieces:
                        ahead(one, lambda _: p, split, late)
                    if m and ch is g.chunks[0]:
                        squares(norm, m - 1, s.groups[m - 1].grp.done)

        def sub_norm(s):
            act.wait_ge(o_done.sem, s.o_wait)
            for t in range(4):
                if t >= 2:
                    act.wait_ge(sub_mm, t - 1)
                act.activation(T1[:, t % 2, 0:T], OF[:, t, :], ACT.Square).then_inc(sub_sq, 1)
                act.wait_ge(sub_mm, t + 1)
                if t >= 2:
                    act.wait_ge(sub_out, t - 1)
                act.activation(T2[:, t % 2, 0:T], B_T[t % 2][:, 0:T], ACT.Sqrt, bias=EPS[:, 0:1], scale=1.0 / P
                               ).then_inc(sub_rt, 1)

        def forget_bias(s):
            act.wait_ge(o_done.sem, s.o_wait)
            act.wait_ge(forget_used, 1)
            act.activation(FD, B_ADA[0:8, 0:T], ACT.Identity, bias=FB[:, 0:1]).then_inc(fg_x, 1)
            act.wait_ge(fg_abs, 1)
            chain.link(act.activation(FD_ABS, FD_ABS, ACT.Exp, scale=-1.0))
            act.activation(FD_ABS, FD_ABS, ACT.Ln, bias=1.0).then_inc(fg_exp, 1)

        def qk_norm(s):
            act.wait_ge(ev_act.sem, s.q_in)

            for i, (t, w) in enumerate(s.items):
                if i >= 2:
                    act.wait_ge(qn_sums.sem, s.sums + i - 1)
                src = QB[:, t, 0:w] if t < 8 else KB[:, t - 8, 0:w]
                act.activation(T1[:, i % 2, 0:w], src, ACT.Square).then_inc(qn_sq.sem, 1)
            act.wait_ge(qn_sums.sem, s.sums + 13)
            act.activation(RB[0:26, :], B_STAT[0:26, :], ACT.Sqrt, bias=EPS[0:26, 1:2], scale=1.0 / HD
                           ).then_inc(qn_root.sem, 1)

        def attn(s):
            def pair(at):
                for hh in range(2):
                    for qt in range(2):
                        j, nk = 2 * hh + qt, P * s.nblk(qt)
                        back = j % 2 if s.diff else j
                        act.wait_ge(nmax.sem, at(lambda p: s.mx + 4 * p + j + 1))
                        wait_apart(act, turned.sem, at(lambda p: s.tu + s.tper * (p - 1) + back + 1), act_waited)
                        if s.sink:
                            act.activation(ES[:, j:j + 1], SINK[:, bass.ds(at(lambda p: s.sink(p, hh)), 1)],
                                           ACT.Exp, bias=NM[:, j:j + 1]).then_inc(sink_done.sem, 1)
                        act.activation(PR[:, j, 0:nk], BANK[j][:, 0:nk], ACT.Exp, bias=NM[:, j:j + 1],
                                       accum_out=RS[:, j:j + 1]).then_inc(exp_done.sem, 1)
                act.wait_ge(pv_done.sem, at(lambda p: s.pv + p))
                for jj in range(s.tper):
                    nb = s.nblk(jj % 2)
                    act.wait_ge(turned.sem, at(lambda p: s.tu + s.tper * p + jj + 1))
                    act.activation(PT[:, jj, 0:nb, :], B_T[jj % 2][:, 0:P * nb].rearrange("p (b n) -> p b n", n=P),
                                   ACT.Copy).then_inc(copied.sem, 1)
            each(act, 0, s.pairs, s.unroll, pair)

        for before, s, after in zip([None] + PLAN, PLAN, PLAN[1:] + [None]):
            if s.kind == "setup":
                setup()
            elif s.kind == "ada":
                flush()
            elif s.kind in ("mod", "ln", "rms"):
                if s.kind != "mod":
                    stats(s, before)
                if not s.last_ln:
                    modulate(s)
            elif s.kind == "qkv":
                qkv(s)
            elif s.kind == "ffn_in":
                ffn_in(s)
            elif s.kind == "proj":
                proj(s, after)
            elif s.kind == "sub_norm":
                sub_norm(s)
            elif s.kind == "forget_bias":
                forget_bias(s)
            elif s.kind == "qk_norm":
                qk_norm(s)
            elif s.kind == "attn":
                attn(s)
            elif s.kind == "finish":
                for b in (0, 2):
                    act.wait_ge(out_mm, b + 1)
                    act.activation(OUTR[:, b // 2, 0:512], BANK[b][:, :], ACT.Copy).then_inc(out_cp, 1)

    @block.vector
    def _(dve):
        chain = Chain(dve, dve_chain)
        late = list(range(SPLIT))
        closed = {"at": 0, "read": 0}
        one = At(None, 0, 1, 1)

        def split(at, f):
            split_low(dve, 0, at, f)

        def flush():
            while late:
                g = late.pop(0)
                split(one, lambda _: PIECES[g])

        def used(at, f):
            dve.wait_ge(piece_used.sem, at(lambda s: f(s).g + SPLIT + 1))

        def ada(at, f, part=0, parts=1):
            ch = f(at.u)
            if part == 0 and ch.raw_order > closed["at"] + 1:
                columns(at, lambda s: ADA[f(s).raw_order - 2])
            if part == 0:
                wait_landed(dve, at, f)
                if ch.raw_order >= 2:
                    dve.wait_ge(ada_sum, at(lambda s: f(s).raw_order - 1))
            w, nv = raw_ap(ch.n, KC, CW), 1 if ch.order[0] < 2 else 2
            for k in range(KC * part // parts, KC * (part + 1) // parts):
                for v in range(nv):
                    acc = ACC[:, ch.raw_order % 2, v, :]
                    i = k if nv == 1 else 8 + 2 * k + v
                    if k == 0:
                        ins = dve.tensor_scalar(acc, w[:, k, :], SILU_C[:, i:i + 1], None, ALU.mult)
                    else:
                        ins = dve.scalar_tensor_tensor(out=acc, in0=w[:, k, :], scalar=SILU_C[:, i:i + 1], in1=acc,
                                                       op0=ALU.mult, op1=ALU.add)
                if k < KC - 1:
                    chain.link(ins)
            if part == parts - 1:
                ins.then_inc(ada_used, 1)

        def ahead_of(at, f, host=None):
            n = len(f(at.u).pieces)
            for i in range(n):
                ahead(at, lambda k: f(k).pieces[i], split, late)
                if host:
                    ada(at, host, i, n)

        def close(a):
            while closed["read"] < a:
                columns(one, lambda _: ADA[closed["read"]])
            closed["at"] = a

        def columns(at, f):
            ch = f(at.u)
            m = ch.order[0]
            nv = 1 if m < 2 else 2
            bias = (B1 if m < 2 else B2)[:, m % 2, :]
            col = at(lambda s: 2 * f(s).order[1])
            dve.wait_ge(ada_sum, at(lambda s: f(s).raw_order + 1))
            b = bias[:, bass.ds(col, 2)]
            if nv == 2:
                b = b[:, :, None].broadcast_to([P, 2, 2])
                o, i = AD[m][:, bass.ds(col, 2), :], B_ADA[:, 0:4].rearrange("p (c v) -> p c v", v=2)
            else:
                o, i = AD[m][:, bass.ds(col, 2), 0], B_ADA[:, 0:2]
            dve.tensor_tensor(o, i, b, ALU.add).then_inc(ada_out, 1)
            closed["read"] = max(closed["read"], f(at.u + at.unroll * (at.n - 1)).raw_order + 1)

        def setup():
            dve.memset(EPS[:, 0:1], LN_EPS)
            dve.memset(EPS[:, 1:2], NORM_EPS)
            dve.wait_ge(setup_mm, 1)
            b0 = BANK[0]
            dve.tensor_copy(C_COLS[:, :], b0[:, 0:24])
            dve.tensor_copy(B1[:, :, :], b0[:, 24:120].rearrange("p (l n) -> p l n", l=2))
            dve.tensor_copy(B2[:, :, :], b0[:, 120:264].rearrange("p (l n) -> p l n", l=2))
            dve.tensor_copy(G_COLS[:, :], b0[:, 264:376])
            chain.link(dve.tensor_copy(E_COLS[:, :], b0[:, 376:385]))
            dve.sem_inc(cols_done, 1)
            for j in (1, 2, 4, 5):
                dve.tensor_scalar(B1[:, :, 8 * j:8 * j + 8], B1[:, :, 8 * j:8 * j + 8], 1.0, None, ALU.add)
            for j in (1, 4, 7):
                dve.tensor_scalar(B2[:, :, 8 * j:8 * j + 8], B2[:, :, 8 * j:8 * j + 8], 1.0, None, ALU.add)
            dve.tensor_scalar(E_COLS[:, 0:1], E_COLS[:, 0:1], 1.0 - LAMBDA_INIT, None, ALU.mult)
            for k in (1, 3, 5, 7):
                ins = dve.tensor_scalar(E_COLS[:, k:k + 1], E_COLS[:, k:k + 1], SCALE, None, ALU.mult)
            chain.link(ins)
            dve.wait_ge(silu_done, 1)

        def lambdas():
            dve.wait_ge(setup_mm, 2)
            dve.tensor_tensor(T5ROW[:, :], BANK[2][0:N_T5, 0:BIAS_L], T5MASK[:, :], ALU.add).then_inc(t5_rows, 1)
            pairs = LROW[:, :, :].rearrange("p (a b) d -> p a b d", b=2)
            chain.link(dve.tensor_tensor(LPROD[:, :, :], pairs[:, :, 0, :], pairs[:, :, 1, :], ALU.mult))
            dve.tensor_reduce(LAM[:, 0:2], LPROD[:, :, :], AX.X, ALU.add).then_inc(lam_sum, 1)
            dve.wait_ge(lam_exp, 1)
            ins = dve.scalar_tensor_tensor(out=LAM[:, 4:5], in0=LAM[:, 3:4], scalar=LAMBDA_INIT, in1=LAM[:, 2:3],
                                           op0=ALU.subtract, op1=ALU.subtract)
            chain.link(ins)
            dve.sem_inc(region_free, 1)
            dve.wait_ge(setup_act, 8)

        def flat(ap):
            return ap.rearrange("p o n -> p (o n)")

        def norm(s):
            n, ad = s.n, AD[s.ada]
            rms = s.kind == "rms"
            if rms:
                g = G_COLS[:, s.gain:s.gain + 8][:, :, None].broadcast_to([P, 8, 2])
                chain.link(dve.tensor_tensor(GS[:, :, :], ad[:, 8 * s.scale:8 * s.scale + 8, :], g, ALU.mult))
            if s.kind == "ln":
                dve.wait_ge(mean_mm.sem, s.mean + 1)
                for t in range(NT):
                    dve.scalar_tensor_tensor(out=X[:, t, 0:n], in0=B_STAT[:, 0:n], scalar=-1.0 / D, in1=X[:, t, 0:n],
                                             op0=ALU.mult, op1=ALU.add).then_inc(centred.sem, 1)
                dve.wait_ge(centred.sem, s.cen + NT)
            if s.kind != "mod":
                dve.wait_ge(rstd_sq.sem, s.rstd + 1)
                chain.link(dve.reciprocal(RB[:, 0:n], RB[:, 0:n]))
            linked = s.kind == "ln"

            def tile(at):
                par, t = at.u % 2, at(lambda k: k)
                x = flat(X[:, bass.ds(t, 1), 0:n])
                if s.kind != "mod":
                    if not s.last_ln:
                        dve.wait_ge(mod_t2.sem, at(lambda k: s.t2 + k - 1))
                    ins = dve.tensor_tensor(T1[:, par, 0:n], x, RB[:, 0:n], ALU.mult)
                    if rms:
                        ins.then_inc(mod_src.sem, 1)
                    else:
                        chain.link(ins)
                        ins = dve.tensor_scalar(x, T1[:, par, 0:n],
                                                G_COLS[:, bass.ds(at(lambda k: s.gain + k), 1)],
                                                G_COLS[:, bass.ds(at(lambda k: s.gain_b + k), 1)], ALU.mult, ALU.add)
                        if s.last_ln:
                            return
                        ins.then_inc(mod_src.sem, 1)
                    dve.wait_ge(mod_src.sem, at(lambda k: s.src + k + 1))
                for v in range(n // T):
                    cols = slice(v * T, v * T + T)
                    src = T1[:, par, cols] if rms else flat(X[:, bass.ds(t, 1), cols])
                    sc = GS[:, bass.ds(t, 1), v] if rms else ad[:, bass.ds(at(lambda k: 8 * s.scale + k), 1), v]
                    sh = ad[:, bass.ds(at(lambda k: 8 * s.shift + k), 1), v]
                    ins = dve.tensor_scalar(flat(HH[:, bass.ds(t, 1), cols]), src, sc, sh, ALU.mult, ALU.add)
                ins.then_inc(mod_hi.sem, 1)
            each(dve, 0, 8, 2, tile, chain if linked else None, 2)
            if s.kind == "ln":
                dve.drain().then_inc(x_ready.sem, 1)

        def ffn_in(s):
            n = s.n

            def step(at):
                ahead_of(at, lambda k: s.steps[k].g, (lambda k: s.steps[k].host) if s.host else None)
                ahead_of(at, lambda k: s.steps[k].u)
                used(at, lambda k: s.steps[k].u.pieces[-1])
                dve.wait_ge(silu_g.sem, at(lambda k: s.silu + k + 1))
                dve.wait_ge(act_ready.sem, at(lambda k: s.ready + k))
                pair = PAIR[s.steps[at.u].ug.n % 2]
                for j in range(2):
                    ins = dve.tensor_tensor(T2[:, j, 0:n], T1[:, j, 0:n], pair[j][:, 0:n], ALU.mult)
                ins.then_inc(act32.sem, 1)
                dve.wait_ge(act32.sem, at(lambda k: s.a32 + k + 1))
                dve.sem_inc(ev_dve.sem, 1)
            if s.host:
                step(At(None, 0, 1, 1))
                step(At(None, 1, 1, 1))
                each(dve, 2, 10, unroll(s), step, chain, unroll(s) * (KC - 1))
            else:
                each(dve, 0, 10, 2, step)
            step(At(None, 10, 1, 1))

        def proj(s):
            n, ad = s.n, AD[s.ada]
            dve.wait_ge(ada_out, s.need)
            for m, g in enumerate(s.groups):
                for ch in g.chunks:
                    ahead_of(one, lambda _: ch, (lambda _: g.host) if g.host and ch is g.chunks[-1] else None)
                used(one, lambda _: g.chunks[-1].pieces[-1])
                pair = PAIR[g.grp.n % 2]
                if m == 0 and s.half:
                    chain.link(dve.tensor_scalar(GS[:, :, :], ad[:, 8 * s.gate:8 * s.gate + 8, :], 0.5, None, ALU.mult))
                if s.first:
                    for j in range(2):
                        t = 2 * m + j
                        ins = dve.tensor_scalar(T2[:, j, 0:n], pair[j][:, 0:n], ad[:, 8 * s.gate + t, :], None, ALU.mult)
                    chain.link(ins)
                    ins = dve.scalar_tensor_tensor(out=X[:, 2 * m:2 * m + 2, 0:n], in0=X[:, 2 * m:2 * m + 2, 0:n],
                                                   scalar=ALPHA, in1=T2[:, :, 0:n], op0=ALU.mult, op1=ALU.add)
                else:
                    for j in range(2):
                        t = 2 * m + j
                        for v in range(n // T):
                            cols = slice(v * T, v * T + T)
                            gate = GS[:, t, v:v + 1] if s.half else ad[:, 8 * s.gate + t, v:v + 1]
                            ins = dve.scalar_tensor_tensor(out=X[:, t, cols], in0=pair[j][:, cols], scalar=gate,
                                                           in1=X[:, t, cols], op0=ALU.mult, op1=ALU.add)
                chain.link(ins)
                dve.sem_inc(g.grp.tally.sem, 1)
            dve.sem_inc(x_ready.sem, 1)

        def sub_norm():
            for t in range(4):
                dve.wait_ge(sub_rt, t + 1)
                o, r = OF[:, t, :], T2[:, t % 2, 0:T]
                chain.link(dve.reciprocal(r, r))
                chain.link(dve.scalar_tensor_tensor(out=o, in0=o, scalar=E_COLS[:, 0:1], in1=r, op0=ALU.mult,
                                                    op1=ALU.mult))
                chain.link(dve.tensor_copy(HH[:, t, 0:T], o))
                dve.tensor_tensor(HL[:, t, 0:T], o, HH[:, t, 0:T].bitcast(F32), ALU.subtract).then_inc(sub_out, 1)

        def forget_bias(s):
            dve.wait_ge(fg_x, 1)
            dve.scalar_tensor_tensor(out=FD_ABS, in0=FD, scalar=-1.0, in1=FD, op0=ALU.mult, op1=ALU.max
                                     ).then_inc(fg_abs, 1)
            dve.tensor_scalar(FD_MIN, FD, 0.0, None, ALU.min)
            dve.memset(FD_ONE, 1.0)
            dve.wait_ge(fg_exp, 1)
            chain.link(dve.drain())
            chain.link(dve.tensor_tensor(FD_MIN, FD_MIN, FD_ABS, ALU.subtract))
            dve.tensor_tensor_scan(CUM, FD_ONE.rearrange("p a b -> p (a b)"), FD_MIN, 0.0, ALU.mult, ALU.add
                                   ).then_inc(fg_cum, 1)
            dve.wait_ge(fg_mm, 1)
            chain.link(dve.tensor_copy(CUMT[:, :, :], B_T[0][:, 0:16].rearrange("p (q h) -> p q h", q=2)))
            dve.wait_ge(bias_in.sem, s.bias_in)
            for h in range(8):
                dve.wait_ge(fg_mm, h + 2)
                for q in range(2):
                    nk = P * (q + 1)
                    ins = dve.scalar_tensor_tensor(out=BT[:, 512 * h + T * q:512 * h + T * q + nk],
                                                   in0=BANK[h % 2][:, 0:nk], scalar=CUMT[:, q, h:h + 1],
                                                   in1=CAUSAL[:, T - nk:T], op0=ALU.add, op1=ALU.add)
                ins.then_inc(fg_free, 1)
            dve.wait_ge(fg_free, 8)

        def qk_norm(s):
            dve.wait_ge(bias_in.sem, s.bias_in)
            blocks = BT[:, :].rearrange("p (b k) -> p b k", k=T)
            chain.link(dve.tensor_tensor(blocks, blocks, NEIGH[:, None, :].broadcast_to([P, 16, T]), ALU.add))

            dve.wait_ge(qn_root.sem, s.root + 1)
            dve.reciprocal(RB[0:26, :], RB[0:26, :]).then_inc(qn_rstd, 1)
            for i, (t, w) in enumerate(s.items):
                x = QB[:, t, 0:w] if t < 8 else KB[:, t - 8, 0:w]
                k = 1 + 4 * s.layer + (0 if t < 4 else 2 if t < 8 else 1 if t < 12 else 3)
                dve.wait_ge(qn_mm.sem, s.mm + i + 1)
                dve.scalar_tensor_tensor(out=x, in0=x, scalar=E_COLS[:, k:k + 1], in1=B_T[i % 2][:, 0:w],
                                         op0=ALU.mult, op1=ALU.mult).then_inc(qn_out.sem, 1)
            dve.wait_ge(qn_out.sem, s.out + 13)
            for r in range(5):
                x = QB[:, 3 + r, 0:T] if r else KB[:, 4, 0:T]
                dve.wait_ge(rope_mm.sem, s.rmm + r + 1)
                dve.tensor_tensor(T1[:, r % 2, 0:T], BANK[2 + r % 2][:, 0:T], SIN[:, :], ALU.mult)
                chain.link(dve.tensor_tensor(x, x, COS[:, :], ALU.mult))
                dve.tensor_tensor(x, x, T1[:, r % 2, 0:T], ALU.add).then_inc(rope_out.sem, 1)
            for kv in range(2):
                dve.wait_ge(rope_mm.sem, s.rmm + 6 + kv)
                dve.tensor_copy(KB[:, 5 + kv, :], BANK[kv][:, :]).then_inc(rope_out.sem, 1)

        def attn(s):
            dve.wait_ge(bias_in.sem, s.bias_in)

            def maximum(at, half):
                js = (2 * half, 2 * half + 1)
                if s.bias:
                    added = []
                    for j in js:
                        where, _, w = s.bias(at.u, half, j % 2)
                        b = WINDOW[:, j % 2, :] if where == "window" else \
                            BT[:, bass.ds(at(lambda p: s.bias(p, half, j % 2)[1]), w)]
                        dve.wait_ge(scores.sem, at(lambda p: s.sc + 4 * p + j + 1))
                        added.append(chain.mark(dve.tensor_tensor(BANK[j][:, 0:w], BANK[j][:, 0:w], b, ALU.add)))
                for j in js:
                    if s.bias:
                        chain.wait(added[j % 2])
                    else:
                        dve.wait_ge(scores.sem, at(lambda p: s.sc + 4 * p + j + 1))
                    ins = dve.tensor_reduce(NM[:, j:j + 1], BANK[j][:, 0:P * s.nblk(j % 2)], AX.X, ALU.max,
                                            negate=True)
                    if not s.sink:
                        ins.then_inc(nmax.sem, 1)
                    else:
                        chain.mark(ins)
                if s.sink:
                    for j in js:
                        chain.wait(chain.k - 1 + j % 2)
                        col = SINK[:, bass.ds(at(lambda p: s.sink(p, half)), 1)]
                        dve.scalar_tensor_tensor(out=NM[:, j:j + 1], in0=col, scalar=-1.0, in1=NM[:, j:j + 1],
                                                 op0=ALU.mult, op1=ALU.min).then_inc(nmax.sem, 1)

            def weigh(at, js):
                a, b = js[0], js[-1] + 1
                dve.wait_ge(exp_done.sem, at(lambda p: s.ex + 4 * p + b))
                if s.sink:
                    dve.wait_ge(sink_done.sem, at(lambda p: s.sk + 4 * p + b))
                    chain.link(dve.tensor_tensor(RS[:, a:b], RS[:, a:b], ES[:, a:b], ALU.add))
                chain.link(dve.reciprocal(RI[:, a:b], RS[:, a:b]))
                if s.diff:
                    for qt in range(2):
                        p1 = PR[:, 2 + qt, 0:P * s.nblk(qt)]
                        chain.mark(dve.tensor_scalar(p1, p1, RI[:, 2 + qt:3 + qt], LAM[:, 4:5], ALU.mult, ALU.mult))
                    for qt in range(2):
                        p0, p1 = (PR[:, 2 * h + qt, 0:P * s.nblk(qt)] for h in range(2))
                        chain.wait(chain.k - 1 + qt)
                        dve.scalar_tensor_tensor(out=p0, in0=p0, scalar=RI[:, qt:qt + 1], in1=p1,
                                                 op0=ALU.mult, op1=ALU.add).then_inc(probs.sem, 1)
                else:
                    for j in js:
                        p0 = PR[:, j, 0:P * s.nblk(j % 2)]
                        dve.tensor_scalar(p0, p0, RI[:, j:j + 1], None, ALU.mult).then_inc(probs.sem, 1)

            def weigh_all(at):
                for js in ((0, 1, 2, 3),) if s.diff else ((0, 1), (2, 3)):
                    weigh(at, js)

            def take(at):
                dve.wait_ge(pv_done.sem, at(lambda p: s.pv + p + 1))
                if s.diff:
                    dve.tensor_copy(OF[:, at.u, :] if at.reg is None else
                                    flat(OF[:, bass.ds(at(lambda p: p), 1), :]), B_STAT[:, 0:T]
                                    ).then_inc(o_done.sem, 1)
                else:
                    t = at(s.out)
                    hi = flat(HH[:, bass.ds(t, 1), s.qoff:s.qoff + T])
                    lo = flat(HL[:, bass.ds(t, 1), s.qoff:s.qoff + T])
                    chain.link(dve.tensor_copy(hi, B_STAT[:, 0:T]))
                    dve.tensor_tensor(lo, B_STAT[:, 0:T], hi.bitcast(F32), ALU.subtract).then_inc(o_done.sem, 1)
            per = (4 if s.bias else 0) + 3 + (6 if s.sink else 0)
            def maxima(at):
                for half in range(2):
                    maximum(at, half)

            def body(at):
                weigh_all(at)
                take(At(at.reg, at.u - 1, at.unroll, at.n))
                maxima(At(at.reg, at.u + 1, at.unroll, at.n))
            maxima(one)
            weigh_all(one)
            maxima(At(None, 1, 1, 1))
            each(dve, 1, s.pairs - 1, 1, body, chain, per)
            last = At(None, s.pairs - 1, 1, 1)
            weigh_all(last)
            take(At(None, s.pairs - 2, 1, 1))
            take(last)

        for s in PLAN:
            if s.kind == "setup":
                setup()
            elif s.kind == "ada":
                for ch in s.chunks:
                    ada(one, lambda _, ch=ch: ch)
                    if ch is s.chunks[3]:
                        lambdas()
                close(s.hosted)
                flush()
            elif s.kind in ("mod", "ln", "rms"):
                if s.need:
                    dve.wait_ge(ada_out, s.need)
                norm(s)
            elif s.kind == "qkv":
                for it in s.items:
                    ahead_of(one, lambda _: it.chunk, (lambda _: it.host) if it.host else None)
                    if it is s.items[-2] and s.items[-1].grp is None:
                        close(s.hosted)
                if s.hosted:
                    close(s.hosted)
            elif s.kind == "ffn_in":
                ffn_in(s)
            elif s.kind == "proj":
                proj(s)
            elif s.kind == "sub_norm":
                sub_norm()
            elif s.kind == "forget_bias":
                forget_bias(s)
            elif s.kind == "qk_norm":
                qk_norm(s)
            elif s.kind == "attn":
                attn(s)
            elif s.kind == "finish":
                for b in (1, 3):
                    dve.wait_ge(out_mm, b + 1)
                    dve.tensor_copy(OUTR[:, b // 2, 512:1024], BANK[b][:, :]).then_inc(out_cp, 1)


_INS = ["x", "c", "rel_bias", "w_ada", "b_ada", "ln_g", "ln_b", "w_in_ab", "diff_lambda", "diff_subln_g",
        "w_in_cd", "forget_b", "w_o", "w_ffn_in", "w_ffn_out", "c_2", "ctx_2", "c_ctx_2", "w_ada_2", "b_ada_2",
        "norm_g_2", "w_ffn_up_2", "w_ffn_down_2", "w_in_2", "w_out_2", "qk_norm_g_2", "na_rpb_2", "wa_sink_2"]


def kernel(**inputs):
    import concourse.bacc as _bacc
    from concourse.bass_utils import run_bass_kernel_spmd as _run

    nc = _bacc.Bacc("TRN2", target_bir_lowering=False, num_devices=1)
    arrays, a, c = {}, {}, {}
    for name in _INS:
        v = np.ascontiguousarray(inputs[name])
        arrays[f"in_{name}_dram"] = v
        a[name] = nc.dram_tensor(f"in_{name}_dram", v.shape, mybir.dt.from_np(v.dtype), kind="ExternalInput").ap()
    for name, v in shape_constants().items():
        v = np.ascontiguousarray(v, dtype=np.float32)
        arrays[f"const_{name}_dram"] = v
        c[name] = nc.dram_tensor(f"const_{name}_dram", v.shape, F32, kind="ExternalInput").ap()
    out = nc.dram_tensor("out_0_dram", (1, T, D), F32, kind="ExternalOutput").ap()
    build(nc, a, c, out)
    r = _run(nc, [arrays], core_ids=[0])
    return r.results[0]["out_0_dram"]
```
